# Optimizing a Trainium2 kernel written in Bass

```python
import jax, jax.numpy as jnp
from jax import lax
import numpy as np
import jax
import jax.numpy as jnp

D_MODEL = 1024
BATCH = 1
SEQ = 256
DEPTH = 2

MIX_WIDTH = D_MODEL // 2
N_BRANCH = 3
A_HEAD_DIM = 64
A_HEADS = MIX_WIDTH // A_HEAD_DIM
A_WIDTH = A_HEADS * A_HEAD_DIM
A_RANK_W = 64
A_RANK_A = 64
A_RANK_G = 128
A_GN_EPS = 64e-5
B_KEY_DIM = 128
B_VAL_DIM = 128
B_HEADS = MIX_WIDTH // B_VAL_DIM
B_WIDTH = B_HEADS * B_VAL_DIM
B_CHUNK = 64
C_HEAD_DIM = 64
C_HEADS = MIX_WIDTH // C_HEAD_DIM
C_KV_HEADS = 2
C_WIDTH = C_HEADS * C_HEAD_DIM
IDX_HEADS = 4
IDX_DIM = C_HEAD_DIM
TOPK_MAX = 256
Q_BLOCK = 128
ROPE_THETA = 10000.0
D_FF = 2816
CONV_WIDTH = 3
NORM_EPS = 1e-6

A_COLS = 3 * A_WIDTH + A_RANK_W + A_RANK_A + A_RANK_G
B_COLS = 4 * B_WIDTH
C_COLS = C_WIDTH + 2 * C_KV_HEADS * C_HEAD_DIM + IDX_HEADS * IDX_DIM + IDX_DIM + IDX_HEADS
GATE_COLS = N_BRANCH * D_MODEL
IN_COLS = A_COLS + B_COLS + C_COLS + GATE_COLS


F32 = jnp.float32

def _split(t, sizes):
    out, start = [], 0
    for s in sizes:
        out.append(t[..., start:start + s])
        start += s
    return out

def rms_norm(x, g):
    xf = x.astype(F32)
    y = xf * lax.rsqrt(jnp.mean(xf * xf, axis=-1, keepdims=True) + NORM_EPS)
    return (y * g.astype(F32)).astype(x.dtype)

def token_shift(p):
    return jnp.pad(p, ((0, 0), (1, 0), (0, 0)))[:, :-1]

def rope_tables(seq, dim):
    half = dim // 2
    inv_freq = ROPE_THETA ** (-jnp.arange(half, dtype=F32) * (2.0 / dim))
    ang = jnp.arange(seq, dtype=F32)[:, None] * inv_freq[None, :]
    return jnp.cos(ang), jnp.sin(ang)

def apply_rope(t, cos, sin):
    half = t.shape[-1] // 2
    tf = t.astype(F32)
    t1, t2 = tf[..., :half], tf[..., half:]
    c, s = cos[None, :, None, :], sin[None, :, None, :]
    return jnp.concatenate([t1 * c - t2 * s, t2 * c + t1 * s], axis=-1).astype(t.dtype)

def rwkv7_scan(r, w, k, v, a, b):
    bsz, _, heads, n = r.shape

    def step(state, inp):
        r_t, w_t, k_t, v_t, a_t, b_t = inp
        sa = jnp.einsum('bhij,bhj->bhi', state, a_t)
        state = (state * w_t[:, :, None, :] + sa[..., None] * b_t[:, :, None, :]
                 + v_t[..., None] * k_t[:, :, None, :])
        return state, jnp.einsum('bhij,bhj->bhi', state, r_t)

    xs = tuple(jnp.moveaxis(t, 1, 0) for t in (r, w, k, v, a, b))
    _, ys = lax.scan(step, jnp.zeros((bsz, heads, n, n), F32), xs)
    return jnp.moveaxis(ys, 0, 1)

def rwkv7_branch(p, mu, w0, w_up, a0, a_up, g_up, k_k, k_a, r_k, gn_g, gn_b):
    bsz, seq, _ = p.shape
    p = p + (token_shift(p) - p) * mu
    r, k, v, wd, ad, gd = _split(p, (A_WIDTH, A_WIDTH, A_WIDTH, A_RANK_W, A_RANK_A, A_RANK_G))
    w_log = -jax.nn.softplus(-(w0 + jnp.tanh(wd) @ w_up).astype(F32)) - 0.5
    decay = jnp.exp(-jnp.exp(w_log))
    a = jax.nn.sigmoid((a0 + ad @ a_up).astype(F32))
    g = jax.nn.sigmoid(gd) @ g_up

    def hd(t):
        return t.astype(F32).reshape(bsz, seq, A_HEADS, A_HEAD_DIM)

    kk = hd(k * k_k)
    kk = kk * lax.rsqrt(jnp.maximum(jnp.sum(kk * kk, axis=-1, keepdims=True), 1e-24))
    k_mod = hd(k.astype(F32) * (1.0 + (a - 1.0) * k_a.astype(F32)))
    r_h, v_h, a_h = hd(r), hd(v), hd(a)
    y = rwkv7_scan(r_h, hd(decay), k_mod, v_h, -kk, kk * a_h)
    mean = jnp.mean(y, axis=-1, keepdims=True)
    var = jnp.mean(jnp.square(y - mean), axis=-1, keepdims=True)
    y = ((y - mean) * lax.rsqrt(var + A_GN_EPS)).reshape(bsz, seq, A_WIDTH)
    y = y * gn_g.astype(F32) + gn_b.astype(F32)
    bonus = jnp.sum(r_h * k_mod * r_k.astype(F32), axis=-1, keepdims=True) * v_h
    y = y + bonus.reshape(bsz, seq, A_WIDTH)
    return (y * g.astype(F32)).astype(p.dtype)

def hgrn2_chunk_step(state, inp):
    q, k, g, v = inp
    b = jnp.cumsum(g, axis=2)
    causal = jnp.tril(jnp.ones((B_CHUNK, B_CHUNK), dtype=bool))
    diff = b[:, :, :, None, :] - b[:, :, None, :, :]
    decay = jnp.exp(jnp.where(causal[:, :, None], diff, -jnp.inf))
    scores = jnp.einsum('bhtd,bhsd,bhtsd->bhts', q, k, decay)
    o = (jnp.einsum('bhts,bhsv->bhtv', scores, v)
         + jnp.einsum('bhtd,bhdv->bhtv', q * jnp.exp(b), state))
    b_end = b[:, :, -1:, :]
    state = (state * jnp.exp(b_end)[:, :, 0, :, None]
             + jnp.einsum('bhsd,bhsv->bhdv', k * jnp.exp(b_end - b), v))
    return state, o

def hgrn2_branch(p, lb, gn_g):
    bsz, seq, _ = p.shape
    q, f, i, g = _split(p, (B_WIDTH, B_WIDTH, B_WIDTH, B_WIDTH))
    f = f.astype(F32)
    lb = lb.astype(F32)
    log_f = jnp.logaddexp(jnp.log(lb), jnp.log1p(-lb) + jax.nn.log_sigmoid(f))
    k_in = (1.0 - lb) * jax.nn.sigmoid(-f)
    n_chunk = seq // B_CHUNK

    def chunks(t, d):
        return t.astype(F32).reshape(bsz, n_chunk, B_CHUNK, B_HEADS, d).transpose(1, 0, 3, 2, 4)

    s0 = jnp.zeros((bsz, B_HEADS, B_KEY_DIM, B_VAL_DIM), F32)
    _, o = lax.scan(hgrn2_chunk_step, s0,
                    (chunks(q, B_KEY_DIM), chunks(k_in, B_KEY_DIM),
                     chunks(log_f, B_KEY_DIM), chunks(i, B_VAL_DIM)))
    o = o.transpose(1, 0, 3, 2, 4).reshape(bsz, seq, B_HEADS, B_VAL_DIM)
    o = o * lax.rsqrt(jnp.mean(o * o, axis=-1, keepdims=True) + NORM_EPS)
    o = o.reshape(bsz, seq, B_WIDTH) * gn_g.astype(F32) * jax.nn.silu(g.astype(F32))
    return o.astype(p.dtype)

def dsa_branch(p, cos, sin):
    bsz, seq, _ = p.shape
    kv_w = C_KV_HEADS * C_HEAD_DIM
    q, k, v, qi, ki, wi = _split(p, (C_WIDTH, kv_w, kv_w, IDX_HEADS * IDX_DIM, IDX_DIM, IDX_HEADS))
    q = apply_rope(q.reshape(bsz, seq, C_HEADS, C_HEAD_DIM), cos, sin)
    k = apply_rope(k.reshape(bsz, seq, C_KV_HEADS, C_HEAD_DIM), cos, sin)
    v = v.reshape(bsz, seq, C_KV_HEADS, C_HEAD_DIM)
    qi = apply_rope(qi.reshape(bsz, seq, IDX_HEADS, IDX_DIM), cos, sin)
    ki = apply_rope(ki[:, :, None, :], cos, sin)[:, :, 0, :].astype(F32)
    wi = wi.astype(F32) * (IDX_HEADS ** -0.5) * (IDX_DIM ** -0.5)
    n_blk = seq // Q_BLOCK
    k_sel = min(TOPK_MAX, seq // 4)
    group = C_HEADS // C_KV_HEADS
    s_pos = jnp.arange(seq)

    def blockify(t):
        return jnp.moveaxis(t.reshape(bsz, n_blk, Q_BLOCK, *t.shape[2:]), 1, 0)

    def attend(args):
        qb, qib, wib, t0 = args
        t_pos = t0 + jnp.arange(Q_BLOCK)
        causal = s_pos[None, :] <= t_pos[:, None]
        dots = jnp.einsum('bqhd,bsd->bqhs', qib.astype(F32), ki)
        score = jnp.einsum('bqhs,bqh->bqs', jax.nn.relu(dots), wib)
        score = jnp.where(causal[None], score, -jnp.inf)
        _, idx = lax.top_k(score, k_sel)
        kg = jax.vmap(lambda kb, ib: kb[ib])(k, idx)
        vg = jax.vmap(lambda vb, ib: vb[ib])(v, idx)
        valid = idx <= t_pos[None, :, None]
        qg = qb.reshape(bsz, Q_BLOCK, C_KV_HEADS, group, C_HEAD_DIM)
        logits = jnp.einsum('bqcgd,bqkcd->bqcgk', qg, kg).astype(F32) * (C_HEAD_DIM ** -0.5)
        logits = jnp.where(valid[:, :, None, None, :], logits, -jnp.inf)
        prob = jax.nn.softmax(logits, axis=-1).astype(vg.dtype)
        out = jnp.einsum('bqcgk,bqkcd->bqcgd', prob, vg)
        return out.reshape(bsz, Q_BLOCK, C_WIDTH)

    outs = lax.map(attend, (blockify(q), blockify(qi), blockify(wi),
                            jnp.arange(n_blk, dtype=jnp.int32) * Q_BLOCK))
    return jnp.moveaxis(outs, 0, 1).reshape(bsz, seq, C_WIDTH).astype(p.dtype)

def conv_glu(h, w_up, conv_w, conv_b, w_down):
    seq = h.shape[1]
    up = h @ w_up
    up_pad = jnp.pad(up, ((0, 0), (CONV_WIDTH - 1, 0), (0, 0)))
    c = conv_b
    for j in range(CONV_WIDTH):
        c = c + conv_w[j] * up_pad[:, j:j + seq]
    gate, val = _split(c, (D_FF, D_FF))
    return (jax.nn.silu(gate) * val) @ w_down

def first_inputs(seed: int = 0) -> dict:
    key = jax.random.key(seed)
    ks = iter(jax.random.split(key, 32))

    def nrm(shape, scale):
        return jax.random.normal(next(ks), shape, F32) * scale

    def uni(shape, lo, hi):
        return jax.random.uniform(next(ks), shape, F32, lo, hi)

    f2 = 2 * D_FF
    return {
        'x': nrm((BATCH, SEQ, D_MODEL), 1.0),
        'norm_mix_g': 1.0 + nrm((DEPTH, D_MODEL), 0.02),
        'w_in': nrm((DEPTH, D_MODEL, IN_COLS), D_MODEL ** -0.5),
        'a_mu': uni((DEPTH, A_COLS), 0.0, 1.0),
        'a_w0': uni((DEPTH, A_WIDTH), -5.0, 0.0),
        'a_w_up': nrm((DEPTH, A_RANK_W, A_WIDTH), 0.5 * A_RANK_W ** -0.5),
        'a_a0': nrm((DEPTH, A_WIDTH), 0.5),
        'a_a_up': nrm((DEPTH, A_RANK_A, A_WIDTH), 0.5 * A_RANK_A ** -0.5),
        'a_g_up': nrm((DEPTH, A_RANK_G, A_WIDTH), A_RANK_G ** -0.5),
        'a_k_k': 0.85 + nrm((DEPTH, A_WIDTH), 0.05),
        'a_k_a': 1.0 + nrm((DEPTH, A_WIDTH), 0.05),
        'a_r_k': nrm((DEPTH, A_HEADS, A_HEAD_DIM), 0.1),
        'a_gn_g': 1.0 + nrm((DEPTH, A_WIDTH), 0.02),
        'a_gn_b': nrm((DEPTH, A_WIDTH), 0.02),
        'b_lb_logits': nrm((DEPTH, B_HEADS * B_KEY_DIM), 1.0),
        'b_gn_g': 1.0 + nrm((DEPTH, B_WIDTH), 0.02),
        'w_branch': nrm((DEPTH, N_BRANCH, MIX_WIDTH, D_MODEL), MIX_WIDTH ** -0.5),
        'w_o': nrm((DEPTH, D_MODEL, D_MODEL), D_MODEL ** -0.5),
        'norm_ffn_g': 1.0 + nrm((DEPTH, D_MODEL), 0.02),
        'w_up': nrm((DEPTH, D_MODEL, f2), D_MODEL ** -0.5),
        'conv_w': nrm((DEPTH, CONV_WIDTH, f2), CONV_WIDTH ** -0.5),
        'conv_b': nrm((DEPTH, f2), 0.02),
        'w_down': nrm((DEPTH, D_FF, D_MODEL), D_FF ** -0.5),
        'norm_final_g': 1.0 + nrm((D_MODEL,), 0.02),
    }

def first_block(x, norm_mix_g, w_in, a_mu, a_w0, a_w_up, a_a0, a_a_up, a_g_up, a_k_k, a_k_a,
              a_r_k, a_gn_g, a_gn_b, b_lb_logits, b_gn_g, w_branch, w_o, norm_ffn_g,
              w_up, conv_w, conv_b, w_down, norm_final_g):
    bsz, seq, _ = x.shape
    cos, sin = rope_tables(seq, C_HEAD_DIM)
    lb_cum = jnp.cumsum(jax.nn.softmax(b_lb_logits.astype(F32), axis=0), axis=0)
    lower_bounds = lb_cum - lb_cum[0]
    h = x
    for layer in range(DEPTH):
        u = rms_norm(h, norm_mix_g[layer])
        p = u @ w_in[layer]
        p_a, p_b, p_c, p_gate = _split(p, (A_COLS, B_COLS, C_COLS, GATE_COLS))
        y_a = rwkv7_branch(p_a, a_mu[layer], a_w0[layer], a_w_up[layer], a_a0[layer],
                           a_a_up[layer], a_g_up[layer], a_k_k[layer], a_k_a[layer],
                           a_r_k[layer], a_gn_g[layer], a_gn_b[layer])
        y_b = hgrn2_branch(p_b, lower_bounds[layer], b_gn_g[layer])
        y_c = dsa_branch(p_c, cos, sin)
        ys = jnp.stack([y_a, y_b, y_c], axis=2)
        branch = jnp.einsum('bsnc,ncd->bsnd', ys, w_branch[layer])
        gates = jax.nn.sigmoid(p_gate.reshape(bsz, seq, N_BRANCH, D_MODEL))
        merged = jnp.sum(gates * branch, axis=2)
        h = h + merged @ w_o[layer]
        u = rms_norm(h, norm_ffn_g[layer])
        h = h + conv_glu(u, w_up[layer], conv_w[layer], conv_b[layer], w_down[layer])
    return rms_norm(h, norm_final_g)


MLSTM_HEADS = 4
MLSTM_DQK = 64
MLSTM_DV = 128
MLSTM_CHUNK = 64
CONV_WIDTH_2 = 4
MOBA_HEADS = 4
MOBA_DH = 64
MOBA_BLOCK = 256
MOBA_TOPK = 3
MOBA_Q_BLOCK = 64
ROPE_THETA_2 = 500000.0
PARTIAL_ROPE_DIM = MOBA_DH // 4
MLA_HEADS = 4
MLA_NOPE = 64
MLA_ROPE = 32
MLA_DV = 64
MLA_Q_LORA = 384
MLA_KV_LORA = 256
MLA_ROPE_THETA = 10000.0
ATTN_Q_BLOCK = 128
D_FF_2 = 4 * D_MODEL

MLSTM_WIDTH = MLSTM_HEADS * MLSTM_DV
MOBA_WIDTH = MOBA_HEADS * MOBA_DH
MLA_WIDTH = MLA_HEADS * MLA_DV
MIX_WIDTH_2 = MLSTM_WIDTH + MOBA_WIDTH + MLA_WIDTH
MLA_QK_DIM = MLA_NOPE + MLA_ROPE
IN_SPLITS = (
    2 * MLSTM_HEADS * MLSTM_DQK,
    MLSTM_WIDTH,
    MLSTM_WIDTH,
    MLSTM_HEADS,
    MLSTM_HEADS,
    3 * MOBA_WIDTH,
    MLA_Q_LORA,
    MLA_KV_LORA,
    MLA_ROPE,
)
D_IN = sum(IN_SPLITS)


def rms_norm_2(x, g):
    xf = x.astype(jnp.float32)
    y = xf * lax.rsqrt(jnp.mean(xf * xf, axis=-1, keepdims=True) + NORM_EPS)
    return (y * g.astype(jnp.float32)).astype(x.dtype)

def rope_tables_2(positions, dim, theta):
    inv_freq = jnp.power(jnp.float32(theta), -jnp.arange(0, dim, 2, dtype=jnp.float32) / dim)
    ang = positions.astype(jnp.float32)[..., None] * inv_freq
    return jnp.cos(ang), jnp.sin(ang)

def rotate(x, cos, sin):
    half = x.shape[-1] // 2
    x1 = x[..., :half].astype(jnp.float32)
    x2 = x[..., half:].astype(jnp.float32)
    c = cos[:, :, None, :]
    s = sin[:, :, None, :]
    return jnp.concatenate([x1 * c - x2 * s, x2 * c + x1 * s], axis=-1).astype(x.dtype)

def causal_depthwise_conv(x, w, b):
    C = x.shape[-1]
    y = lax.conv_general_dilated(
        x, w[:, None, :].astype(x.dtype), window_strides=(1,),
        padding=[(CONV_WIDTH_2 - 1, 0)], dimension_numbers=('NWC', 'WIO', 'NWC'),
        feature_group_count=C)
    return y + b.astype(x.dtype)

def mlstm_chunkwise(q, k, v, i_pre, f_pre):
    B, S, H, DK = q.shape
    DV = v.shape[-1]
    L = MLSTM_CHUNK
    NC = S // L
    f32 = jnp.float32
    q = q.astype(f32) * (DK ** -0.5)
    k = k.astype(f32)
    v = v.astype(f32)
    log_f = jax.nn.log_sigmoid(f_pre.astype(f32))
    log_i = i_pre.astype(f32)

    def chunks(t):
        return t.reshape((B, NC, L) + t.shape[2:]).swapaxes(0, 1)

    causal = jnp.tril(jnp.ones((L, L), dtype=bool))

    def step(carry, inp):
        C, n, m = carry
        qj, kj, vj, lfj, lij = inp
        bt = jnp.cumsum(lfj, axis=1).transpose(0, 2, 1)
        it = lij.transpose(0, 2, 1)
        log_d = bt[:, :, :, None] - bt[:, :, None, :] + it[:, :, None, :]
        log_d = jnp.where(causal, log_d, -jnp.inf)
        log_inter = bt + m[:, :, None]
        m_t = jnp.maximum(log_inter, jnp.max(log_d, axis=-1))
        d = jnp.exp(log_d - m_t[..., None])
        inter = jnp.exp(log_inter - m_t)
        s = jnp.einsum('blhd,bshd->bhls', qj, kj) * d
        num = (jnp.einsum('bhls,bshv->bhlv', s, vj)
               + inter[..., None] * jnp.einsum('blhd,bhvd->bhlv', qj, C))
        den = jnp.sum(s, axis=-1) + inter * jnp.einsum('blhd,bhd->bhl', qj, n)
        h = num / jnp.maximum(jnp.abs(den), jnp.exp(-m_t))[..., None]
        b_last = bt[:, :, -1]
        log_w = b_last[:, :, None] - bt + it
        m_new = jnp.maximum(b_last + m, jnp.max(log_w, axis=-1))
        w = jnp.exp(log_w - m_new[..., None])
        decay = jnp.exp(b_last + m - m_new)
        C_new = decay[..., None, None] * C + jnp.einsum('bhs,bshv,bshd->bhvd', w, vj, kj)
        n_new = decay[..., None] * n + jnp.einsum('bhs,bshd->bhd', w, kj)
        return (C_new, n_new, m_new), h.transpose(0, 2, 1, 3)

    init = (jnp.zeros((B, H, DV, DK), f32), jnp.zeros((B, H, DK), f32), jnp.zeros((B, H), f32))
    _, h = lax.scan(step, init, (chunks(q), chunks(k), chunks(v), chunks(log_f), chunks(log_i)))
    return h.swapaxes(0, 1).reshape(B, S, H, DV)

def moba_attention(q, k, v):
    B, S, H, D = q.shape
    BS = MOBA_BLOCK
    QB = MOBA_Q_BLOCK
    NB = -(-S // BS)
    S_pad = NB * BS
    K = min(MOBA_TOPK, NB)
    scale = D ** -0.5
    qh = q.transpose(0, 2, 1, 3)
    pad = ((0, 0), (0, 0), (0, S_pad - S), (0, 0))
    kb = jnp.pad(k.transpose(0, 2, 1, 3), pad).reshape(B, H, NB, BS, D)
    vb = jnp.pad(v.transpose(0, 2, 1, 3), pad).reshape(B, H, NB, BS, D)
    k_mean = jnp.mean(kb.astype(jnp.float32), axis=3)
    b_idx = jnp.arange(B)[:, None, None, None]
    h_idx = jnp.arange(H)[None, :, None, None]

    def one_block(qi):
        start = qi * QB
        q_blk = lax.dynamic_slice_in_dim(qh, start, QB, axis=2)
        own = start // BS
        gate = jnp.einsum('bhqd,bhnd->bhqn', q_blk.astype(jnp.float32), k_mean)
        gate = jnp.where(jnp.arange(NB) < own, gate, -jnp.inf)
        _, sel = lax.top_k(gate, K)
        sel_valid = jnp.arange(K) < own
        k_sel = kb[b_idx, h_idx, sel]
        v_sel = vb[b_idx, h_idx, sel]
        s_sel = jnp.einsum('bhqd,bhqkjd->bhqkj', q_blk, k_sel).astype(jnp.float32) * scale
        s_sel = jnp.where(sel_valid[:, None], s_sel, -jnp.inf)
        k_own = lax.dynamic_index_in_dim(kb, own, axis=2, keepdims=False)
        v_own = lax.dynamic_index_in_dim(vb, own, axis=2, keepdims=False)
        s_own = jnp.einsum('bhqd,bhjd->bhqj', q_blk, k_own).astype(jnp.float32) * scale
        q_pos = start + jnp.arange(QB)
        k_pos = own * BS + jnp.arange(BS)
        s_own = jnp.where(k_pos[None, :] <= q_pos[:, None], s_own, -jnp.inf)
        s = jnp.concatenate([s_sel.reshape(B, H, QB, K * BS), s_own], axis=-1)
        p = jax.nn.softmax(s, axis=-1).astype(v.dtype)
        p_sel = p[..., :K * BS].reshape(B, H, QB, K, BS)
        p_own = p[..., K * BS:]
        return (jnp.einsum('bhqkj,bhqkjd->bhqd', p_sel, v_sel)
                + jnp.einsum('bhqj,bhjd->bhqd', p_own, v_own))

    out = lax.map(one_block, jnp.arange(S // QB))
    return out.transpose(1, 0, 3, 2, 4).reshape(B, S, H, D)

def causal_block_attention(q, k, v):
    B, S, H, Dk = q.shape
    Dv = v.shape[-1]
    QB = ATTN_Q_BLOCK
    scale = Dk ** -0.5
    qh = q.transpose(0, 2, 1, 3)
    kh = k.transpose(0, 2, 1, 3)
    vh = v.transpose(0, 2, 1, 3)
    k_pos = jnp.arange(S)

    def one_block(qi):
        start = qi * QB
        q_blk = lax.dynamic_slice_in_dim(qh, start, QB, axis=2)
        s = jnp.einsum('bhqd,bhkd->bhqk', q_blk, kh).astype(jnp.float32) * scale
        q_pos = start + jnp.arange(QB)
        s = jnp.where(k_pos[None, :] <= q_pos[:, None], s, -jnp.inf)
        p = jax.nn.softmax(s, axis=-1).astype(vh.dtype)
        return jnp.einsum('bhqk,bhkd->bhqd', p, vh)

    out = lax.map(one_block, jnp.arange(S // QB))
    return out.transpose(1, 0, 3, 2, 4).reshape(B, S, H, Dv)

def hybrid_layer(x, cos_p, sin_p, cos_d, sin_d, w_in, conv_w, conv_b, b_igate, b_fgate,
                 g_mix_norm, g_mlstm_out, g_moba_q, g_moba_k, g_moba_out, g_cq, g_ckv,
                 w_uq, w_ukv, g_mla_q, g_mla_k, g_mla_out, w_out, g_mlp_norm, w_up, w_down):
    B, S, _ = x.shape
    h = rms_norm_2(x, g_mix_norm)
    proj = h @ w_in
    offsets = [int(o) for o in np.cumsum(IN_SPLITS)[:-1]]
    m_qk, m_v, m_o, m_i, m_f, moba_qkv, cq, ckv, kpe = jnp.split(proj, offsets, axis=-1)

    qk = jax.nn.silu(causal_depthwise_conv(m_qk, conv_w, conv_b))
    mq, mk = jnp.split(qk, 2, axis=-1)
    mq = mq.reshape(B, S, MLSTM_HEADS, MLSTM_DQK)
    mk = mk.reshape(B, S, MLSTM_HEADS, MLSTM_DQK)
    mv = m_v.reshape(B, S, MLSTM_HEADS, MLSTM_DV)
    hm = mlstm_chunkwise(mq, mk, mv, m_i + b_igate, m_f + b_fgate).astype(x.dtype)
    hm = rms_norm_2(hm, g_mlstm_out) * jax.nn.sigmoid(m_o).reshape(B, S, MLSTM_HEADS, MLSTM_DV)

    aq, ak, av = jnp.split(moba_qkv.reshape(B, S, 3 * MOBA_HEADS, MOBA_DH), 3, axis=2)
    aq = rms_norm_2(aq, g_moba_q)
    ak = rms_norm_2(ak, g_moba_k)
    aq = jnp.concatenate([rotate(aq[..., :PARTIAL_ROPE_DIM], cos_p, sin_p), aq[..., PARTIAL_ROPE_DIM:]], axis=-1)
    ak = jnp.concatenate([rotate(ak[..., :PARTIAL_ROPE_DIM], cos_p, sin_p), ak[..., PARTIAL_ROPE_DIM:]], axis=-1)
    ha = rms_norm_2(moba_attention(aq, ak, av), g_moba_out)

    lq = (rms_norm_2(cq, g_cq) @ w_uq).reshape(B, S, MLA_HEADS, MLA_QK_DIM)
    kv = (rms_norm_2(ckv, g_ckv) @ w_ukv).reshape(B, S, MLA_HEADS, MLA_NOPE + MLA_DV)
    lk = jnp.concatenate(
        [kv[..., :MLA_NOPE], jnp.broadcast_to(kpe[:, :, None, :], (B, S, MLA_HEADS, MLA_ROPE))], axis=-1)
    lv = kv[..., MLA_NOPE:]
    lq = rms_norm_2(lq, g_mla_q)
    lk = rms_norm_2(lk, g_mla_k)
    lq = jnp.concatenate([lq[..., :MLA_NOPE], rotate(lq[..., MLA_NOPE:], cos_d, sin_d)], axis=-1)
    lk = jnp.concatenate([lk[..., :MLA_NOPE], rotate(lk[..., MLA_NOPE:], cos_d, sin_d)], axis=-1)
    hl = rms_norm_2(causal_block_attention(lq, lk, lv), g_mla_out)

    mix = jnp.concatenate([hm.reshape(B, S, MLSTM_WIDTH), ha.reshape(B, S, MOBA_WIDTH),
                           hl.reshape(B, S, MLA_WIDTH)], axis=-1)
    x = x + mix @ w_out

    h2 = rms_norm_2(x, g_mlp_norm)
    x = x + jnp.square(jax.nn.relu(h2 @ w_up)) @ w_down
    return x

def second_inputs(seed: int = 0) -> dict:
    key = jax.random.key(seed)
    ks = jax.random.split(key, 24)
    f32 = jnp.float32

    def nrm(k, shape, scale):
        return jax.random.normal(k, shape, f32) * scale

    def gain(k, shape):
        return 1.0 + 0.02 * jax.random.normal(k, shape, f32)

    Ld = DEPTH
    x = nrm(ks[0], (BATCH, SEQ, D_MODEL), 1.0)
    offset = jax.random.randint(ks[1], (BATCH, 1), 0, 4096, dtype=jnp.int32)
    positions = offset + jnp.arange(SEQ, dtype=jnp.int32)[None, :]
    return {
        'x': x,
        'positions': positions,
        'w_in': nrm(ks[2], (Ld, D_MODEL, D_IN), D_MODEL ** -0.5),
        'conv_w': nrm(ks[3], (Ld, CONV_WIDTH_2, 2 * MLSTM_HEADS * MLSTM_DQK), 0.5),
        'conv_b': nrm(ks[4], (Ld, 2 * MLSTM_HEADS * MLSTM_DQK), 0.01),
        'b_igate': nrm(ks[5], (Ld, MLSTM_HEADS), 0.1),
        'b_fgate': 3.0 + nrm(ks[6], (Ld, MLSTM_HEADS), 0.5),
        'g_mix_norm': gain(ks[7], (Ld, D_MODEL)),
        'g_mlstm_out': gain(ks[8], (Ld, MLSTM_HEADS, MLSTM_DV)),
        'g_moba_q': gain(ks[9], (Ld, MOBA_DH)),
        'g_moba_k': gain(ks[10], (Ld, MOBA_DH)),
        'g_moba_out': gain(ks[11], (Ld, MOBA_HEADS, MOBA_DH)),
        'g_cq': gain(ks[12], (Ld, MLA_Q_LORA)),
        'g_ckv': gain(ks[13], (Ld, MLA_KV_LORA)),
        'w_uq': nrm(ks[14], (Ld, MLA_Q_LORA, MLA_HEADS * MLA_QK_DIM), MLA_Q_LORA ** -0.5),
        'w_ukv': nrm(ks[15], (Ld, MLA_KV_LORA, MLA_HEADS * (MLA_NOPE + MLA_DV)), MLA_KV_LORA ** -0.5),
        'g_mla_q': gain(ks[16], (Ld, MLA_QK_DIM)),
        'g_mla_k': gain(ks[17], (Ld, MLA_QK_DIM)),
        'g_mla_out': gain(ks[18], (Ld, MLA_HEADS, MLA_DV)),
        'w_out': nrm(ks[19], (Ld, MIX_WIDTH_2, D_MODEL), 0.5 * MIX_WIDTH_2 ** -0.5),
        'g_mlp_norm': gain(ks[20], (Ld, D_MODEL)),
        'w_up': nrm(ks[21], (Ld, D_MODEL, D_FF_2), D_MODEL ** -0.5),
        'w_down': nrm(ks[22], (Ld, D_FF_2, D_MODEL), 0.5 * D_FF_2 ** -0.5),
    }

def second_block(x, positions, w_in, conv_w, conv_b, b_igate, b_fgate, g_mix_norm, g_mlstm_out,
              g_moba_q, g_moba_k, g_moba_out, g_cq, g_ckv, w_uq, w_ukv, g_mla_q, g_mla_k,
              g_mla_out, w_out, g_mlp_norm, w_up, w_down):
    cos_p, sin_p = rope_tables_2(positions, PARTIAL_ROPE_DIM, ROPE_THETA_2)
    cos_d, sin_d = rope_tables_2(positions, MLA_ROPE, MLA_ROPE_THETA)
    for l in range(DEPTH):
        x = hybrid_layer(
            x, cos_p, sin_p, cos_d, sin_d, w_in[l], conv_w[l], conv_b[l], b_igate[l], b_fgate[l],
            g_mix_norm[l], g_mlstm_out[l], g_moba_q[l], g_moba_k[l], g_moba_out[l], g_cq[l], g_ckv[l],
            w_uq[l], w_ukv[l], g_mla_q[l], g_mla_k[l], g_mla_out[l], w_out[l], g_mlp_norm[l],
            w_up[l], w_down[l])
    return x


def setup_inputs(seed=0):
    out = dict(first_inputs(seed))
    for name, value in second_inputs(seed + 1).items():
        if name != "x":
            out[name + "_2"] = value
    return out


def reference(
    x, norm_mix_g, w_in, a_mu, a_w0, a_w_up, a_a0, a_a_up, a_g_up, a_k_k, a_k_a, a_r_k, a_gn_g,
    a_gn_b, b_lb_logits, b_gn_g, w_branch, w_o, norm_ffn_g, w_up, conv_w, conv_b, w_down,
    norm_final_g, positions_2, w_in_2, conv_w_2, conv_b_2, b_igate_2, b_fgate_2, g_mix_norm_2,
    g_mlstm_out_2, g_moba_q_2, g_moba_k_2, g_moba_out_2, g_cq_2, g_ckv_2, w_uq_2, w_ukv_2,
    g_mla_q_2, g_mla_k_2, g_mla_out_2, w_out_2, g_mlp_norm_2, w_up_2, w_down_2,
):
    x = first_block(
        x, norm_mix_g, w_in, a_mu, a_w0, a_w_up, a_a0, a_a_up, a_g_up, a_k_k, a_k_a, a_r_k,
        a_gn_g, a_gn_b, b_lb_logits, b_gn_g, w_branch, w_o, norm_ffn_g, w_up, conv_w, conv_b,
        w_down, norm_final_g,
    )
    return second_block(
        x, positions_2, w_in_2, conv_w_2, conv_b_2, b_igate_2, b_fgate_2, g_mix_norm_2,
        g_mlstm_out_2, g_moba_q_2, g_moba_k_2, g_moba_out_2, g_cq_2, g_ckv_2, w_uq_2, w_ukv_2,
        g_mla_q_2, g_mla_k_2, g_mla_out_2, w_out_2, g_mlp_norm_2, w_up_2, w_down_2,
    )


_drawn_inputs = setup_inputs


def setup_inputs(seed=0):
    import zlib

    import numpy as np

    out = dict(_drawn_inputs(seed))
    spreads = {}
    factors = {'a_w_up': 3.135,
     'a_k_k': 3.148,
     'a_gn_g': 4.657,
     'a_gn_b': 2.828,
     'b_gn_g': 4.341,
     'conv_b_2': 21.225,
     'b_igate_2': 8.0,
     'g_mix_norm_2': 3.202,
     'g_mlstm_out_2': 8.0,
     'g_moba_q_2': 8.0,
     'g_moba_k_2': 8.0,
     'g_moba_out_2': 8.0,
     'g_cq_2': 8.0,
     'g_ckv_2': 6.783,
     'g_mla_q_2': 8.0,
     'g_mla_k_2': 8.0,
     'g_mla_out_2': 8.0,
     'g_mlp_norm_2': 3.66}
    for name, (base, spread) in spreads.items():
        noise = np.random.default_rng([zlib.crc32(name.encode()), seed]).standard_normal(out[name].shape)
        drawn = base * np.exp(spread * noise) if base else spread * noise
        out[name] = jnp.asarray(drawn.astype(out[name].dtype))
    for name, factor in factors.items():
        out[name] = (out[name] * factor).astype(out[name].dtype)
    return out
```

```python
from contextlib import ExitStack

import numpy as np

import concourse.bass as bass
from concourse import mybir
from concourse.alu_op_type import AluOpType as ALU

F32 = mybir.dt.float32
I32 = mybir.dt.int32
U8 = mybir.dt.uint8
ACT = mybir.ActivationFunctionType
AX_X = mybir.AxisListType.X

P = 128
T = 256
NT = T // P
D = 1024
KD = D // P
LAYERS = 2
EPS = 1e-6

A_W, A_COLS = 512, 1792
GN_EPS = 64e-5
KAPPA = float(np.exp(-0.5))
C_OFF, G_OFF = 3840, 4932
FF1 = 2816
TOPK, TOP_STEP = 64, 8
NEG, TAKEN = -1e30, -3e38
FF2 = 4096
MLA_D = 96

CHUNK = 20
RING = 4
BLOCKS1, BLOCKS2 = 1200, 800
CH1, CH2 = BLOCKS1 // CHUNK, BLOCKS2 // CHUNK
assert CH1 % RING == 0 and CH2 % RING == 0
LEVELS = 7


class Columns:

    def __init__(self, *runs):
        self.at, self.size = {}, 0
        for name, n in runs:
            self.at[name] = (self.size, n)
            self.size += n

    def of(self, table, name):
        a, n = self.at[name]
        return table[:, a:a + n]


PAR1 = Columns(("g_mix", 8), ("mu", 14), ("w0", 4), ("a0", 4), ("k_k", 4), ("k_a", 4), ("r_k", 4), ("gn_g", 4),
               ("gn_b", 4), ("lb0", 4), ("lb1", 4), ("not_first", 4), ("b_gn", 4), ("g_ffn", 8), ("conv_b", 44),
               ("conv_w0", 44), ("conv_w1", 44), ("conv_w2", 44), ("g_final", 8), ("wa_up", A_W), ("g_up", A_W))
PAR2 = Columns(("g_mix", 8), ("conv_w", 16), ("conv_b", 4), ("b_i", 1), ("b_f", 1), ("g_mlstm", 4), ("g_mq", 1),
               ("g_mk", 1), ("g_mobaout", 2), ("g_cq", 3), ("g_ckv", 2), ("g_lq", 1), ("g_lk", 1), ("g_mlaout", 2),
               ("g_mlp", 8))
CST = Columns(("ident", P), ("ones", P), ("bones", P), ("pairmask", 4 * P), ("lower", P), ("cneg", T),
              ("rot", P), ("dup0", P), ("dup1", P), ("rdup0", P), ("rdup1", P), ("rotp", P), ("rotd", P),
              ("cos", T), ("sin", T), ("sel", 4 * P), ("freq", 2))
MASKS = Columns(("up", LEVELS * P), ("low", LEVELS * P), ("diag", P))


def blocks(w):
    k, n = w.shape
    w = np.pad(w, ((0, 0), (0, -n % P)))
    return w.reshape(k // P, P, -1, P).transpose(2, 0, 1, 3).reshape(-1, P, P)


def row_blocks(w):
    k, n = w.shape
    w = np.pad(w, ((0, 0), (0, -n % P)))
    return w.reshape(k // P, P, -1, P).transpose(0, 2, 1, 3).reshape(-1, P, P)


def stream1(w_in, w_branch, w_o, w_up, w_down):
    b, c = A_COLS, C_OFF
    out = [blocks(w_in[:, :b + 1024]), row_blocks(w_in[:, b + 1024:b + 1536]), blocks(w_in[:, b + 1536:c + 640])]
    ki = w_in[:, c + 1024:c + 1088]
    out += [blocks(w_in[:, c + 768:c + 1024]), blocks(np.concatenate([ki, ki], 1)),
            row_blocks(w_in[:, c + 640:c + 768]), row_blocks(w_in[:, c + 1088:c + 1092])]
    for j in range(0, D, 2 * P):
        for n in range(3):
            g = G_OFF + n * D + j
            out += [blocks(w_in[:, g:g + 2 * P]), blocks(w_branch[n][:, j:j + 2 * P])]
    out.append(blocks(w_o))
    for i in range(0, FF1, P):
        out += [blocks(w_up[:, i:i + P]), blocks(w_up[:, FF1 + i:FF1 + i + P])]
    out.append(blocks(w_down))
    return np.concatenate(out)


def stream2(w_in, w_uq, w_ukv, w_out, w_up, w_down):
    i, f = w_in[:, 1536:1540], w_in[:, 1540:1544]
    gap = np.zeros((D, 28), w_in.dtype)
    uq = np.pad(w_uq.reshape(384, 4, MLA_D), ((0, 0), (0, 0), (0, P - MLA_D))).reshape(384, 4 * P)
    kv = w_ukv.reshape(256, 4, 2, 64)
    out = [blocks(w_in[:, :512]), row_blocks(w_in[:, 512:1024]), blocks(w_in[:, 1024:1536]),
           blocks(np.concatenate([i, gap, f], 1)), blocks(w_in[:, 1544:2056]), row_blocks(w_in[:, 2056:2312]),
           blocks(w_in[:, 2312:2952]), blocks(w_in[:, 2952:2984]), blocks(uq),
           blocks(kv[:, :, 0].reshape(256, 256)), row_blocks(kv[:, :, 1].reshape(256, 256)),
           blocks(w_out), blocks(w_up), blocks(w_down)]
    out = np.concatenate(out)
    return np.concatenate([out, np.zeros((BLOCKS2 - len(out), P, P), out.dtype)])


def chunks(b):
    return b.reshape(-1, CHUNK, P, P).transpose(0, 2, 1, 3).reshape(-1, P, CHUNK * P)


def cols(v):
    return np.ascontiguousarray(v.reshape(-1, P).T)


def col(v, rows=P):
    return np.pad(v.reshape(-1, 1), ((0, rows - v.size), (0, 0)))


def constants():
    s, t = np.arange(P)[:, None], np.arange(P)[None, :]
    f = np.float32
    incl, strict = (s <= t).astype(f), (s < t).astype(f)

    def rotate(n, half, start, size):
        m = np.zeros((P, P), f)
        for base in range(0, n, size):
            for i in range(half):
                a, b = base + start + i, base + start + half + i
                m[b, a], m[a, b] = -1, 1
        return m

    rot = rotate(P, 32, 0, 64)
    dup = [np.zeros((P, P), f) for _ in range(2)]
    for c in range(2):
        for i in range(P):
            dup[c][64 * c + i % 64, i] = 1
    inv = (np.float32(10000.0) ** (-np.arange(32, dtype=f) * f(2.0 / 64))).astype(f)
    ang = (np.arange(T, dtype=f)[None, :] * np.tile(inv, 4)[:, None]).astype(f)
    sel = np.zeros((P, 4 * P), f)
    for h in range(4):
        sel[h, h * P:(h + 1) * P] = 1
    freq = np.zeros((P, 2), f)
    fp = np.power(f(500000.0), -np.arange(0, 16, 2, dtype=f) / f(16)).astype(f)
    fd = np.power(f(10000.0), -np.arange(0, 32, 2, dtype=f) / f(32)).astype(f)
    for base in (0, 64):
        freq[base:base + 16, 0] = np.tile(fp, 2)
    freq[64:96, 1] = np.tile(fd, 2)
    parts = {"ident": np.eye(P, dtype=f), "ones": np.ones((P, P), f), "bones": ((s // 64) == (t // 64)).astype(f),
             "pairmask": np.concatenate([strict, incl] * 2, 1), "lower": (s > t).astype(f),
             "cneg": np.concatenate([np.zeros((P, P), f), np.where(t <= s, f(0), f(NEG))], 1),
             "rot": rot, "dup0": dup[0], "dup1": dup[1], "rdup0": dup[0] @ rot, "rdup1": dup[1] @ rot,
             "rotp": rotate(P, 8, 0, 64), "rotd": rotate(MLA_D, 16, 64, MLA_D),
             "cos": np.cos(ang).astype(f), "sin": np.sin(ang).astype(f), "sel": sel, "freq": freq}
    assert list(parts) == list(CST.at)
    up = []
    for k in range(LEVELS):
        m = 1 << k
        up.append(((s // (2 * m)) == (t // (2 * m))) & (s // m % 2 == 0) & (t // m % 2 == 1))
    masks = np.concatenate(up + [x.T for x in up] + [s == t], 1).astype(f)
    return np.concatenate([parts[n] for n in parts], 1).astype(f), masks


class Chain:

    def __init__(self, eng, sem):
        self.eng, self.sem, self.count = eng, sem, {}

    def link(self, ins, sem=None):
        sem = self.sem if sem is None else sem
        self.count[sem.num] = self.count.get(sem.num, 0) + 1
        ins.then_inc(sem, 1)
        self.eng.wait_ge(sem, self.count[sem.num])


class Banks:

    def __init__(self, names, tiles, full, free):
        self.slot = {n: (i % 8, i // 8) for i, n in enumerate(names)}
        assert len(self.slot) == len(names)
        self.tiles, self.full, self.free = tiles, full, free

    def open(self, pe, name):
        b, use = self.slot[name]
        if use:
            pe.wait_ge(self.free[b], use)
        return self.tiles[b]

    def full_of(self, name):
        return self.full[self.slot[name][0]]

    def wait(self, eng, name):
        b, use = self.slot[name]
        eng.wait_ge(self.full[b], use + 1)
        return self.tiles[b]

    def release(self, eng, name):
        eng.sem_inc(self.free[self.slot[name][0]], 1)


class Weights:

    def __init__(self, pe, ring, landed, used, first):
        self.pe, self.ring, self.landed, self.used, self.first = pe, ring, landed, used, first
        self.seen, self.next, self.pending = 0, 0, 0

    def take(self, n):
        q = self.next
        self.next += n
        while self.seen * CHUNK < self.next:
            c = self.seen
            self.pe.wait_ge(self.landed[c % RING], (self.first + c // RING + 1) * 16)
            self.seen += 1
        return q

    def block(self, q, n=1):
        c, at = q // CHUNK % RING, q % CHUNK * P
        assert q % CHUNK + n <= CHUNK
        return self.ring[:, c, at:at + n * P]

    def done(self, q):
        if q % CHUNK == CHUNK - 1:
            self.pending += 1


ATT1 = [("0a", 0, [0, 2, 4, 6]), ("0b", 0, [1, 3, 5, 7]), ("1a", 1, [0, 2]), ("1b", 1, [4, 6]), ("1c", 1, [1, 3]), ("1d", 1, [5, 7])]
ATT2 = [("0a", 0, [0, 2]), ("0b", 0, [1, 3]), ("1a", 1, [0, 2]), ("1b", 1, [1, 3])]
INDEX = [("I0a", 0, [0, 2]), ("I0b", 0, [1, 3]), ("I1a", 1, [0, 2]), ("I1b", 1, [1, 3])]
HALVES = [[0, 2, 4, 6], [1, 3, 5, 7]]


def att_groups(tag, batches):
    out = []
    for b, tt, heads in batches:
        out += [f"{tag}L{b}", f"{tag}P{b}"]
        if b == [x[0] for x in batches if x[1] == tt][0]:
            out.append(f"{tag}O{tt}")
    return out


def groups1():
    g = ["norm"] + [f"A{i}" for i in range(7)] + ["Wup0", "Wup1", "Aup0", "Aup1", "Gup0", "Gup1"]
    g += ["Bq0", "Bq1", "Bf0", "Bf1", "Bi0", "Bi1", "Bg0", "Bg1", "KK0", "KK1"]
    g += ["Cq0", "Cq1", "Ck", "Cqi", "Cki", "Cv", "BON0", "BON1"]
    for c in range(2):
        g += [f"Tb{c}", f"Tk{c}", f"Tv{c}"]
    for c in range(2):
        g += [f"S{c}{h}" for h in range(8)] + [f"N{c}0", f"N{c}1"]
        for k in range(1, LEVELS):
            for q in range(2):
                g += [f"O{c}{k}{q}", f"X{c}{k}{q}"] + ([f"Z{c}{k}{q}"] if k < LEVELS - 1 else [])
        g += [f"R{c}", f"SA{c}", f"Y{c}"] + (["ST"] if c == 0 else [])
    g += ["GM0", "GM1", "GV0", "GV1"]
    g += ["HT", "HS"] + [f"H{k}{c}" for k in range(LEVELS + 1) for c in range(2)] + ["HO0", "HO1", "HN0", "HN1"]
    g += ["Rq0", "Rq1", "Rkd", "Rkr", "Rqi", "Rki"] + [n for n, _, _ in INDEX]
    g += att_groups("C", ATT1)
    for j in range(4):
        for n in range(3):
            g += [f"G{j}{n}", f"M{j}{n}"]
    g += [f"WO{j}" for j in range(4)] + ["norm2"] + [f"U{i}" for i in range(22)] + [f"D{j}" for j in range(4)]
    return g


def groups2():
    g = ["norm", "qk0", "qk1", "mv0", "mv1", "mo0", "mo1", "if", "aq", "ak", "av", "cq0", "cq1", "ckv", "kpe"]
    g += ["acol"] + [x + str(h) for h in range(4) for x in ("gb", "sc", "nd")]
    g += ["mn0", "mn1", "nq", "nk", "rq", "rk"] + att_groups("B", ATT2) + ["bn"]
    g += ["ncq", "nckv", "uq0", "uq1", "uk0", "uk1", "uv", "nlq0", "nlq1", "nlk0", "nlk1", "rlq0", "rlq1", "rlk0", "rlk1"]
    g += att_groups("M", ATT2) + ["ln"]
    g += [f"WO{j}" for j in range(4)] + ["norm2"] + [f"U{i}" for i in range(16)] + [f"D{j}" for j in range(4)]
    return g


SIGNALS = """act_chain dve_chain squares_ready u_ready ready
    pmu_ready pmu_used raw_ready rwkv_low_ready squash_ready cum_ready decay_ready kk_ready kksq_ready rstd_in rstd_out
    rwkv_ops_ready bonus_in tm_ready sc_ready n_ready o1_ready xz_ready rhs_ready sa_ready state_ready y_ready gsq_ready
    ya_ready f_ready hcol_in hcol_out ls_in ls_out lse_in lse_out cum_b pairs_in pairs_ready hk_ready hqe_ready ketm_ready
    hstate_ready hsc_ready hosq_ready yb_ready rope_ready cv_ready logits_ready probs_in probs_ready pt_ready pv_done
    yc_ready gate_ready gate_used merged_ready conv_in conv_mid conv_out hidden_ready h_ready fresh_norm bi_ready
    bsg_ready gA_ready d_diff d_exp s_ready dn_ready v_ready em_ready latents_sq latents_ready""".split()


def build(nc, x, params1, params2, stream, cst_in, masks_in, pos_in, out, layers=(LAYERS, LAYERS)):
    ctx = ExitStack()
    with ctx:
        def sb(name, shape, dt=F32):
            return ctx.enter_context(nc.sbuf_tensor(name, shape, dt))

        def sem(name):
            return ctx.enter_context(nc.semaphore(name))

        landed = [sem(f"chunk_landed{i}") for i in range(RING)]
        slots_free, inputs_in, params_in, stored = sem("slots_free"), sem("inputs_in"), sem("params_in"), sem("stored")
        arrived, gathered, released, ready = sem("arrived"), sem("gathered"), sem("released"), sem("masks_ready")
        bank_full = [sem(f"bank_full{i}") for i in range(8)]
        bank_free = [sem(f"bank_free{i}") for i in range(8)]
        S = {n: sem(n) for n in SIGNALS}
        per_layer = range(bank_full[0].num, S[SIGNALS[-1]].num + 1)
        assert len(per_layer) == 16 + len(SIGNALS)

        ring = sb("ring", [P, RING, CHUNK * P])
        h = sb("h", [P, KD, T])
        u = sb("u", [P, KD, T])
        par = sb("par", [P, max(PAR1.size, PAR2.size)])
        cst = sb("cst", [P, CST.size])
        msk = sb("msk", [P, MASKS.size], U8)
        small = sb("small", [P, 128])
        ARENA = 33600
        arena = sb("arena", [P, ARENA])
        banks = [ctx.enter_context(nc.psum_tensor(f"bank{i}", [P, 512], F32)) for i in range(8)]

        class Carve:
            def __init__(self, start=0):
                self.at = start

            def __call__(self, n):
                a = self.at
                self.at += n
                assert self.at <= ARENA, self.at
                return arena[:, a:a + n]

        def K(name):
            return CST.of(cst, name)

        def v3(ap, n):
            return ap.rearrange("p (a b) -> p a b", a=n)

        def spread(ap, n):
            return ap.unsqueeze(1).to_broadcast([ap.shape[0], n, ap.shape[1]])

        def along(ap, n):
            return ap.unsqueeze(2).to_broadcast([ap.shape[0], ap.shape[1], n])

        upm = v3(MASKS.of(msk, "up"), LEVELS)
        lowm = v3(MASKS.of(msk, "low"), LEVELS)
        diagm = MASKS.of(msk, "diag")
        ident, ones, bones = K("ident"), K("ones"), K("bones")

        cv = Carve()
        pa = v3(cv(14 * T), 14)
        cc = v3(cv(8 * 129), 8)
        ar = cv(2048).rearrange("p (j a t) -> p j a t", j=8, a=2)
        einv, av, kk, kmod, bonus, gA = (cv(1024) for _ in range(6))
        low = cv(2 * T)
        tw, sg = low[:, 0:T], low[:, T:2 * T]
        rs = low
        btm, ktm, vtm = (v3(cv(1024), 2) for _ in range(3))
        sc = cv(4096).rearrange("p (h a t) -> p h a t", h=8, a=4)
        nn, xx, zz = (v3(cv(1024), 8) for _ in range(3))
        o1_flat = cv(1032)
        o1 = v3(o1_flat[:, 0:1024], 8)
        pmu = v3(o1_flat[:, 0:1028], 4)
        bq, bf, bsg, yb, yc = (cv(1024) for _ in range(5))
        sa, st = yc[:, 0:512], v3(yc[:, 512:1024], 4)
        bi = v3(cv(1024), 2)
        craw = v3(cv(9 * T), 9)
        cvt = v3(cv(T), 2)
        wi = cv(8)
        ya = pa[:, 0:4, :].rearrange("p a t -> p (a t)")
        merged = craw[:, 0:8, :].rearrange("p a t -> p (a t)")
        mask_in = craw.rearrange("p a t -> p (a t)")[:, 0:MASKS.size]
        end1 = cv.at
        hv = Carve(14 * T)
        hb, hE, hqk, hsc, hke, hqe, hks, hls = (hv(1024) for _ in range(8))
        ketm, hst = hv(512), hv(512)
        assert hv.at <= end1 - 5 * 1024 - 1024 - 9 * T - T - 8
        xv = Carve(14 * T)
        scr = v3(xv(512), 2)
        work = v3(xv(512), 2)
        tmp = xv(512)
        amask = v3(xv(512), 2)
        lg = [xv(512), xv(512)]
        pT = [xv(512), xv(512)]
        fv = Carve()
        hidden = v3(fv(32 * T), 32)
        cb = [v3(fv(512), 2) for _ in range(4)]
        squares = v3(sc.rearrange("p h a t -> p (h a t)")[:, 0:2048], KD)
        gate_buf = [lg[0], lg[1]]
        mtmp = pT[0]
        bv = Carve(len(range(32 * T)) + 4 * 512)
        tabs = [bv(T) for _ in range(4)]
        sq2 = v3(bv(8 * T), 8)
        qkraw = v3(bv(4 * T), 4)
        mvt = v3(bv(1024), 2)
        mo = v3(bv(4 * T), 4)
        ifr = bv(8 * T)
        acol = v3(bv(8), 2)
        dT = bv(384)
        sT = [bv(384), bv(384)]
        em, dn = bv(T), bv(T)
        mix = v3(bv(8 * T), 8)
        aqk = v3(bv(4 * T), 4)
        avt = v3(bv(512), 2)
        cqk = v3(bv(5 * T), 5)
        lqk = v3(bv(8 * T), 8)
        kpe = bv(T)
        lvt = v3(bv(512), 2)
        t512 = bv(512)
        lg2 = [bv(512), bv(512)]
        pT2 = [bv(512), bv(512)]
        sqb = bv(1024)
        mid, emid, eend = small[:, 0:8], small[:, 8:16], small[:, 16:24]
        lbc, lnA, ln1m, omlb = (small[:, 24 + 4 * i:28 + 4 * i] for i in range(4))
        m8, nmax, ssum = small[:, 40:48], small[:, 48:56], small[:, 56:64]
        omu = small[:, 64:78]
        nbf = small[:, 80:81]
        isz = small[:, 84:88]

        b1 = Banks(groups1(), banks, bank_full, bank_free)
        b2 = Banks(groups2(), banks, bank_full, bank_free)

        block = ctx.enter_context(nc.Block())

        def layer_end(eng, done, leader):
            eng.sem_inc(arrived, 1)
            if leader:
                eng.wait_ge(arrived, (done + 1) * 3)
                eng.sem_inc(gathered, 1)
                eng.sem_clear(per_layer)
                eng.sem_inc(released, 1)
            else:
                eng.wait_ge(released, done + 1)

        @block.sync
        def _(sp):
            sp.dma_start(h[:], x).then_inc(inputs_in, 16)
            sp.dma_start(cst[:], cst_in).then_inc(inputs_in, 16)
            sp.dma_start(mask_in, masks_in).then_inc(inputs_in, 16)
            n = (layers[0] * CH1 + layers[1] * CH2) // RING
            with sp.Fori(0, n) as r:
                for s in range(RING):
                    sp.wait_ge(slots_free, r * RING + (s + 1))
                    sp.dma_start(ring[:, s, :], stream[bass.ds(r * RING + s, 1)].rearrange("a p n -> p (a n)"))\
                      .then_inc(landed[s], 16)

        @block.tensor
        def _(pe):
            pe.sem_inc(slots_free, RING)

            def runner(B, W):
                def mm(o, l, r, start=True, stop=True, full=None, done=None):
                    ins = nc.tensor.matmul(o, l, r, start=start, stop=stop)
                    if full is not None:
                        ins.then_inc(B.full_of(full), 1)
                    elif done is not None:
                        ins.then_inc(done, 1)
                    elif W.pending:
                        W.pending -= 1
                        ins.then_inc(slots_free, 1)

                def project(name, tiles, act, K_=KD):
                    bank = B.open(pe, name)
                    for i in range(tiles):
                        q = W.take(K_)
                        for k in range(K_):
                            mm(bank[:, i * T:(i + 1) * T], W.block(q + k), act[:, k, :], k == 0, k == K_ - 1,
                               full=name if (i, k) == (tiles - 1, K_ - 1) else None)
                            W.done(q + k)

                def project_rows(names, act, width, K_=KD, ncols=None, at=0):
                    q = W.take(K_ * width)
                    n = width * P if ncols is None else ncols
                    for t in range(NT):
                        both = len(names) == 1
                        if t == 0 or not both:
                            bank = B.open(pe, names[t])
                        o = at + t * n if both else at
                        for k in range(K_):
                            last = (k == K_ - 1) and (not both or t == NT - 1)
                            mm(bank[:, o:o + n], act[:, k, t * P:(t + 1) * P], W.block(q + k * width, width)[:, 0:n],
                               k == 0, k == K_ - 1, full=names[-1 if both else t] if last else None)
                    for b in range(q, q + K_ * width):
                        W.done(b)

                def sums(name, mat, act, n, rows=P):
                    bank = B.open(pe, name)
                    for i in range(n):
                        mm(bank[0:rows, i * T:(i + 1) * T], mat, act[:, i, :], full=name if i == n - 1 else None)

                def total(name, act, n, mat=ones):
                    bank = B.open(pe, name)
                    for i in range(n):
                        mm(bank[:, 0:T], mat, act[:, i, :], i == 0, i == n - 1, full=name if i == n - 1 else None)

                def turn(name, tiles):
                    bank = B.open(pe, name)
                    for i, a in enumerate(tiles):
                        ins = nc.tensor.transpose(bank[:, i * P:(i + 1) * P], a, ident)
                    ins.then_inc(B.full_of(name), 1)

                def attention(tag, batches, q, k, v, pt, before=None):
                    def logits(i):
                        b, tt, heads = batches[i]
                        w = (tt + 1) * P
                        bank = B.open(pe, f"{tag}L{b}")
                        for j, hd in enumerate(heads):
                            mm(bank[:, j * w:(j + 1) * w], q(hd)[:, tt * P:(tt + 1) * P], k(hd)[:, 0:w],
                               full=f"{tag}L{b}" if j == len(heads) - 1 else None)

                    def value(i):
                        b, tt, heads = batches[i]
                        pe.wait_ge(S["probs_ready"], att_base[0] + i + 1)
                        turn(f"{tag}P{b}", [pt[0][i % 2][:, j * P:(j + 1) * P] for j in range(len(heads) * (tt + 1))])
                        pe.wait_ge(S["pt_ready"], att_base[0] + i + 1)
                        firsts = [x_[0] for x_ in batches if x_[1] == tt]
                        if b == firsts[0]:
                            B.open(pe, f"{tag}O{tt}")
                        o = B.tiles[B.slot[f"{tag}O{tt}"][0]]
                        for j, hd in enumerate(heads):
                            r, c = 64 * (hd % 2), hd // 2 * P
                            for s in range(tt + 1):
                                last = j == len(heads) - 1 and s == tt
                                at = (j * (tt + 1) + s) * P
                                mm(o[r:r + 64, c:c + P], v(hd, s), pt[1][i % 2][:, at:at + P], s == 0, s == tt,
                                   full=f"{tag}O{tt}" if last and b == firsts[-1] else None,
                                   done=S["pv_done"] if last and b != firsts[-1] else None)

                    for i in range(len(batches)):
                        logits(i)
                        value(i)
                    att_base[0] += len(batches)

                att_base = [0]
                return mm, project, project_rows, sums, total, turn, attention

            pe.wait_ge(inputs_in, 48)
            with pe.Fori(0, layers[0]) as l:
                W = Weights(pe, ring, landed, slots_free, l * (CH1 // RING))
                B = b1
                mm, project, project_rows, sums, total, turn, attention = runner(B, W)
                pe.wait_ge(S["squares_ready"], 1)
                total("norm", squares, KD)
                pe.wait_ge(S["u_ready"], KD)
                for i in range(7):
                    project(f"A{i}", 2, u)
                pe.wait_ge(params_in, (l + 1) * 16)
                up = PAR1.of(par, "wa_up")
                pe.wait_ge(S["rwkv_low_ready"], 1)
                for a, n in ((0, "Wup"), (64, "Aup")):
                    rhs = tw[0:64, :] if a == 0 else pa[64:128, 12, :]
                    for g in range(2):
                        bank = B.open(pe, f"{n}{g}")
                        for i in range(2):
                            j = 2 * g + i
                            mm(bank[:, i * T:(i + 1) * T], up[a:a + 64, j * P:(j + 1) * P], rhs,
                               full=f"{n}{g}" if i else None)
                pe.wait_ge(S["rwkv_low_ready"], 2)
                for g in range(2):
                    bank = B.open(pe, f"Gup{g}")
                    for i in range(2):
                        j = 2 * g + i
                        mm(bank[:, i * T:(i + 1) * T], PAR1.of(par, "g_up")[:, j * P:(j + 1) * P], sg,
                           full=f"Gup{g}" if i else None)
                for n in ("Bq0", "Bq1", "Bf0", "Bf1"):
                    project(n, 2, u)
                project_rows(["Bi0", "Bi1"], u, 4)
                for n in ("Bg0", "Bg1"):
                    project(n, 2, u)
                pe.wait_ge(S["kksq_ready"], 1)
                for g in range(2):
                    sums(f"KK{g}", bones, v3(bonus, 4)[:, 2 * g:2 * g + 2, :], 2)
                project("Cq0", 2, u)
                project("Cq1", 2, u)
                project("Ck", 1, u)
                project("Cqi", 2, u)
                project("Cki", 1, u)
                q = W.take(KD)
                bank = B.open(pe, "Cv")
                for t in range(NT):
                    for k in range(KD):
                        mm(bank[:, t * P:(t + 1) * P], u[:, k, t * P:(t + 1) * P], W.block(q + k), k == 0, k == KD - 1)
                for k in range(KD):
                    W.done(q + k)
                q = W.take(KD)
                for t in range(NT):
                    for k in range(KD):
                        mm(bank[:, T + 4 * t:T + 4 * t + 4], u[:, k, t * P:(t + 1) * P], W.block(q + k)[:, 0:4],
                           k == 0, k == KD - 1, full="Cv" if (t, k) == (NT - 1, KD - 1) else None)
                for k in range(KD):
                    W.done(q + k)
                pe.wait_ge(S["bonus_in"], 1)
                for g in range(2):
                    sums(f"BON{g}", bones, v3(bonus, 4)[:, 2 * g:2 * g + 2, :], 2)
                pe.wait_ge(S["rwkv_ops_ready"], 1)
                bt, kt = v3(av, 8), v3(einv, 8)
                for c in range(2):
                    turn(f"Tb{c}", [bt[:, 2 * j + c, :] for j in range(4)])
                    turn(f"Tk{c}", [kt[:, 2 * j + c, :] for j in range(4)])
                    turn(f"Tv{c}", [pa[:, 8 + j, c * P:(c + 1) * P] for j in range(4)])
                for c in range(2):
                    for hd in range(8):
                        r, j = 64 * (hd % 2), hd // 2 * 2 + c
                        bank = B.open(pe, f"S{c}{hd}")
                        both = ar[r:r + 64, j, :, :].rearrange("p a t -> p (a t)")
                        mm(bank[:, 0:T], bt[r:r + 64, j, :], both)
                        mm(bank[:, T:2 * T], kt[r:r + 64, j, :], both, full=f"S{c}{hd}")
                    for q in range(2):
                        bank = B.open(pe, f"N{c}{q}")
                        for i, hd in enumerate(HALVES[q]):
                            r, j = 64 * (hd % 2), hd // 2 * 2 + c
                            mm(bank[:, i * P:(i + 1) * P], ar[r:r + 64, j, 0, :], bt[r:r + 64, j, :],
                               full=f"N{c}{q}" if i == 3 else None)
                    for k in range(1, LEVELS):
                        for q in range(2):
                            pe.wait_ge(S["xz_ready"], c * 2 * LEVELS + (k - 1) * 2 + q + 1)
                            bank = B.open(pe, f"O{c}{k}{q}")
                            for i in range(4):
                                hd = 4 * q + i
                                mm(bank[:, i * P:(i + 1) * P], nn[:, hd, :], xx[:, hd, :],
                                   full=f"O{c}{k}{q}" if i == 3 else None)
                        for q in range(2):
                            pe.wait_ge(S["o1_ready"], c * 2 * (LEVELS - 1) + (k - 1) * 2 + q + 1)
                            for n, l_, r_ in (("X", zz, o1), ("Z", o1, zz)):
                                if n == "Z" and k == LEVELS - 1:
                                    continue
                                bank = B.open(pe, f"{n}{c}{k}{q}")
                                for i in range(4):
                                    hd = 4 * q + i
                                    mm(bank[:, i * P:(i + 1) * P], l_[:, hd, :], r_[:, hd, :],
                                       full=f"{n}{c}{k}{q}" if i == 3 else None)
                    pe.wait_ge(S["tm_ready"], 6)
                    bank = B.open(pe, f"R{c}")
                    for j in range(4):
                        if c:
                            if j == 0:
                                pe.wait_ge(S["state_ready"], 1)
                            mm(bank[:, j * P:(j + 1) * P], ar[:, 2 * j + c, 0, :], st[:, j, :], True, False)
                        for hd in (2 * j, 2 * j + 1):
                            mm(bank[:, hd * 64:hd * 64 + 64], sc[:, hd, 2, :], vtm[:, c, hd * 64:hd * 64 + 64], c == 0, c == 0 or hd % 2 == 1,
                               full=f"R{c}" if hd == 7 else None)
                    pe.wait_ge(S["rhs_ready"], c + 1)
                    pe.wait_ge(S["xz_ready"], (c + 1) * 2 * LEVELS)
                    bank = B.open(pe, f"SA{c}")
                    for hd in range(8):
                        mm(bank[:, hd * 64:hd * 64 + 64], xx[:, 4 * (hd % 2) + hd // 2, :], rs[:, hd * 64:hd * 64 + 64],
                           full=f"SA{c}" if hd == 7 else None)
                    pe.wait_ge(S["sa_ready"], c + 1)
                    bank = B.open(pe, f"Y{c}")
                    for j in range(4):
                        if c:
                            mm(bank[:, j * P:(j + 1) * P], st[:, j, :], ar[:, 2 * j + c, 1, :], True, False)
                        for hd in (2 * j, 2 * j + 1):
                            r = 64 * (hd % 2)
                            o = bank[r:r + 64, j * P:(j + 1) * P]
                            mm(o, sa[:, hd * 64:hd * 64 + 64], sc[:, hd, 1, :], c == 0, False)
                            mm(o, vtm[:, c, hd * 64:hd * 64 + 64], sc[:, hd, 3, :], False, True,
                               full=f"Y{c}" if hd == 7 else None)
                    if c == 0:
                        bank = B.open(pe, "ST")
                        for hd in range(8):
                            r, j = 64 * (hd % 2), hd // 2
                            o = bank[r:r + 64, j * 64:(j + 1) * 64]
                            mm(o, btm[:, 0, hd * 64:hd * 64 + 64], sa[:, hd * 64:hd * 64 + 64], True, False)
                            mm(o, ktm[:, 0, hd * 64:hd * 64 + 64], vtm[:, 0, hd * 64:hd * 64 + 64], False, True,
                               full="ST" if hd == 7 else None)
                pe.wait_ge(S["y_ready"], 2)
                for g in range(2):
                    sums(f"GM{g}", bones, v3(ya, 4)[:, 2 * g:2 * g + 2, :], 2)
                pe.wait_ge(S["gsq_ready"], 1)
                for g in range(2):
                    sums(f"GV{g}", bones, v3(kk, 4)[:, 2 * g:2 * g + 2, :], 2)
                pe.wait_ge(S["hk_ready"], 1)
                turn("HT", [v3(hke, 8)[:, hd, :] for hd in range(4)])
                pe.wait_ge(S["ketm_ready"], 1)
                pe.wait_ge(S["bi_ready"], 2)
                bank = B.open(pe, "HS")
                for hd in range(4):
                    mm(bank[:, hd * P:(hd + 1) * P], ketm[:, hd * P:(hd + 1) * P], bi[:, 0, hd * P:(hd + 1) * P],
                       full="HS" if hd == 3 else None)
                for k in range(LEVELS + 1):
                    pe.wait_ge(S["pairs_ready"], k + 1)
                    qk = v3(hqk, 8)
                    for c in range(2):
                        bank = B.open(pe, f"H{k}{c}")
                        for hd in range(4):
                            i = 2 * hd + c
                            l_, r_ = (qk[:, i, :], qk[:, i, :]) if k < LEVELS else (v3(hks, 8)[:, i, :], v3(bq, 8)[:, i, :])
                            mm(bank[:, hd * P:(hd + 1) * P], l_, r_, full=f"H{k}{c}" if hd == 3 else None)
                pe.wait_ge(S["hsc_ready"], 1)
                pe.wait_ge(S["hqe_ready"], 1)
                pe.wait_ge(S["hstate_ready"], 1)
                for c in range(2):
                    bank = B.open(pe, f"HO{c}")
                    for hd in range(4):
                        o = bank[:, hd * P:(hd + 1) * P]
                        mm(o, bi[:, c, hd * P:(hd + 1) * P], v3(hsc, 8)[:, 2 * hd + c, :], True, c == 0,
                           full=f"HO{c}" if c == 0 and hd == 3 else None)
                        if c:
                            mm(o, v3(hst, 4)[:, hd, :], v3(hqe, 8)[:, hd, :], False, True,
                               full=f"HO{c}" if hd == 3 else None)
                pe.wait_ge(S["hosq_ready"], 2)
                for g in range(2):
                    sums(f"HN{g}", ones, v3(hE, 4)[:, 2 * g:2 * g + 2, :], 2)
                pe.wait_ge(S["raw_ready"], 5)
                sums("Rq0", K("rot"), craw[:, 0:2, :], 2)
                sums("Rq1", K("rot"), craw[:, 2:4, :], 2)
                for n, ms in (("Rkd", ("dup0", "dup1")), ("Rkr", ("rdup0", "rdup1"))):
                    bank = B.open(pe, n)
                    for i, m in enumerate(ms):
                        mm(bank[:, i * T:(i + 1) * T], K(m), craw[:, 7, :], full=n if i else None)
                sums("Rqi", K("rot"), craw[:, 4:6, :], 2)
                sums("Rki", K("rot"), craw[:, 6:7, :], 1)
                pe.wait_ge(S["rope_ready"], 1)

                def index(name, tt, heads):
                    w = (tt + 1) * P
                    bank = B.open(pe, name)
                    for i, hd in enumerate(heads):
                        r = 64 * (hd % 2)
                        mm(bank[:, i * w:(i + 1) * w], craw[r:r + 64, 4 + hd // 2, tt * P:(tt + 1) * P],
                           craw[r:r + 64, 6, 0:w], full=name if i == len(heads) - 1 else None)

                for n, tt, heads in INDEX:
                    index(n, tt, heads)

                def part(hd):
                    return slice(64 * (hd % 2), 64 * (hd % 2) + 64)

                attention("C", ATT1, lambda hd: craw[part(hd), hd // 2, :], lambda hd: craw[part(hd), 7 + hd // 4, :],
                          lambda hd, s: cvt[:, s, hd // 4 * 64:hd // 4 * 64 + 64], (lg, pT))
                pe.wait_ge(S["ya_ready"], 1)
                pe.wait_ge(S["yb_ready"], 1)
                pe.wait_ge(S["yc_ready"], 2)
                ys = [v3(ya, 4), v3(yb, 4), v3(yc, 4)]
                for j in range(4):
                    for n in range(3):
                        project(f"G{j}{n}", 2, u)
                        project(f"M{j}{n}", 2, ys[n], 4)
                pe.wait_ge(S["merged_ready"], 4)
                for j in range(4):
                    project(f"WO{j}", 2, v3(merged, KD))
                pe.wait_ge(S["squares_ready"], 2)
                total("norm2", squares, KD)
                pe.wait_ge(S["u_ready"], 2 * KD)
                for i in range(22):
                    project(f"U{i}", 2, u)
                pe.wait_ge(S["hidden_ready"], 22)
                for j in range(4):
                    project(f"D{j}", 2, hidden, 22)
                B.wait(pe, "D3")
                pe.sem_inc(slots_free, W.pending)
                assert W.next == BLOCKS1
                layer_end(pe, l, False)

            W = Weights(pe, ring, landed, slots_free, 0)
            total_ = runner(b2, W)[4]
            pe.wait_ge(S["squares_ready"], 1)
            total_("norm", squares, KD)
            pe.wait_ge(S["ready"], 1)
            nc.tensor.matmul(banks[1][:, 0:T], ones[0:1, :], t512[0:1, 0:T], start=True, stop=True)\
              .then_inc(bank_full[1], 1)
            layer_end(pe, layers[0], False)

            if not layers[1]:
                return
            with pe.Fori(0, layers[1]) as l:
                W = Weights(pe, ring, landed, slots_free, l * (CH2 // RING) + layers[0] * (CH1 // RING))
                B = b2
                mm, project, project_rows, sums, total, turn, attention = runner(B, W)
                pe.wait_ge(S["squares_ready"], 1)
                total("norm", squares, KD)
                pe.wait_ge(S["u_ready"], KD)
                project("qk0", 2, u)
                project("qk1", 2, u)
                project_rows(["mv0", "mv1"], u, 4)
                project("mo0", 2, u)
                project("mo1", 2, u)
                bank = B.open(pe, "if")
                q = W.take(KD)
                for i in range(2):
                    for k in range(KD):
                        mm(bank[0:4, i * T:(i + 1) * T], W.block(q + k)[:, 32 * i:32 * i + 4], u[:, k, :], k == 0, k == KD - 1,
                           full="if" if (i, k) == (1, KD - 1) else None)
                for k in range(KD):
                    W.done(q + k)
                project("aq", 2, u)
                project("ak", 2, u)
                project_rows(["av"], u, 2)
                project("cq0", 2, u)
                project("cq1", 1, u)
                project("ckv", 2, u)
                bank = B.open(pe, "kpe")
                q = W.take(KD)
                for k in range(KD):
                    mm(bank[64:96, 0:T], W.block(q + k)[:, 0:32], u[:, k, :], k == 0, k == KD - 1,
                       full="kpe" if k == KD - 1 else None)
                    W.done(q + k)
                pe.wait_ge(S["d_diff"], 1)
                bank = B.open(pe, "acol")
                for t in range(NT):
                    ins = nc.tensor.transpose(bank[:, 4 * t:4 * t + 4], ifr[0:4, t * P:(t + 1) * P], ident[0:4, 0:4])
                ins.then_inc(B.full_of("acol"), 1)
                pe.wait_ge(S["conv_out"], 4)
                pe.wait_ge(S["v_ready"], 2)
                for hd in range(4):
                    bank = B.open(pe, f"gb{hd}")
                    mm(bank[:, 0:2 * T], K("sel")[0:4, hd * P:(hd + 1) * P], ifr[0:4, 2 * T:4 * T], full=f"gb{hd}")
                    bank = B.open(pe, f"sc{hd}")
                    r = 64 * (hd % 2)
                    qh, kh = qkraw[r:r + 64, hd // 2, :], qkraw[r:r + 64, 2 + hd // 2, :]
                    mm(bank[:, 0:T], kh[:, 0:P], qh)
                    mm(bank[:, T:T + P], kh[:, P:T], qh[:, P:T], full=f"sc{hd}")
                    pe.wait_ge(S["s_ready"], hd + 1)
                    bank = B.open(pe, f"nd{hd}")
                    s_ = sT[hd % 2]
                    for o, l0, l1 in ((0, mvt[:, 0, hd * P:(hd + 1) * P], mvt[:, 1, hd * P:(hd + 1) * P]), (T, ones, ones)):
                        mm(bank[:, o:o + T], l0, s_[:, 0:T], True, False)
                        mm(bank[:, o + P:o + T], l1, s_[:, T:T + P], False, True, full=f"nd{hd}" if o else None)
                pe.wait_ge(S["hosq_ready"], 1)
                for g in range(2):
                    sums(f"mn{g}", ones, v3(sqb, 4)[:, 2 * g:2 * g + 2, :], 2)
                pe.wait_ge(S["kksq_ready"], 1)
                sums("nq", bones, v3(sqb, 4)[:, 0:2, :], 2)
                sums("nk", bones, v3(sqb, 4)[:, 2:4, :], 2)
                pe.wait_ge(S["kk_ready"], 1)
                sums("rq", K("rotp"), aqk[:, 0:2, :], 2)
                sums("rk", K("rotp"), aqk[:, 2:4, :], 2)
                pe.wait_ge(S["rope_ready"], 1)

                def part(hd):
                    return slice(64 * (hd % 2), 64 * (hd % 2) + 64)

                attention("B", ATT2, lambda hd: aqk[part(hd), hd // 2, :], lambda hd: aqk[part(hd), 2 + hd // 2, :],
                          lambda hd, s: avt[:, s, hd * 64:hd * 64 + 64], (lg2, pT2))
                pe.wait_ge(S["gsq_ready"], 2)
                sums("bn", bones, v3(sqb, 4)[:, 0:2, :], 2)
                pe.wait_ge(S["latents_sq"], 1)
                total("ncq", sq2[:, 0:3, :], 3)
                total("nckv", sq2[:, 3:5, :], 2)
                pe.wait_ge(S["latents_ready"], 1)
                for g in range(2):
                    bank = B.open(pe, f"uq{g}")
                    for i in range(2):
                        q = W.take(3)
                        for k in range(3):
                            mm(bank[0:MLA_D, i * T:(i + 1) * T], W.block(q + k)[:, 0:MLA_D], cqk[:, k, :], k == 0, k == 2,
                               full=f"uq{g}" if (i, k) == (1, 2) else None)
                            W.done(q + k)
                for g in range(2):
                    bank = B.open(pe, f"uk{g}")
                    q = W.take(2)
                    for i in range(2):
                        for k in range(2):
                            mm(bank[0:64, i * T:(i + 1) * T], W.block(q + k)[:, 64 * i:64 * i + 64], cqk[:, 3 + k, :],
                               k == 0, k == 1, full=f"uk{g}" if (i, k) == (1, 1) else None)
                    W.done(q)
                    W.done(q + 1)
                project_rows(["uv"], cqk[:, 3:5, :], 2, 2)
                pe.wait_ge(S["lse_in"], 1)
                for n, o in (("nlq", 0), ("nlk", 4)):
                    for g in range(2):
                        sums(f"{n}{g}", ones[0:MLA_D, 0:MLA_D], sq2[0:MLA_D, o + 2 * g:o + 2 * g + 2, :], 2, MLA_D)
                pe.wait_ge(S["lse_out"], 1)
                for n, o in (("rlq", 0), ("rlk", 4)):
                    for g in range(2):
                        sums(f"{n}{g}", K("rotd")[0:MLA_D, 0:MLA_D], lqk[0:MLA_D, o + 2 * g:o + 2 * g + 2, :], 2, MLA_D)
                pe.wait_ge(S["rope_ready"], 2)
                attention("M", ATT2, lambda hd: lqk[0:MLA_D, hd, :], lambda hd: lqk[0:MLA_D, 4 + hd, :],
                          lambda hd, s: lvt[:, s, hd * 64:hd * 64 + 64], (lg2, pT2))
                pe.wait_ge(S["gsq_ready"], 4)
                sums("ln", bones, v3(sqb, 4)[:, 0:2, :], 2)
                pe.wait_ge(S["yc_ready"], 1)
                for j in range(4):
                    project(f"WO{j}", 2, mix)
                pe.wait_ge(S["squares_ready"], 2)
                total("norm2", squares, KD)
                pe.wait_ge(S["u_ready"], 2 * KD)
                for i in range(16):
                    project(f"U{i}", 2, u)
                pe.wait_ge(S["hidden_ready"], 16)
                for j in range(4):
                    project(f"D{j}", 2, hidden, 32)
                B.wait(pe, "D3")
                W.take(BLOCKS2 - W.next)
                pe.sem_inc(slots_free, W.pending + 1)
                layer_end(pe, l + (layers[0] + 1), False)

        @block.scalar
        def _(act):
            def A(o, i, f, **kw):
                return nc.scalar.activation(o, i, f, **kw)

            def norm_squares(C):
                C.link(A(squares.rearrange("p k t -> p (k t)"), h[:].rearrange("p k t -> p (k t)"), ACT.Square), S["squares_ready"])

            def root(C, ap, n):
                act.wait_ge(S["rstd_in"], n)
                C.link(A(ap, ap, ACT.Sqrt), S["rstd_out"])

            def attention(C, B, tag, batches, base, lgs, pts, take):
                for i, (b, tt, heads) in enumerate(batches):
                    w = (tt + 1) * P
                    act.wait_ge(S["probs_in"], base + i + 1)
                    for j in range(len(heads)):
                        C.link(A(lgs[i % 2][:, j * w:(j + 1) * w], lgs[i % 2][:, j * w:(j + 1) * w], ACT.Exp,
                                 bias=nmax[:, j:j + 1], accum_out=ssum[:, j:j + 1]))
                    act.sem_inc(S["logits_ready"], 1)
                    bank = B.wait(act, f"{tag}P{b}")
                    C.link(A(pts[i % 2][:, 0:len(heads) * w], bank[:, 0:len(heads) * w], ACT.Copy), S["pt_ready"])
                    B.release(act, f"{tag}P{b}")
                    if b == [x_[0] for x_ in batches if x_[1] == tt][-1]:
                        bank = B.wait(act, f"{tag}O{tt}")
                        take(tt, bank)
                        B.release(act, f"{tag}O{tt}")

            act.wait_ge(inputs_in, 48)
            with act.Fori(0, layers[0]) as l:
                C, B = Chain(act, S["act_chain"]), b1
                act.dma_start(par[:, 0:PAR1.size], params1[bass.ds(l, 1)].rearrange("a p n -> p (a n)")).then_inc(params_in, 16)
                norm_squares(C)
                root(C, tw, 1)
                act.wait_ge(params_in, (l + 1) * 16)
                mu = PAR1.of(par, "mu")
                for i in range(14):
                    bank = B.wait(act, f"A{i // 2}")
                    if i == 0:
                        act.wait_ge(S["pmu_used"], 1)
                    if i >= 4:
                        act.wait_ge(S["pmu_used"], 2 * (i // 2) - 1)
                    C.link(A(pmu[:, i % 4, 1:], bank[:, i % 2 * T:(i % 2 + 1) * T], ACT.Copy, scale=mu[:, i:i + 1]), S["pmu_ready"])
                act.wait_ge(S["pmu_used"], 15)
                C.link(A(tw[0:64, :], pa[0:64, 12, :], ACT.Tanh), S["rwkv_low_ready"])
                C.link(A(sg, pa[:, 13, :], ACT.Sigmoid), S["rwkv_low_ready"])
                for n, o, z in (("Wup", einv, "w0"), ("Aup", av, "a0")):
                    for g in range(2):
                        bank = B.wait(act, f"{n}{g}")
                        for i in range(2):
                            j = 2 * g + i
                            C.link(A(v3(o, 4)[:, j, :], bank[:, i * T:(i + 1) * T], ACT.Sigmoid,
                                     bias=PAR1.of(par, z)[:, j:j + 1]), S["squash_ready"])
                        B.release(act, f"{n}{g}")
                for g in range(2):
                    bank = B.wait(act, f"Gup{g}")
                    C.link(A(gA[:, g * 512:(g + 1) * 512], bank[:, :], ACT.Copy), S["gA_ready"])
                    B.release(act, f"Gup{g}")
                act.wait_ge(S["kk_ready"], 1)
                C.link(A(bonus, kk, ACT.Square), S["kksq_ready"])
                for g in range(2):
                    bank = B.wait(act, f"Bq{g}")
                    C.link(A(bq[:, g * 512:(g + 1) * 512], bank[:, :], ACT.Copy))
                    B.release(act, f"Bq{g}")
                act.wait_ge(S["cum_ready"], 1)
                C.link(A(emid, mid, ACT.Exp, scale=-KAPPA))
                C.link(A(eend, cc[:, :, P], ACT.Exp, scale=-KAPPA))
                C.link(A(ar[:, :, 0, :], cc[:, :, 0:P], ACT.Exp, scale=-KAPPA))
                C.link(A(ar[:, :, 1, :], cc[:, :, 1:P + 1], ACT.Exp, scale=-KAPPA))
                C.link(A(v3(einv, 8), cc[:, :, 1:P + 1], ACT.Exp, scale=KAPPA), S["decay_ready"])
                for t in range(NT):
                    bank = B.wait(act, f"Bi{t}")
                    C.link(A(bi[:, t, :], bank[:, :], ACT.Copy), S["bi_ready"])
                    B.release(act, f"Bi{t}")
                for g in range(2):
                    bank = B.wait(act, f"Bg{g}")
                    C.link(A(bsg[:, g * 512:(g + 1) * 512], bank[:, :], ACT.Silu), S["bsg_ready"])
                    B.release(act, f"Bg{g}")
                root(C, bonus, 2)
                for n, o, w in (("Cq0", 0, 2), ("Cq1", 2, 2), ("Ck", 7, 1), ("Cqi", 4, 2), ("Cki", 6, 1)):
                    bank = B.wait(act, n)
                    C.link(A(craw[:, o:o + w, :].rearrange("p a t -> p (a t)"), bank[:, 0:w * T], ACT.Copy), S["raw_ready"])
                    B.release(act, n)
                for c in range(2):
                    for n, o in (("Tb", btm), ("Tk", ktm), ("Tv", vtm)):
                        bank = B.wait(act, f"{n}{c}")
                        C.link(A(o[:, c, :], bank[:, :], ACT.Copy), S["tm_ready"])
                        B.release(act, f"{n}{c}")
                for c in range(2):
                    for k in range(1, LEVELS):
                        for q in range(2):
                            bank = B.wait(act, f"O{c}{k}{q}")
                            C.link(A(o1[:, 4 * q:4 * q + 4, :].rearrange("p a t -> p (a t)"), bank[:, :], ACT.Copy), S["o1_ready"])
                            B.release(act, f"O{c}{k}{q}")
                    bank = B.wait(act, f"R{c}")
                    C.link(A(rs, bank[:, :], ACT.Copy), S["rhs_ready"])
                    B.release(act, f"R{c}")
                    bank = B.wait(act, f"SA{c}")
                    C.link(A(sa, bank[:, :], ACT.Copy), S["sa_ready"])
                    B.release(act, f"SA{c}")
                    bank = B.wait(act, f"Y{c}")
                    C.link(A(v3(ya, 4)[:, :, c * P:(c + 1) * P], v3(bank[:, :], 4), ACT.Copy), S["y_ready"])
                    B.release(act, f"Y{c}")
                act.wait_ge(S["fresh_norm"], 1)
                C.link(A(kk, ya, ACT.Square), S["gsq_ready"])
                root(C, kk, 3)
                act.wait_ge(S["hcol_in"], 1)
                C.link(A(lbc, lbc, ACT.Exp), S["hcol_out"])
                act.wait_ge(S["hcol_in"], 2)
                C.link(A(lnA, lnA, ACT.Ln))
                C.link(A(ln1m, ln1m, ACT.Ln), S["hcol_out"])
                act.wait_ge(S["ls_in"], 1)
                C.link(A(hE, bf, ACT.Abs))
                C.link(A(hE, hE, ACT.Exp, scale=-1.0))
                C.link(A(hE, hE, ACT.Ln, bias=1.0), S["ls_out"])
                act.wait_ge(S["lse_in"], 1)
                C.link(A(hks, hks, ACT.Exp))
                C.link(A(hE, hE, ACT.Abs))
                C.link(A(hE, hE, ACT.Exp, scale=-1.0))
                C.link(A(hE, hE, ACT.Ln, bias=1.0), S["lse_out"])
                act.wait_ge(S["cum_b"], 1)
                b8 = v3(hb, 8)
                for hd in range(4):
                    C.link(A(v3(hke, 8)[:, hd, :], b8[:, 2 * hd, :], ACT.Exp, scale=-1.0, bias=b8[:, 2 * hd, P - 1:P]))
                C.link(A(v3(hqe, 8)[:, 0:4, :], b8[:, 1:8:2, :], ACT.Exp), S["d_exp"])
                for k in range(LEVELS):
                    act.wait_ge(S["pairs_in"], k + 1)
                    C.link(A(hE, hE, ACT.Exp), S["d_exp"])
                    if k == 0:
                        bank = B.wait(act, "HT")
                        C.link(A(ketm, bank[:, :], ACT.Copy), S["ketm_ready"])
                        B.release(act, "HT")
                        bank = B.wait(act, "HS")
                        C.link(A(hst, bank[:, :], ACT.Copy), S["hstate_ready"])
                        B.release(act, "HS")
                for c in range(2):
                    bank = B.wait(act, f"HO{c}")
                    C.link(A(v3(yb, 4)[:, :, c * P:(c + 1) * P], v3(bank[:, :], 4), ACT.Copy))
                    C.link(A(v3(hE, 4)[:, :, c * P:(c + 1) * P], v3(bank[:, :], 4), ACT.Square), S["hosq_ready"])
                    B.release(act, f"HO{c}")
                root(C, hE, 4)

                def take_c(tt, bank):
                    C.link(A(v3(yc, 4)[:, :, tt * P:(tt + 1) * P], v3(bank[:, :], 4), ACT.Copy), S["yc_ready"])

                attention(C, B, "C", ATT1, 0, lg, pT, take_c)
                for i in range(12):
                    n = f"G{i // 3}{i % 3}"
                    bank = B.wait(act, n)
                    if i == 0:
                        act.wait_ge(S["h_ready"], 1)
                    if i >= 2:
                        act.wait_ge(S["gate_used"], i - 1)
                    C.link(A(gate_buf[i % 2], bank[:, :], ACT.Sigmoid), S["gate_ready"])
                    B.release(act, n)
                act.wait_ge(S["h_ready"], 2)
                norm_squares(C)
                root(C, tmp[:, 0:T], 5)
                for i in range(23):
                    if i < 22:
                        bank = B.wait(act, f"U{i}")
                        if i >= 4:
                            act.wait_ge(S["hidden_ready"], i - 3)
                        for j, t in ((0, i), (1, 22 + i)):
                            C.link(A(cb[i % 4][:, j, :], bank[:, j * T:(j + 1) * T], ACT.Identity,
                                     scale=PAR1.of(par, "conv_w2")[:, t:t + 1], bias=PAR1.of(par, "conv_b")[:, t:t + 1]))
                        act.sem_inc(S["conv_in"], 1)
                    if i:
                        act.wait_ge(S["conv_mid"], i)
                        C.link(A(cb[(i - 1) % 4][:, 0, :], cb[(i - 1) % 4][:, 0, :], ACT.Silu), S["conv_out"])
                layer_end(act, l, False)

            C, B = Chain(act, S["act_chain"]), b2
            act.dma_start(t512.bitcast(I32)[0:1, T:2 * T], pos_in).then_inc(inputs_in, 16)
            norm_squares(C)
            root(C, tmp[:, 0:T], 1)
            for i in range(4):
                act.wait_ge(S["cum_ready"], i + 1)
                C.link(A(tabs[i], tabs[i], ACT.Sin), S["decay_ready"])
            layer_end(act, layers[0], False)

            if not layers[1]:
                act.dma_start(out, h[:]).then_inc(stored, 16)
                act.wait_ge(stored, 16)
                return
            with act.Fori(0, layers[1]) as l:
                C, B = Chain(act, S["act_chain"]), b2
                act.dma_start(par[:, 0:PAR2.size], params2[bass.ds(l, 1)].rearrange("a p n -> p (a n)")).then_inc(params_in, 16)
                norm_squares(C)
                root(C, dn, 1)
                act.wait_ge(params_in, (l + (layers[0] + 1)) * 16)
                cw = v3(PAR2.of(par, "conv_w"), 4)
                for i in range(4):
                    bank = B.wait(act, f"qk{i // 2}")
                    C.link(A(qkraw[:, i, :], bank[:, i % 2 * T:(i % 2 + 1) * T], ACT.Identity, scale=cw[:, 3, i:i + 1],
                             bias=PAR2.of(par, "conv_b")[:, i:i + 1]), S["conv_in"])
                for t in range(NT):
                    bank = B.wait(act, f"mv{t}")
                    C.link(A(mvt[:, t, :], bank[:, :], ACT.Copy), S["v_ready"])
                    B.release(act, f"mv{t}")
                for i in range(4):
                    act.wait_ge(S["conv_mid"], i + 1)
                    C.link(A(qkraw[:, i, :], qkraw[:, i, :], ACT.Silu), S["conv_out"])
                for g in range(2):
                    bank = B.wait(act, f"mo{g}")
                    C.link(A(mo[:, 2 * g:2 * g + 2, :].rearrange("p a t -> p (a t)"), bank[:, :], ACT.Sigmoid), S["bsg_ready"])
                    B.release(act, f"mo{g}")
                act.wait_ge(S["ls_in"], 1)
                fz = ifr[0:4, 4 * T:5 * T]
                C.link(A(fz, fz, ACT.Abs))
                C.link(A(fz, fz, ACT.Exp, scale=-1.0))
                C.link(A(fz, fz, ACT.Ln, bias=1.0), S["hcol_out"])
                for n, o, w in (("aq", aqk[:, 0:2, :], 2), ("ak", aqk[:, 2:4, :], 2)):
                    bank = B.wait(act, n)
                    C.link(A(o.rearrange("p a t -> p (a t)"), bank[:, :], ACT.Copy), S["raw_ready"])
                    B.release(act, n)
                bank = B.wait(act, "av")
                C.link(A(avt.rearrange("p a t -> p (a t)"), bank[:, :], ACT.Copy))
                B.release(act, "av")
                for n, o, w in (("cq0", 0, 2), ("cq1", 2, 1), ("ckv", 3, 2)):
                    bank = B.wait(act, n)
                    C.link(A(cqk[:, o:o + w, :].rearrange("p a t -> p (a t)"), bank[:, 0:w * T], ACT.Copy))
                    B.release(act, n)
                bank = B.wait(act, "kpe")
                C.link(A(kpe[64:96, :], bank[64:96, 0:T], ACT.Copy), S["raw_ready"])
                B.release(act, "kpe")
                for hd in range(4):
                    bank = B.wait(act, f"gb{hd}")
                    if hd:
                        act.wait_ge(S["dn_ready"], hd)
                    C.link(A(em, bank[:, T:2 * T], ACT.Exp), S["em_ready"])
                    act.wait_ge(S["pairs_in"], hd + 1)
                    C.link(A(dT, dT, ACT.Exp, scale=-1.0), S["d_exp"])
                act.wait_ge(S["dn_ready"], 4)
                C.link(A(sqb, mix[:, 0:4, :].rearrange("p a t -> p (a t)"), ACT.Square), S["hosq_ready"])
                root(C, sqb, 2)
                act.wait_ge(S["yb_ready"], 1)
                C.link(A(sqb, aqk[:, :, :].rearrange("p a t -> p (a t)"), ACT.Square), S["kksq_ready"])
                root(C, sqb, 3)

                def take_heads(o):
                    def take(tt, bank):
                        C.link(A(mix[:, o:o + 2, tt * P:(tt + 1) * P], v3(bank[:, 0:2 * P], 2), ACT.Copy))
                        C.link(A(v3(sqb, 4)[:, 0:2, tt * P:(tt + 1) * P], v3(bank[:, 0:2 * P], 2), ACT.Square), S["gsq_ready"])
                    return take

                attention(C, B, "B", ATT2, 0, lg2, pT2, take_heads(4))
                root(C, sqb[:, 0:512], 4)
                C.link(A(sq2[:, 0:5, :].rearrange("p a t -> p (a t)"), cqk[:, :, :].rearrange("p a t -> p (a t)"), ACT.Square), S["latents_sq"])
                root(C, t512, 5)
                for n, o in (("uq", 0), ("uk", 4)):
                    rows = MLA_D if n == "uq" else 64
                    for g in range(2):
                        bank = B.wait(act, f"{n}{g}")
                        C.link(A(lqk[0:rows, o + 2 * g:o + 2 * g + 2, :].rearrange("p a t -> p (a t)"), bank[0:rows, :], ACT.Copy))
                        B.release(act, f"{n}{g}")
                C.link(A(lqk[64:96, 4:8, :], spread(kpe, 4)[64:96], ACT.Copy))
                bank = B.wait(act, "uv")
                C.link(A(lvt.rearrange("p a t -> p (a t)"), bank[:, :], ACT.Copy))
                B.release(act, "uv")
                C.link(A(sq2[0:MLA_D].rearrange("p a t -> p (a t)"), lqk[0:MLA_D].rearrange("p a t -> p (a t)"), ACT.Square), S["lse_in"])
                root(C, sq2[0:MLA_D].rearrange("p a t -> p (a t)"), 6)
                attention(C, B, "M", ATT2, len(ATT2), lg2, pT2, take_heads(6))
                root(C, sqb[:, 0:512], 7)
                act.wait_ge(S["h_ready"], 1)
                norm_squares(C)
                root(C, dn, 8)
                for i in range(16):
                    bank = B.wait(act, f"U{i}")
                    C.link(A(hidden[:, 2 * i:2 * i + 2, :].rearrange("p a t -> p (a t)"), bank[:, :], ACT.Relu), S["conv_in"])
                    B.release(act, f"U{i}")
                layer_end(act, l + (layers[0] + 1), False)
            act.dma_start(out, h[:]).then_inc(stored, 16)
            act.wait_ge(stored, 16)

        @block.vector
        def _(dve):
            V = nc.vector

            def norm(C, B, name, gain, dst, n, buf, sig="u_ready"):
                bank = B.wait(dve, name)
                C.link(V.tensor_scalar(buf, bank[:, 0:T], 1.0 / D, EPS, ALU.mult, ALU.add))
                B.release(dve, name)
                C.link(V.reciprocal(buf, buf), S["rstd_in"])
                dve.wait_ge(S["rstd_out"], n)
                for k in range(KD):
                    C.link(V.scalar_tensor_tensor(dst[:, k, :], h[:, k, :], gain[:, k:k + 1], buf, ALU.mult, ALU.mult), S[sig])

            def rstd(C, B, names, buf, scale, eps, n, rows=P, floor=None, width=512):
                for g, name in enumerate(names):
                    bank = B.wait(dve, name)
                    o = buf[0:rows, g * width:(g + 1) * width]
                    if floor is None:
                        C.link(V.tensor_scalar(o, bank[0:rows, 0:width], scale, eps, ALU.mult, ALU.add))
                    else:
                        C.link(V.tensor_scalar(o, bank[0:rows, 0:width], floor, None, ALU.max))
                    B.release(dve, name)
                full = buf[0:rows, 0:len(names) * width]
                C.link(V.reciprocal(full, full), S["rstd_in"])
                dve.wait_ge(S["rstd_out"], n)

            def rope(C, B, name, x_, n, cos, sin, t, rows=P):
                bank = B.wait(dve, name)
                C.link(V.tensor_tensor(t, v3(bank[0:rows, 0:n * T], n), spread(sin, n), ALU.mult))
                B.release(dve, name)
                C.link(V.tensor_tensor(x_, x_, spread(cos, n), ALU.mult))
                C.link(V.tensor_tensor(x_, x_, t, ALU.add))

            def attention(C, B, tag, batches, base, scale, mask, lgs):
                for i, (b, tt, heads) in enumerate(batches):
                    w, n = (tt + 1) * P, len(heads)
                    bank = B.wait(dve, f"{tag}L{b}")
                    if i >= 2:
                        B.wait(dve, f"{tag}P{batches[i - 2][0]}")
                    x_ = v3(lgs[i % 2][:, 0:n * w], n)
                    C.link(V.scalar_tensor_tensor(x_, v3(bank[:, 0:n * w], n), scale, spread(mask(tt), n), ALU.mult, ALU.add))
                    B.release(dve, f"{tag}L{b}")
                    C.link(V.tensor_reduce(nmax[:, 0:n], x_, AX_X, ALU.max, negate=True), S["probs_in"])
                    dve.wait_ge(S["logits_ready"], base + i + 1)
                    C.link(V.reciprocal(ssum[:, 0:n], ssum[:, 0:n]))
                    C.link(V.tensor_tensor(x_, x_, along(ssum[:, 0:n], w), ALU.mult), S["probs_ready"])

            dve.wait_ge(inputs_in, 48)
            C = Chain(dve, ready)
            C.link(V.tensor_copy(msk[:], mask_in))
            with dve.Fori(0, layers[0]) as l:
                C, B = Chain(dve, S["dve_chain"]), b1
                dve.wait_ge(params_in, (l + 1) * 16)
                p = lambda n: PAR1.of(par, n)
                C.link(V.tensor_scalar(omu, p("mu"), -1.0, 1.0, ALU.mult, ALU.add))
                C.link(V.memset(pmu[:, :, 0:1], 0.0), S["pmu_used"])
                C.link(V.memset(cc[:, :, 0:1], 0.0))
                norm(C, B, "norm", p("g_mix"), u, 1, tw)
                for i in range(14):
                    dve.wait_ge(S["pmu_ready"], 2 * (i // 2) + 2)
                    bank = B.wait(dve, f"A{i // 2}")
                    C.link(V.scalar_tensor_tensor(pa[:, i, :], bank[:, i % 2 * T:(i % 2 + 1) * T], omu[:, i:i + 1],
                                                  pmu[:, i % 4, 0:T], ALU.mult, ALU.add), S["pmu_used"])
                    if i % 2:
                        B.release(dve, f"A{i // 2}")
                for j in range(4):
                    C.link(V.tensor_scalar(v3(kk, 4)[:, j, :], pa[:, 4 + j, :], p("k_k")[:, j:j + 1], None, ALU.mult))
                dve.sem_inc(S["kk_ready"], 1)
                dve.wait_ge(S["squash_ready"], 4)
                for i in range(8):
                    C.link(V.tensor_tensor_scan(cc[:, i, 1:P + 1], ones, v3(einv, 8)[:, i, :], 0.0, ALU.mult, ALU.add))
                C.link(V.tensor_copy(mid, cc[:, :, 64]))
                C.link(V.tensor_tensor(cc, cc, along(mid, P + 1), ALU.subtract), S["cum_ready"])
                dve.wait_ge(S["squash_ready"], 8)
                for j in range(4):
                    C.link(V.tensor_scalar(v3(kmod, 4)[:, j, :], v3(av, 4)[:, j, :], -1.0, p("k_a")[:, j:j + 1], ALU.add, ALU.mult))
                k_flat = pa[:, 4:8, :].rearrange("p a t -> p (a t)")
                C.link(V.scalar_tensor_tensor(kmod, kmod, 1.0, k_flat, ALU.add, ALU.mult))
                for g in range(2):
                    bank = B.wait(dve, f"Bf{g}")
                    C.link(V.tensor_copy(bf[:, g * 512:(g + 1) * 512], bank[:, :]))
                    B.release(dve, f"Bf{g}")
                for g in range(2):
                    B.wait(dve, f"KK{g}")
                rstd(C, B, ["KK0", "KK1"], bonus, None, None, 2, floor=1e-24)
                C.link(V.tensor_tensor(kk, kk, bonus, ALU.mult))
                for j in range(4):
                    C.link(V.scalar_tensor_tensor(v3(bonus, 4)[:, j, :], pa[:, j, :], p("r_k")[:, j:j + 1],
                                                  v3(kmod, 4)[:, j, :], ALU.mult, ALU.mult))
                dve.sem_inc(S["bonus_in"], 1)
                dve.wait_ge(S["decay_ready"], 1)
                C.link(V.scalar_tensor_tensor(ar[:, :, 0, :], v3(kk, 8), -1.0, ar[:, :, 0, :], ALU.mult, ALU.mult))
                r8 = pa[:, 0:4, :].rearrange("p a (c t) -> p (a c) t", c=2)
                C.link(V.tensor_tensor(ar[:, :, 1, :], r8, ar[:, :, 1, :], ALU.mult))
                C.link(V.tensor_tensor(av, av, kk, ALU.mult))
                C.link(V.tensor_tensor(av, av, einv, ALU.mult))
                C.link(V.tensor_tensor(einv, einv, kmod, ALU.mult), S["rwkv_ops_ready"])
                bank = B.wait(dve, "Cv")
                C.link(V.tensor_copy(cvt.rearrange("p a t -> p (a t)"), bank[:, 0:T]))
                C.link(V.tensor_scalar(wi, bank[:, T:T + 8], 1.0 / 16, None, ALU.mult))
                B.release(dve, "Cv")
                for g in range(2):
                    B.wait(dve, f"BON{g}")
                for g in range(2):
                    bank = B.wait(dve, f"BON{g}")
                    vv = pa[:, 8 + 2 * g:10 + 2 * g, :].rearrange("p a t -> p (a t)")
                    C.link(V.tensor_tensor(bonus[:, g * 512:(g + 1) * 512], bank[:, :], vv, ALU.mult))
                    B.release(dve, f"BON{g}")
                for c in range(2):
                    if c:
                        B.wait(dve, "ST")
                    for hd in range(8):
                        bank = B.wait(dve, f"S{c}{hd}")
                        C.link(V.tensor_tensor(sc[:, hd].rearrange("p a t -> p (a t)"), bank[:, :], K("pairmask"), ALU.mult))
                        B.release(dve, f"S{c}{hd}")
                    for q in range(2):
                        bank = B.wait(dve, f"N{c}{q}")
                        C.link(V.tensor_tensor(nn[:, 4 * q:4 * q + 4, :], v3(bank[:, :], 4), spread(K("lower"), 4), ALU.mult))
                        B.release(dve, f"N{c}{q}")
                    for q in range(2):
                        hs = slice(4 * q, 4 * q + 4)
                        for o, m, s_ in ((xx, upm, sc[:, q:8:2, 0, :]), (zz, lowm, nn[:, hs, :])):
                            C.link(V.tensor_copy(o[:, hs, :], spread(ident, 4)))
                            C.link(V.copy_predicated(o[:, hs, :], spread(m[:, 0, :], 4), s_))
                        dve.sem_inc(S["xz_ready"], 1)
                    for k in range(1, LEVELS):
                        for q in range(2):
                            hs = slice(4 * q, 4 * q + 4)
                            if k < LEVELS - 1:
                                B.wait(dve, f"Z{c}{k}{q}")
                            for n, o, m in (("X", xx, upm), ("Z", zz, lowm)):
                                if n == "Z" and k == LEVELS - 1:
                                    continue
                                bank = B.wait(dve, f"{n}{c}{k}{q}")
                                C.link(V.copy_predicated(o[:, hs, :], spread(m[:, k, :], 4), v3(bank[:, :], 4)))
                                B.release(dve, f"{n}{c}{k}{q}")
                            dve.sem_inc(S["xz_ready"], 1)
                    if c == 0:
                        bank = B.wait(dve, "ST")
                        e8 = eend.rearrange("p (j c) -> p j c", c=2)
                        m8_ = emid.rearrange("p (j c) -> p j c", c=2)
                        C.link(V.memset(st, 0.0))
                        for j in range(4):
                            for r in (0, 64):
                                C.link(V.tensor_scalar(st[r:r + 64, j, r:r + 64], bank[r:r + 64, j * 64:(j + 1) * 64],
                                                       e8[r:r + 64, j, 0:1], m8_[r:r + 64, j, 1:2], ALU.mult, ALU.mult))
                        dve.sem_inc(S["state_ready"], 1)
                        B.release(dve, "ST")
                for g in range(2):
                    B.wait(dve, f"GM{g}")
                for g in range(2):
                    bank = B.wait(dve, f"GM{g}")
                    y_ = ya[:, g * 512:(g + 1) * 512]
                    C.link(V.scalar_tensor_tensor(y_, bank[:, :], -1.0 / 64, y_, ALU.mult, ALU.add))
                    B.release(dve, f"GM{g}")
                dve.sem_inc(S["fresh_norm"], 1)
                for g in range(2):
                    B.wait(dve, f"GV{g}")
                rstd(C, B, ["GV0", "GV1"], kk, 1.0 / 64, GN_EPS, 3)
                C.link(V.tensor_tensor(ya, ya, kk, ALU.mult))
                for j in range(4):
                    C.link(V.tensor_scalar(v3(ya, 4)[:, j, :], v3(ya, 4)[:, j, :], p("gn_g")[:, j:j + 1], p("gn_b")[:, j:j + 1], ALU.mult, ALU.add))
                C.link(V.tensor_tensor(ya, ya, bonus, ALU.add))
                dve.wait_ge(S["gA_ready"], 2)
                C.link(V.tensor_tensor(ya, ya, gA, ALU.mult), S["ya_ready"])
                C.link(V.tensor_tensor(lbc, p("lb0"), p("lb1"), ALU.subtract), S["hcol_in"])
                dve.wait_ge(S["hcol_out"], 1)
                C.link(V.tensor_scalar(lbc, lbc, 1e30, 1.0, ALU.min, ALU.add))
                C.link(V.reciprocal(lbc, lbc))
                C.link(V.tensor_tensor(lbc, lbc, p("not_first"), ALU.mult))
                C.link(V.tensor_scalar(isz, lbc, 0.0, NEG, ALU.is_le, ALU.mult))
                C.link(V.tensor_scalar(omlb, lbc, -1.0, 1.0, ALU.mult, ALU.add))
                C.link(V.tensor_scalar(lnA, lbc, 2.0 ** -64, None, ALU.max))
                C.link(V.tensor_scalar(ln1m, omlb, 2.0 ** -64, None, ALU.max), S["hcol_in"])
                dve.wait_ge(S["hcol_out"], 2)
                C.link(V.tensor_tensor(lnA, lnA, isz, ALU.add))
                C.link(V.tensor_scalar(hls, bf, 0.0, None, ALU.min), S["ls_in"])
                dve.wait_ge(S["ls_out"], 1)
                C.link(V.tensor_tensor(hls, hls, hE, ALU.subtract))
                C.link(V.tensor_tensor(hks, hls, bf, ALU.subtract))
                for j in range(4):
                    s_ = v3(hls, 4)[:, j, :]
                    C.link(V.tensor_scalar(v3(hE, 4)[:, j, :], s_, ln1m[:, j:j + 1], lnA[:, j:j + 1], ALU.add, ALU.subtract))
                    C.link(V.tensor_scalar(s_, s_, ln1m[:, j:j + 1], lnA[:, j:j + 1], ALU.add, ALU.max))
                dve.sem_inc(S["lse_in"], 1)
                dve.wait_ge(S["lse_out"], 1)
                C.link(V.tensor_tensor(hls, hls, hE, ALU.add))
                for j in range(4):
                    C.link(V.tensor_scalar(v3(hks, 4)[:, j, :], v3(hks, 4)[:, j, :], omlb[:, j:j + 1], None, ALU.mult))
                for i in range(8):
                    C.link(V.tensor_tensor_scan(v3(hb, 8)[:, i, :], ones, v3(hls, 8)[:, i, :], 0.0, ALU.mult, ALU.add))
                dve.sem_inc(S["cum_b"], 1)
                dve.wait_ge(S["d_exp"], 1)
                C.link(V.tensor_tensor(v3(hke, 8)[:, 0:4, :], v3(hke, 8)[:, 0:4, :], v3(hks, 8)[:, 0:8:2, :], ALU.mult), S["hk_ready"])
                C.link(V.tensor_tensor(v3(hqe, 8)[:, 0:4, :], v3(hqe, 8)[:, 0:4, :], v3(bq, 8)[:, 1:8:2, :], ALU.mult), S["hqe_ready"])
                C.link(V.memset(hsc, 0.0))

                def halves(ap, m):
                    return ap.rearrange("p (n a t) -> p n a t", a=2, t=m)

                def take_pairs(k):
                    for c in range(2):
                        bank = B.wait(dve, f"H{k}{c}")
                        m = upm[:, k, :] if k < LEVELS else diagm
                        C.link(V.copy_predicated(v3(hsc, 8)[:, c:8:2, :], spread(m, 4), v3(bank[:, :], 4)))
                        B.release(dve, f"H{k}{c}")

                for k in range(LEVELS):
                    m = 1 << k
                    b_, e_, o_ = halves(hb, m), halves(hE, m), halves(hqk, m)
                    n = 1024 // (2 * m)
                    ref = b_[:, :, 0, m - 1:m].to_broadcast([P, n, m])
                    C.link(V.tensor_tensor(e_[:, :, 0, :], ref, b_[:, :, 0, :], ALU.subtract))
                    C.link(V.tensor_tensor(e_[:, :, 1, :], b_[:, :, 1, :], ref, ALU.subtract), S["pairs_in"])
                    if k:
                        take_pairs(k - 1)
                    dve.wait_ge(S["d_exp"], k + 2)
                    C.link(V.tensor_tensor(o_[:, :, 0, :], halves(hks, m)[:, :, 0, :], e_[:, :, 0, :], ALU.mult))
                    C.link(V.tensor_tensor(o_[:, :, 1, :], halves(bq, m)[:, :, 1, :], e_[:, :, 1, :], ALU.mult), S["pairs_ready"])
                dve.sem_inc(S["pairs_ready"], 1)
                take_pairs(LEVELS - 1)
                take_pairs(LEVELS)
                dve.sem_inc(S["hsc_ready"], 1)
                for g in range(2):
                    B.wait(dve, f"HN{g}")
                rstd(C, B, ["HN0", "HN1"], hE, 1.0 / 128, EPS, 4)
                C.link(V.tensor_tensor(yb, yb, hE, ALU.mult))
                dve.wait_ge(S["bsg_ready"], 2)
                for j in range(4):
                    C.link(V.scalar_tensor_tensor(v3(yb, 4)[:, j, :], v3(yb, 4)[:, j, :], p("b_gn")[:, j:j + 1], v3(bsg, 4)[:, j, :], ALU.mult, ALU.mult))
                dve.sem_inc(S["yb_ready"], 1)
                cos, sin = K("cos"), K("sin")
                rope(C, B, "Rq0", craw[:, 0:2, :], 2, cos, sin, scr)
                rope(C, B, "Rq1", craw[:, 2:4, :], 2, cos, sin, scr)
                bank = B.wait(dve, "Rkr")
                C.link(V.tensor_tensor(scr, v3(bank[:, :], 2), spread(sin, 2), ALU.mult))
                B.release(dve, "Rkr")
                bank = B.wait(dve, "Rkd")
                C.link(V.tensor_tensor(craw[:, 7:9, :], v3(bank[:, :], 2), spread(cos, 2), ALU.mult))
                B.release(dve, "Rkd")
                C.link(V.tensor_tensor(craw[:, 7:9, :], craw[:, 7:9, :], scr, ALU.add))
                rope(C, B, "Rqi", craw[:, 4:6, :], 2, cos, sin, scr)
                rope(C, B, "Rki", craw[:, 6:7, :], 1, cos, sin, scr[:, 0:1, :])
                dve.sem_inc(S["rope_ready"], 1)
                for tt in range(NT):
                    w = (tt + 1) * P
                    for n, _, heads in INDEX[2 * tt:2 * tt + 2]:
                        bank = B.wait(dve, n)
                        for i, hd in enumerate(heads):
                            o = scr[:, tt, 0:w] if hd == 0 else tmp[:, 0:w]
                            C.link(V.tensor_scalar(o, bank[:, i * w:(i + 1) * w], 0.0, wi[:, 4 * tt + hd:4 * tt + hd + 1], ALU.max, ALU.mult))
                            if hd:
                                C.link(V.tensor_tensor(scr[:, tt, 0:w], scr[:, tt, 0:w], o, ALU.add))
                        B.release(dve, n)
                    neg = K("cneg")[:, T - w:T]
                    C.link(V.tensor_tensor(scr[:, tt, 0:w], scr[:, tt, 0:w], neg, ALU.add))
                    C.link(V.tensor_copy(work[:, tt, 0:w], scr[:, tt, 0:w]))
                    for _ in range(TOPK // TOP_STEP):
                        C.link(V.max(m8, work[:, tt, 0:w]))
                        C.link(V.match_replace(work[:, tt, 0:w], m8, work[:, tt, 0:w], TAKEN))
                    C.link(V.tensor_scalar(amask[:, tt, 0:w], work[:, tt, 0:w], 2 * NEG, None, ALU.is_le))
                    C.link(V.tensor_scalar(amask[:, tt, 0:w], amask[:, tt, 0:w], -1.0, -NEG, ALU.add, ALU.mult))
                    C.link(V.tensor_tensor(amask[:, tt, 0:w], amask[:, tt, 0:w], neg, ALU.min))
                attention(C, B, "C", ATT1, 0, 0.125, lambda tt: amask[:, tt, 0:(tt + 1) * P], lg)
                dve.wait_ge(S["yc_ready"], 2)
                dve.sem_inc(S["h_ready"], 1)
                for i in range(12):
                    j, n = i // 3, i % 3
                    bank = B.wait(dve, f"M{j}{n}")
                    dve.wait_ge(S["gate_ready"], i + 1)
                    o = merged[:, j * 512:(j + 1) * 512]
                    C.link(V.tensor_tensor(mtmp if n else o, bank[:, :], gate_buf[i % 2], ALU.mult), S["gate_used"])
                    B.release(dve, f"M{j}{n}")
                    if n:
                        C.link(V.tensor_tensor(o, o, mtmp, ALU.add), S["merged_ready"] if n == 2 else None)
                for j in range(4):
                    bank = B.wait(dve, f"WO{j}")
                    o = h[:, 2 * j:2 * j + 2, :].rearrange("p a t -> p (a t)")
                    C.link(V.tensor_tensor(o, o, bank[:, :], ALU.add))
                    B.release(dve, f"WO{j}")
                dve.sem_inc(S["h_ready"], 1)
                norm(C, B, "norm2", p("g_ffn"), u, 5, tmp[:, 0:T])
                for i in range(23):
                    if i < 22:
                        bank = B.wait(dve, f"U{i}")
                        dve.wait_ge(S["conv_in"], i + 1)
                        for j, t in ((0, i), (1, 22 + i)):
                            c_ = cb[i % 4][:, j, :]
                            x_ = bank[:, j * T:(j + 1) * T]
                            C.link(V.scalar_tensor_tensor(c_[:, 1:], x_[:, 0:T - 1], p("conv_w1")[:, t:t + 1], c_[:, 1:], ALU.mult, ALU.add))
                            C.link(V.scalar_tensor_tensor(c_[:, 2:], x_[:, 0:T - 2], p("conv_w0")[:, t:t + 1], c_[:, 2:], ALU.mult, ALU.add),
                                   S["conv_mid"] if j else None)
                        B.release(dve, f"U{i}")
                    if i:
                        dve.wait_ge(S["conv_out"], i)
                        c_ = cb[(i - 1) % 4]
                        C.link(V.tensor_tensor(hidden[:, i - 1, :], c_[:, 0, :], c_[:, 1, :], ALU.mult), S["hidden_ready"])
                for j in range(4):
                    bank = B.wait(dve, f"D{j}")
                    o = h[:, 2 * j:2 * j + 2, :].rearrange("p a t -> p (a t)")
                    C.link(V.tensor_tensor(o, o, bank[:, :], ALU.add))
                    B.release(dve, f"D{j}")
                layer_end(dve, l, True)

            C, B = Chain(dve, S["dve_chain"]), b2
            norm(C, B, "norm", PAR1.of(par, "g_final"), h, 1, tmp[:, 0:T])
            dve.wait_ge(inputs_in, 64)
            C.link(V.tensor_copy(t512[0:1, 0:T], t512.bitcast(I32)[0:1, T:2 * T]), S["ready"])
            dve.wait_ge(bank_full[1], 1)
            two_pi = 2.0 * np.pi
            hi = float(np.float32(6.28125))
            lo = float(np.float32(two_pi - 6.28125))
            rest = float(two_pi - 6.28125 - np.float64(np.float32(two_pi - 6.28125)))
            for i in range(4):
                ang, tn = tabs[i], em
                C.link(V.tensor_scalar(ang, banks[1][:, 0:T], K("freq")[:, i // 2:i // 2 + 1], None, ALU.mult))
                shift = 0.25 if i % 2 == 0 else 0.0
                C.link(V.tensor_scalar(tn, ang, 1.0 / two_pi, shift, ALU.mult, ALU.add))
                C.link(V.tensor_scalar(tn, tn, 12582912.0, None, ALU.add))
                C.link(V.tensor_scalar(tn, tn, -12582912.0, None, ALU.add))
                for part_ in (hi, lo, rest):
                    C.link(V.scalar_tensor_tensor(ang, tn, -part_, ang, ALU.mult, ALU.add))
                if i % 2 == 0:
                    C.link(V.tensor_scalar(ang, ang, np.pi / 2, None, ALU.add))
                C.link(V.tensor_scalar(ang, ang, 3.1415925, -3.1415925, ALU.min, ALU.max), S["cum_ready"])
            dve.wait_ge(S["decay_ready"], 4)
            layer_end(dve, layers[0], True)

            if not layers[1]:
                return
            with dve.Fori(0, layers[1]) as l:
                C, B = Chain(dve, S["dve_chain"]), b2
                dve.wait_ge(params_in, (l + (layers[0] + 1)) * 16)
                p = lambda n: PAR2.of(par, n)
                norm(C, B, "norm", p("g_mix"), u, 1, dn)
                cw = v3(p("conv_w"), 4)
                for i in range(4):
                    bank = B.wait(dve, f"qk{i // 2}")
                    dve.wait_ge(S["conv_in"], 2 * (i // 2) + 2)
                    x_ = bank[:, i % 2 * T:(i % 2 + 1) * T]
                    for d in (1, 2, 3):
                        o = qkraw[:, i, d:]
                        C.link(V.scalar_tensor_tensor(o, x_[:, 0:T - d], cw[:, 3 - d, i:i + 1], o, ALU.mult, ALU.add),
                               S["conv_mid"] if d == 3 else None)
                    if i % 2:
                        B.release(dve, f"qk{i // 2}")
                bank = B.wait(dve, "if")
                a_, f_, g_, e_, z_, w_ = (ifr[0:4, i * T:(i + 1) * T] for i in range(6))
                C.link(V.tensor_scalar(a_, bank[0:4, 0:T], p("b_i")[0:4], None, ALU.add))
                C.link(V.tensor_scalar(f_, bank[0:4, T:2 * T], p("b_f")[0:4], None, ALU.add))
                B.release(dve, "if")
                C.link(V.tensor_copy(z_, f_), S["ls_in"])
                C.link(V.tensor_scalar(f_, f_, 0.0, None, ALU.min))
                dve.wait_ge(S["hcol_out"], 1)
                C.link(V.tensor_tensor(f_, z_, f_, ALU.subtract))
                C.link(V.memset(w_, 1.0))
                C.link(V.tensor_tensor_scan(z_, w_, f_, 0.0, ALU.mult, ALU.add))
                C.link(V.tensor_tensor(a_, a_, z_, ALU.add))
                C.link(V.tensor_tensor_scan(g_, a_, a_, 0.0, ALU.max, ALU.max))
                C.link(V.tensor_tensor(e_, z_, g_, ALU.subtract), S["d_diff"])
                bank = B.wait(dve, "acol")
                C.link(V.tensor_copy(acol.rearrange("p a t -> p (a t)"), bank[:, 0:8]))
                B.release(dve, "acol")
                for hd in range(4):
                    bank = B.wait(dve, f"gb{hd}")
                    dve.wait_ge(S["em_ready"], hd + 1)
                    C.link(V.tensor_scalar(dT[:, 0:T], bank[:, 0:T], acol[:, 0, hd:hd + 1], 0.0, ALU.subtract, ALU.max))
                    C.link(V.tensor_scalar(dT[:, T:T + P], bank[:, P:T], acol[:, 1, hd:hd + 1], 0.0, ALU.subtract, ALU.max), S["pairs_in"])
                    dve.wait_ge(S["d_exp"], hd + 1)
                    B.release(dve, f"gb{hd}")
                    for o in (0, T):
                        C.link(V.tensor_tensor(dT[:, o:o + P], dT[:, o:o + P], K("pairmask")[:, P:2 * P], ALU.mult))
                    bank = B.wait(dve, f"sc{hd}")
                    if hd >= 2:
                        B.wait(dve, f"nd{hd - 2}")
                    C.link(V.scalar_tensor_tensor(sT[hd % 2], bank[:, 0:T + P], 0.125, dT, ALU.mult, ALU.mult), S["s_ready"])
                    B.release(dve, f"sc{hd}")
                    bank = B.wait(dve, f"nd{hd}")
                    C.link(V.tensor_tensor(dn, bank[:, T:2 * T], em, ALU.max))
                    C.link(V.scalar_tensor_tensor(dn, bank[:, T:2 * T], -1.0, dn, ALU.mult, ALU.max))
                    C.link(V.reciprocal(dn, dn))
                    C.link(V.tensor_tensor(mix[:, hd, :], bank[:, 0:T], dn, ALU.mult), S["dn_ready"])
                    B.release(dve, f"nd{hd}")
                for g in range(2):
                    B.wait(dve, f"mn{g}")
                rstd(C, B, ["mn0", "mn1"], sqb, 1.0 / 128, EPS, 2)
                flat = mix[:, 0:4, :].rearrange("p a t -> p (a t)")
                C.link(V.tensor_tensor(flat, flat, sqb, ALU.mult))
                dve.wait_ge(S["bsg_ready"], 2)
                for hd in range(4):
                    C.link(V.scalar_tensor_tensor(mix[:, hd, :], mix[:, hd, :], p("g_mlstm")[:, hd:hd + 1], mo[:, hd, :], ALU.mult, ALU.mult))
                dve.sem_inc(S["yb_ready"], 1)
                dve.wait_ge(S["raw_ready"], 3)
                for n in ("nq", "nk"):
                    B.wait(dve, n)
                rstd(C, B, ["nq", "nk"], sqb, 1.0 / 64, EPS, 3)
                for i, n in ((0, "g_mq"), (2, "g_mk")):
                    x_ = aqk[:, i:i + 2, :].rearrange("p a t -> p (a t)")
                    C.link(V.scalar_tensor_tensor(x_, x_, p(n), sqb[:, i * T:(i + 2) * T], ALU.mult, ALU.mult))
                dve.sem_inc(S["kk_ready"], 1)
                t2 = v3(t512, 2)
                for n in ("rq", "rk"):
                    B.wait(dve, n)
                rope(C, B, "rq", aqk[:, 0:2, :], 2, tabs[0], tabs[1], t2)
                rope(C, B, "rk", aqk[:, 2:4, :], 2, tabs[0], tabs[1], t2)
                dve.sem_inc(S["rope_ready"], 1)
                causal = lambda tt: K("cneg")[:, T - (tt + 1) * P:T]
                attention(C, B, "B", ATT2, 0, 0.125, causal, lg2)

                def head_norm(name, o, gain, n):
                    B.wait(dve, name)
                    rstd(C, B, [name], sqb, 1.0 / 64, EPS, n)
                    for i in range(2):
                        C.link(V.scalar_tensor_tensor(mix[:, o + i, :], mix[:, o + i, :], p(gain)[:, i:i + 1], v3(sqb, 4)[:, i, :], ALU.mult, ALU.mult))

                head_norm("bn", 4, "g_mobaout", 4)
                for g, (n, width) in enumerate((("ncq", 384), ("nckv", 256))):
                    bank = B.wait(dve, n)
                    C.link(V.tensor_scalar(t512[:, g * T:(g + 1) * T], bank[:, 0:T], 1.0 / width, EPS, ALU.mult, ALU.add))
                    B.release(dve, n)
                C.link(V.reciprocal(t512, t512), S["rstd_in"])
                dve.wait_ge(S["rstd_out"], 5)
                for i in range(5):
                    g_ = p("g_cq")[:, i:i + 1] if i < 3 else p("g_ckv")[:, i - 3:i - 2]
                    C.link(V.scalar_tensor_tensor(cqk[:, i, :], cqk[:, i, :], g_, t512[:, (i // 3) * T:(i // 3 + 1) * T], ALU.mult, ALU.mult))
                dve.sem_inc(S["latents_ready"], 1)
                for n in ("nlq0", "nlq1", "nlk0", "nlk1"):
                    B.wait(dve, n)
                s2f = sq2.rearrange("p a t -> p (a t)")
                rstd(C, B, ["nlq0", "nlq1", "nlk0", "nlk1"], s2f, 1.0 / MLA_D, EPS, 6, MLA_D)
                for i, n in ((0, "g_lq"), (4, "g_lk")):
                    x_ = lqk[0:MLA_D, i:i + 4, :].rearrange("p a t -> p (a t)")
                    C.link(V.scalar_tensor_tensor(x_, x_, p(n)[0:MLA_D], s2f[0:MLA_D, i * T:(i + 4) * T], ALU.mult, ALU.mult))
                dve.sem_inc(S["lse_out"], 1)
                for n in ("rlq0", "rlq1", "rlk0", "rlk1"):
                    B.wait(dve, n)
                for g, n in enumerate(("rlq0", "rlq1", "rlk0", "rlk1")):
                    rope(C, B, n, lqk[0:MLA_D, 2 * g:2 * g + 2, :], 2, tabs[2][0:MLA_D], tabs[3][0:MLA_D], t2[0:MLA_D], MLA_D)
                dve.sem_inc(S["rope_ready"], 1)
                attention(C, B, "M", ATT2, len(ATT2), float(MLA_D) ** -0.5, causal, lg2)
                head_norm("ln", 6, "g_mlaout", 7)
                dve.sem_inc(S["yc_ready"], 1)
                for j in range(4):
                    bank = B.wait(dve, f"WO{j}")
                    o = h[:, 2 * j:2 * j + 2, :].rearrange("p a t -> p (a t)")
                    C.link(V.tensor_tensor(o, o, bank[:, :], ALU.add))
                    B.release(dve, f"WO{j}")
                dve.sem_inc(S["h_ready"], 1)
                norm(C, B, "norm2", p("g_mlp"), u, 8, dn)
                for i in range(16):
                    dve.wait_ge(S["conv_in"], 4 + i + 1)
                    x_ = hidden[:, 2 * i:2 * i + 2, :].rearrange("p a t -> p (a t)")
                    C.link(V.tensor_tensor(x_, x_, x_, ALU.mult), S["hidden_ready"])
                for j in range(4):
                    bank = B.wait(dve, f"D{j}")
                    o = h[:, 2 * j:2 * j + 2, :].rearrange("p a t -> p (a t)")
                    C.link(V.tensor_tensor(o, o, bank[:, :], ALU.add))
                    B.release(dve, f"D{j}")
                layer_end(dve, l + (layers[0] + 1), True)


def lay_out(i):
    f = np.float32
    p1 = []
    for l in range(LAYERS):
        v = {"g_mix": cols(i["norm_mix_g"][l]), "mu": cols(i["a_mu"][l]), "w0": cols(i["a_w0"][l]), "a0": cols(i["a_a0"][l]),
             "k_k": cols(i["a_k_k"][l]), "k_a": cols(i["a_k_a"][l]), "r_k": cols(i["a_r_k"][l].reshape(-1)),
             "gn_g": cols(i["a_gn_g"][l]), "gn_b": cols(i["a_gn_b"][l]), "lb0": cols(i["b_lb_logits"][0]),
             "lb1": cols(i["b_lb_logits"][1]), "not_first": np.full((P, 4), float(l > 0), f), "b_gn": cols(i["b_gn_g"][l]),
             "g_ffn": cols(i["norm_ffn_g"][l]), "conv_b": cols(i["conv_b"][l]), "conv_w0": cols(i["conv_w"][l][0]),
             "conv_w1": cols(i["conv_w"][l][1]), "conv_w2": cols(i["conv_w"][l][2]), "g_final": cols(i["norm_final_g"]),
             "wa_up": np.concatenate([i["a_w_up"][l], i["a_a_up"][l]], 0), "g_up": i["a_g_up"][l]}
        assert list(v) == list(PAR1.at)
        p1.append(np.concatenate(list(v.values()), 1))
    p2 = []
    for l in range(LAYERS):
        w = {n[:-2]: a[l] for n, a in i.items() if n.endswith("_2") and n != "positions_2"}
        v = {"g_mix": cols(w["g_mix_norm"]), "conv_w": np.concatenate([cols(w["conv_w"][j]) for j in range(4)], 1),
             "conv_b": cols(w["conv_b"]), "b_i": col(w["b_igate"]), "b_f": col(w["b_fgate"]),
             "g_mlstm": cols(w["g_mlstm_out"].reshape(-1)), "g_mq": col(np.tile(w["g_moba_q"], 2)),
             "g_mk": col(np.tile(w["g_moba_k"], 2)), "g_mobaout": cols(w["g_moba_out"].reshape(-1)), "g_cq": cols(w["g_cq"]),
             "g_ckv": cols(w["g_ckv"]), "g_lq": col(w["g_mla_q"]), "g_lk": col(w["g_mla_k"]),
             "g_mlaout": cols(w["g_mla_out"].reshape(-1)), "g_mlp": cols(w["g_mlp_norm"])}
        assert list(v) == list(PAR2.at)
        p2.append(np.concatenate(list(v.values()), 1))
    s = [chunks(stream1(i["w_in"][l], i["w_branch"][l], i["w_o"][l], i["w_up"][l], i["w_down"][l])) for l in range(LAYERS)]
    s += [chunks(stream2(*(i[n + "_2"][l] for n in ("w_in", "w_uq", "w_ukv", "w_out", "w_up", "w_down")))) for l in range(LAYERS)]
    c, m = constants()
    return {"x": np.ascontiguousarray(i["x"][0].T.reshape(KD, P, T).transpose(1, 0, 2)), "params1": np.stack(p1), "params2": np.stack(p2),
            "stream": np.concatenate(s), "cst": c, "masks": m, "positions": np.ascontiguousarray(i["positions_2"])}


def kernel(**inputs):
    import concourse.bacc as bacc
    from concourse.bass_utils import run_bass_kernel_spmd

    arrays = lay_out({n: np.asarray(a) for n, a in inputs.items()})
    nc = bacc.Bacc("TRN2", target_bir_lowering=False, num_devices=1)
    args = [nc.dram_tensor(f"in_{n}", a.shape, mybir.dt.from_np(a.dtype), kind="ExternalInput").ap() for n, a in arrays.items()]
    out = nc.dram_tensor("out", (P, KD, T), F32, kind="ExternalOutput").ap()
    build(nc, *args, out)
    r = run_bass_kernel_spmd(nc, [{f"in_{n}": a for n, a in arrays.items()}], core_ids=[0])
    got = r.results[0]["out"]
    return np.ascontiguousarray(got.transpose(1, 0, 2).reshape(D, T).T)[None]
```

```python
from contextlib import ExitStack

import numpy as np

import concourse.bass as bass
from concourse import mybir
from concourse.alu_op_type import AluOpType as ALU

F32 = mybir.dt.float32
I32 = mybir.dt.int32
F32R = mybir.dt.float32r
U8 = mybir.dt.uint8
ACT = mybir.ActivationFunctionType
AX_X = mybir.AxisListType.X

P = 128
T = 256
NT = T // P
D = 1024
KD = D // P
LAYERS = 2
EPS = 1e-6

A_W, A_COLS = 512, 1792
GN_EPS = 64e-5
KAPPA = float(np.exp(-0.5))
C_OFF, G_OFF = 3840, 4932
FF1 = 2816
TOPK, TOP_STEP = 64, 8
BRANCHES = (1, 2, 0)
NEG, TAKEN = -1e30, -3e38
FF2 = 4096
MLA_D = 96

CHUNK = 4
RING = 8
PIECE = 4
HI_RING = 4
LEAD = HI_RING - 1
BLOCKS1, BLOCKS2 = 1216, 800
CH1, CH2 = BLOCKS1 // CHUNK, BLOCKS2 // CHUNK
PIECES1, PIECES2 = BLOCKS1 // PIECE, BLOCKS2 // PIECE
assert CH1 % RING == 0 and CH2 % RING == 0 and CHUNK % PIECE == 0
assert PIECES1 % HI_RING == 0 and PIECES2 % HI_RING == 0
LEVELS = 7
LN_EXP = "natural_log_exp_and_others"


class Columns:

    def __init__(self, *runs):
        self.at, self.size = {}, 0
        for name, n in runs:
            self.at[name] = (self.size, n)
            self.size += n

    def of(self, table, name):
        a, n = self.at[name]
        return table[:, a:a + n]


PAR1 = Columns(("g_mix", 8), ("mu", 14), ("w0", 4), ("a0", 4), ("k_k", 4), ("k_a", 4), ("r_k", 4), ("gn_g", 4),
               ("gn_b", 4), ("lb0", 4), ("lb1", 4), ("not_first", 4), ("b_gn", 4), ("g_ffn", 8), ("conv_b", 44),
               ("conv_w0", 44), ("conv_w1", 44), ("conv_w2", 44), ("g_final", 8), ("wa_up", A_W), ("g_up", A_W))
PAR2 = Columns(("g_mix", 8), ("conv_w", 16), ("conv_b", 4), ("b_i", 1), ("b_f", 1), ("g_mlstm", 4), ("g_mq", 1),
               ("g_mk", 1), ("g_mobaout", 2), ("g_cq", 3), ("g_ckv", 2), ("g_lq", 1), ("g_lk", 1), ("g_mlaout", 2),
               ("g_mlp", 8))
CST = Columns(("ident", P), ("ones", P), ("bones", P), ("pairmask", 2 * P), ("lower", P), ("cneg", T),
              ("rot", P), ("rotp", P), ("rotd", P), ("cos", T), ("sin", T), ("freq", 2),
              ("eps", 1), ("gn_eps", 1))
MASKS = Columns(("up", LEVELS * P), ("low", LEVELS * P), ("diag", P))


def blocks(w):
    k, n = w.shape
    w = np.pad(w, ((0, 0), (0, -n % P)))
    return w.reshape(k // P, P, -1, P).transpose(2, 0, 1, 3).reshape(-1, P, P)


def row_blocks(w):
    k, n = w.shape
    w = np.pad(w, ((0, 0), (0, -n % P)))
    return w.reshape(k // P, P, -1, P).transpose(0, 2, 1, 3).reshape(-1, P, P)


def filled(b, n):
    return np.concatenate([b, np.zeros((n - len(b), P, P), b.dtype)])


def stream1(w_in, w_branch, w_o, w_up, w_down):
    b, c = A_COLS, C_OFF
    ki = w_in[:, c + 1024:c + 1088]
    out = [blocks(w_in[:, :b]), blocks(w_in[:, b + 1536:b + 2048]), blocks(w_in[:, b:b + 1024]),
           blocks(w_in[:, c:c + 512]), blocks(np.concatenate([w_in[:, c + 512 + 64 * (i // 2):c + 576 + 64 * (i // 2)] for i in range(4)], 1)),
           row_blocks(w_in[:, b + 1024:b + 1536]), blocks(w_in[:, c + 768:c + 1024]), blocks(np.concatenate([ki, ki], 1)),
           row_blocks(np.concatenate([w_in[:, c + 640:c + 768], w_in[:, c + 1088:c + 1092]], 1))]
    for n in BRANCHES:
        for j in range(0, D, 2 * P):
            g = G_OFF + n * D + j
            out += [blocks(w_in[:, g:g + 2 * P]), blocks(w_branch[n][:, j:j + 2 * P])]
    out.append(blocks(w_o))
    for i in range(0, FF1, P):
        out += [blocks(w_up[:, i:i + P]), blocks(w_up[:, FF1 + i:FF1 + i + P])]
    out.append(blocks(w_down))
    return filled(np.concatenate(out), BLOCKS1)


def stream2(w_in, w_uq, w_ukv, w_out, w_up, w_down):
    i, f = w_in[:, 1536:1540], w_in[:, 1540:1544]
    gap = np.zeros((D, 28), w_in.dtype)
    uq = np.pad(w_uq.reshape(384, 4, MLA_D), ((0, 0), (0, 0), (0, P - MLA_D))).reshape(384, 4 * P)
    kv = w_ukv.reshape(256, 4, 2, 64)
    out = [blocks(w_in[:, :512]), row_blocks(w_in[:, 512:1024]), blocks(w_in[:, 1024:1536]),
           blocks(np.concatenate([i, gap, f], 1)), blocks(w_in[:, 1544:2056]), row_blocks(w_in[:, 2056:2312]),
           blocks(w_in[:, 2312:2952]), blocks(np.pad(w_in[:, 2952:2984], ((0, 0), (64, 32)))), blocks(uq),
           blocks(kv[:, :, 0].reshape(256, 256)), row_blocks(kv[:, :, 1].reshape(256, 256)),
           blocks(w_out), blocks(w_up), blocks(w_down)]
    return filled(np.concatenate(out), BLOCKS2)


def chunks(b):
    return b.reshape(-1, CHUNK, P, P).transpose(0, 2, 1, 3).reshape(-1, P, CHUNK * P)


def cols(v):
    return np.ascontiguousarray(v.reshape(-1, P).T)


def col(v, rows=P):
    return np.pad(v.reshape(-1, 1), ((0, rows - v.size), (0, 0)))


def constants():
    s, t = np.arange(P)[:, None], np.arange(P)[None, :]
    f = np.float32
    incl, strict = (s <= t).astype(f), (s < t).astype(f)

    def rotate(n, half, start, size):
        m = np.zeros((P, P), f)
        for base in range(0, n, size):
            for i in range(half):
                a, b = base + start + i, base + start + half + i
                m[b, a], m[a, b] = -1, 1
        return m

    rot = rotate(P, 32, 0, 64)
    inv = (np.float32(10000.0) ** (-np.arange(32, dtype=f) * f(2.0 / 64))).astype(f)
    ang = (np.arange(T, dtype=f)[None, :] * np.tile(inv, 4)[:, None]).astype(f)
    freq = np.zeros((P, 2), f)
    fp = np.power(f(500000.0), -np.arange(0, 16, 2, dtype=f) / f(16)).astype(f)
    fd = np.power(f(10000.0), -np.arange(0, 32, 2, dtype=f) / f(32)).astype(f)
    for base in (0, 64):
        freq[base:base + 16, 0] = np.tile(fp, 2)
    freq[64:96, 1] = np.tile(fd, 2)
    parts = {"ident": np.eye(P, dtype=f), "ones": np.ones((P, P), f), "bones": ((s // 64) == (t // 64)).astype(f),
             "pairmask": np.concatenate([strict, incl], 1), "lower": (s > t).astype(f),
             "cneg": np.concatenate([np.zeros((P, P), f), np.where(t <= s, f(0), f(NEG))], 1),
             "rot": rot, "rotp": rotate(P, 8, 0, 64), "rotd": rotate(MLA_D, 16, 64, MLA_D),
             "cos": np.cos(ang).astype(f), "sin": np.sin(ang).astype(f), "freq": freq,
             "eps": np.full((P, 1), EPS, f), "gn_eps": np.full((P, 1), GN_EPS, f)}
    assert list(parts) == list(CST.at)
    up = []
    for k in range(LEVELS):
        m = 1 << k
        up.append(((s // (2 * m)) == (t // (2 * m))) & (s // m % 2 == 0) & (t // m % 2 == 1))
    masks = np.concatenate(up + [x.T for x in up] + [s == t], 1).astype(f)
    return np.concatenate([parts[n] for n in parts], 1).astype(f), masks


class Chain:

    def __init__(self, eng, sem):
        self.eng, self.sem, self.count = eng, sem, {}

    def link(self, ins, sem=None):
        sem = self.sem if sem is None else sem
        self.count[sem.num] = self.count.get(sem.num, 0) + 1
        ins.then_inc(sem, 1)
        self.eng.wait_ge(sem, self.count[sem.num])


class Banks:

    def __init__(self, names, tiles, full, free):
        self.slot = {n: (i % 8, i // 8) for i, n in enumerate(names)}
        assert len(self.slot) == len(names)
        self.tiles, self.full, self.free = tiles, full, free

    def open(self, pe, name):
        b, use = self.slot[name]
        if use:
            pe.wait_ge(self.free[b], use)
        return self.tiles[b]

    def full_of(self, name):
        return self.full[self.slot[name][0]]

    def wait(self, eng, name):
        b, use = self.slot[name]
        eng.wait_ge(self.full[b], use + 1)
        return self.tiles[b]

    def release(self, eng, name):
        eng.sem_inc(self.free[self.slot[name][0]], 1)


class Weights:

    def __init__(self, pe, lo_ring, hi_ring, split, used, first, ends):
        self.pe, self.lo_ring, self.hi_ring, self.split, self.used, self.first = pe, lo_ring, hi_ring, split, used, first
        self.ends, self.seen, self.next, self.pending, self.told = ends, 0, 0, 0, 0

    def take(self, name, n):
        q = self.next
        self.next += n
        self.ends[name] = -(-self.next // PIECE)
        return q

    def block(self, q, n=1):
        p, at = q // PIECE, q % PIECE * P
        assert q % PIECE + n <= PIECE
        if p >= self.seen:
            self.pe.wait_ge(self.split, self.first + (p + 1))
            self.seen = p + 1
        c, o = q // CHUNK % RING, q % CHUNK * P
        return (self.hi_ring[:, p % HI_RING, at:at + n * P], self.lo_ring[:, c, o:o + n * P])

    def skip(self, n):
        self.take("end", n - self.next)
        self.block(n - PIECE)
        self.pe.sem_inc(self.used, self.pending + n // PIECE - self.told)

    def done(self, q):
        if q % PIECE == PIECE - 1:
            self.pending += 1
            self.told += 1


ATT1 = [("0a", 0, [0, 2, 4, 6]), ("0b", 0, [1, 3, 5, 7]), ("1a", 1, [0, 2]), ("1b", 1, [4, 6]), ("1c", 1, [1, 3]), ("1d", 1, [5, 7])]
ATT2 = [("0a", 0, [0, 2]), ("0b", 0, [1, 3]), ("1a", 1, [0, 2]), ("1b", 1, [1, 3])]
INDEX = [("I0a", 0, [0, 2]), ("I0b", 0, [1, 3]), ("I1a", 1, [0, 2]), ("I1b", 1, [1, 3])]
HALVES = [[0, 2, 4, 6], [1, 3, 5, 7]]


def att_groups(tag, batches):
    out = []
    for b, tt, heads in batches:
        out += [f"{tag}L{b}", f"{tag}P{b}"]
        if b == [x[0] for x in batches if x[1] == tt][0]:
            out.append(f"{tag}O{tt}")
    return out


def groups1():
    g = ["norm"] + [f"A{i}" for i in range(7)] + ["Bg0", "Wup0", "Wup1", "Aup0", "Aup1", "Gup0", "Gup1", "Bg1"]
    g += ["KK0", "KK1", "Bq0", "Bq1", "Bf0", "Bf1", "Cq0", "Cq1", "BON0", "BON1", "Ck"]
    for c in range(2):
        g += [f"Tb{c}", f"Tk{c}", f"Tv{c}"]
    rope = ["Rq0", "Rq1", "Rk", "Rqi", "Rki"]
    beside = {1: ["Cqi"], 2: ["Cki"], 3: ["Cv"], 4: rope, 5: [n for n, _, _ in INDEX], 6: ["HT"]}
    for c in range(2):
        g += [f"S{c}{h}" for h in range(8)] + [f"N{c}0", f"N{c}1"] + (["Bi0", "Bi1"] if c == 0 else [])
        for k in range(1, LEVELS):
            g += [f"O{c}{k}0", f"O{c}{k}1"]
            if c:
                g += [f"CL{ATT1[k - 1][0]}"] + [f"CO{ATT1[k - 3][0]}"] * (k > 2) + [f"CP{ATT1[k - 2][0]}"] * (k > 1)
            for q in range(2):
                g += [f"X{c}{k}{q}"] + ([f"Z{c}{k}{q}"] if k < LEVELS - 1 else [])
            if c == 0:
                g += beside[k]
            elif k > 1:
                g += [f"H{k - 2}0", f"H{k - 2}1"]
        if c:
            g += [f"CO{ATT1[-2][0]}", f"CP{ATT1[-1][0]}", f"H{LEVELS - 2}0", f"H{LEVELS - 2}1", f"CO{ATT1[-1][0]}"]
            g += [f"H{k}{t}" for k in (LEVELS - 1, LEVELS) for t in range(2)]
        g += [f"R{c}", f"SA{c}", f"Y{c}"] + (["ST", "HS"] if c == 0 else [])
    g += ["HO0", "HO1", "GM0", "GM1", "HN0", "HN1", "GV0", "GV1"]
    for n in BRANCHES:
        for j in range(4):
            g += [f"G{j}{n}", f"M{j}{n}"]
    g += [f"WO{j}" for j in range(4)] + ["norm2"] + [f"U{i}" for i in range(22)] + [f"D{j}" for j in range(4)]
    return g


def groups2():
    g = ["norm", "qk0", "qk1", "mv0", "mv1", "mo0", "mo1", "if", "aq", "ak", "av", "cq0", "cq1", "ckv", "kpe"]
    g += ["acol"] + [x + str(h) for h in range(4) for x in ("gb", "sc", "nd")]
    g += ["mn0", "mn1", "nq", "nk", "rq", "rk"] + att_groups("B", ATT2) + ["bn"]
    g += ["ncq", "nckv", "uq0", "uq1", "uk0", "uk1", "uv", "nlq0", "nlq1", "nlk0", "nlk1", "rlq0", "rlq1", "rlk0", "rlk1"]
    g += att_groups("M", ATT2) + ["ln"]
    g += [f"WO{j}" for j in range(4)] + ["norm2"] + [f"U{i}" for i in range(16)] + [f"D{j}" for j in range(4)]
    return g


SIGNALS = """act_chain dve_chain squares_ready u_ready ready
    pmu_ready pmu_used raw_ready rwkv_low_ready squash_ready cum_ready decay_ready kk_ready kksq_ready rstd_in rstd_out
    rwkv_ops_ready bonus_in tm_ready sc_ready n_ready o1_ready xz_ready rhs_ready sa_ready state_ready y_ready gsq_ready
    ya_ready f_ready hcol_in hcol_out ls_in ls_out lse_in lse_out cum_b pairs_in pairs_ready hk_ready hqe_ready ketm_ready
    hstate_ready hsc_ready hosq_ready yb_ready rope_ready cv_ready logits_ready probs_in probs_ready pt_ready pv_done
    yc_ready yc_split gate_ready gate_used merged_ready conv_in conv_mid conv_out hidden_ready h_ready fresh_norm bi_ready
    bsg_ready gA_ready d_diff d_exp s_ready dn_ready v_ready em_ready latents_sq latents_ready""".split()


def build(nc, x, params1, params2, stream, cst_in, masks_in, pos_in, out, layers=(LAYERS, LAYERS)):
    ctx = ExitStack()
    with ctx:
        def sb(name, shape, dt=F32):
            return ctx.enter_context(nc.sbuf_tensor(name, shape, dt))

        def sem(name):
            return ctx.enter_context(nc.semaphore(name))

        landed = [sem(f"chunk_landed{i}") for i in range(RING)]
        inputs_in, params_in, stored = sem("inputs_in"), sem("params_in"), sem("stored")
        hi_written, pieces_split, pieces_used = sem("hi_written"), sem("pieces_split"), sem("pieces_used")
        arrived, gathered, released, ready = sem("arrived"), sem("gathered"), sem("released"), sem("masks_ready")
        bank_full = [sem(f"bank_full{i}") for i in range(8)]
        bank_free = [sem(f"bank_free{i}") for i in range(8)]
        S = {n: sem(n) for n in SIGNALS}
        per_layer = range(bank_full[0].num, S[SIGNALS[-1]].num + 1)
        assert len(per_layer) == 16 + len(SIGNALS)

        def with_twin(name, shape):
            at = -(-nc.sbuf_base // 32) * 32
            t = sb(name, shape)
            return t, nc.alloc_sbuf_tensor_at(name + "_split", shape, F32R, offset=at)

        ring, ring_lo = with_twin("ring", [P, RING, CHUNK * P])
        h = sb("h", [P, KD, T])
        hi_ring = sb("hi_ring", [P, HI_RING, PIECE * P], F32R)
        u, u_lo = with_twin("u", [P, KD, T])
        u_hi = sb("u_hi", [P, KD, T], F32R)
        par = sb("par", [P, max(PAR1.size, PAR2.size)])
        cst = sb("cst", [P, CST.size])
        msk = sb("msk", [P, MASKS.size], U8)
        small = sb("small", [P, 128])
        ARENA = 36192
        arena_at = -(-nc.sbuf_base // 32) * 32
        arena = sb("arena", [P, ARENA])
        banks = [ctx.enter_context(nc.psum_tensor(f"bank{i}", [P, 512], F32)) for i in range(8)]

        class Carve:
            def __init__(self, start=0):
                self.at = start

            def __call__(self, n):
                a = self.at
                self.at += n
                assert self.at <= ARENA, self.at
                return arena[:, a:a + n]

        def twin(name, ap):
            n = int(np.prod(ap.shape[1:]))
            return nc.alloc_sbuf_tensor_at(name, [P, n], F32R, offset=arena_at + 4 * ap.offset)[:]

        def K(name):
            return CST.of(cst, name)

        def v3(ap, n):
            return ap.rearrange("p (a b) -> p a b", a=n)

        def spread(ap, n):
            return ap.unsqueeze(1).to_broadcast([ap.shape[0], n, ap.shape[1]])

        def along(ap, n):
            return ap.unsqueeze(2).to_broadcast([ap.shape[0], ap.shape[1], n])

        upm = v3(MASKS.of(msk, "up"), LEVELS)
        lowm = v3(MASKS.of(msk, "low"), LEVELS)
        diagm = MASKS.of(msk, "diag")
        ident, ones, bones = K("ident"), K("ones"), K("bones")

        cv = Carve()
        pa = v3(cv(14 * T), 14)
        cc = v3(cv(8 * 129), 8)
        ar = cv(2048).rearrange("p (j a t) -> p j a t", j=8, a=2)
        einv, av, kk, kmod, bonus, gA = (cv(1024) for _ in range(6))
        low = cv(2 * T)
        tw, sg = low[:, 0:T], low[:, T:2 * T]
        rs = low
        btm, ktm, vtm = (v3(cv(1024), 2) for _ in range(3))
        sc = cv(4096).rearrange("p (h a t) -> p h a t", h=8, a=4)
        nn_at = cv.at
        nn, xx, zz = (v3(cv(1024), 8) for _ in range(3))
        o1_flat = cv(1032)
        o1 = v3(o1_flat[:, 0:1024], 8)
        pmu = v3(o1_flat[:, 0:1028], 4)
        bq, bf, bsg, yb = (cv(1024) for _ in range(4))
        sa, st = cv(512), v3(cv(512), 4)
        bi = v3(cv(1024), 2)
        craw = v3(cv(9 * T), 9)
        cvt = v3(cv(T), 2)
        wi = cv(8)
        ya = pa[:, 0:4, :].rearrange("p a t -> p (a t)")
        merged = ar.rearrange("p j a t -> p (j a t)")
        mask_in = craw.rearrange("p a t -> p (a t)")[:, 0:MASKS.size]
        hE, hqk = kk, kmod
        hls = hqk
        hb = bf
        hks = cc.rearrange("p a t -> p (a t)")[:, 0:1024]
        hsc = pa[:, 4:8, :].rearrange("p a t -> p (a t)")
        yc = pa[:, 8:12, :].rearrange("p a t -> p (a t)")
        hke = pa[:, 12:14, :].rearrange("p a t -> p (a t)")
        ketm = hke
        hqe, hst = cv(512), cv(512)
        scr, amask = (v3(cv(512), 2) for _ in range(2))
        lg = [cv(512), scr.rearrange("p a t -> p (a t)")]
        work = [lg[0][:, 0:P], craw[:, 6, :]]
        tmp = cv(T)
        pT = craw[:, 4:6, :].rearrange("p a t -> p (a t)")
        fv = Carve()
        hidden = v3(fv(32 * T), 32)
        cb = [v3(fv(512), 2) for _ in range(4)]
        hidden_hi, hidden_lo = v3(twin("hidden_hi", arena[:, fv.at + 4 * T:fv.at + 36 * T]), 32), v3(twin("hidden_lo", hidden), 32)
        sc_flat = sc.rearrange("p h a t -> p (h a t)")
        ya_lo, yb_lo, yc_lo = twin("ya_lo", ya), twin("yb_lo", yb), twin("yc_lo", yc)
        ya_hi, yb_hi, yc_hi = twin("ya_hi", sc_flat[:, 0:1024]), twin("yb_hi", hqk), twin("yc_hi", av)
        ysq = einv
        merged_hi, merged_lo = twin("merged_hi", arena[:, nn_at:nn_at + 2048]), twin("merged_lo", merged)
        squares = v3(sc.rearrange("p h a t -> p (h a t)")[:, 0:2048], KD)
        gate_buf = [lg[0], lg[1]]
        mtmp = pT
        bv = Carve(fv.at)
        tabs = [bv(T) for _ in range(4)]
        sq2 = v3(bv(8 * T), 8)
        qkraw = v3(bv(4 * T), 4)
        mvt = v3(bv(1024), 2)
        mo = v3(bv(4 * T), 4)
        ifr = bv(8 * T)
        acol = v3(bv(8), 2)
        dT = bv(384)
        sT = [bv(384), bv(384)]
        em, dn = bv(T), bv(T)
        mix = v3(bv(8 * T), 8)
        aqk = v3(bv(4 * T), 4)
        avt = v3(bv(512), 2)
        cqk = v3(bv(5 * T), 5)
        lqk = v3(bv(8 * T), 8)
        kpe = bv(T)
        lvt = v3(bv(512), 2)
        t512 = bv(512)
        lg2 = [bv(512), bv(512)]
        pT2 = [bv(512), bv(512)]
        sqb = bv(1024)
        cqk_hi = v3(twin("latents_hi", bv(5 * T)), 5)
        cqk_lo, mix_lo = v3(twin("latents_lo", cqk), 5), v3(twin("mix_lo", mix), 8)
        mix_hi = v3(twin("mix_hi", sq2), 8)
        mid, emid, eend = small[:, 0:8], small[:, 8:16], small[:, 16:24]
        lbc, lnA, ln1m, omlb = (small[:, 24 + 4 * i:28 + 4 * i] for i in range(4))
        m8, nmax, ssum = small[:, 40:48], small[:, 48:56], small[:, 56:64]
        omu = small[:, 64:78]
        nbf = small[:, 80:81]
        isz = small[:, 84:88]

        b1 = Banks(groups1(), banks, bank_full, bank_free)
        b2 = Banks(groups2(), banks, bank_full, bank_free)
        ends1, ends2 = {}, {}
        u_parts = (u_hi, u_lo)

        block = ctx.enter_context(nc.Block())

        def layer_end(eng, done, leader):
            eng.sem_inc(arrived, 1)
            if leader:
                eng.wait_ge(arrived, (done + 1) * 3)
                eng.sem_inc(gathered, 1)
                eng.sem_clear(per_layer)
                eng.sem_inc(released, 1)
            else:
                eng.wait_ge(released, done + 1)

        @block.sync
        def _(sp):
            sp.dma_start(h[:], x).then_inc(inputs_in, 16)
            sp.dma_start(cst[:], cst_in).then_inc(inputs_in, 16)
            sp.dma_start(mask_in, masks_in).then_inc(inputs_in, 16)
            n = (layers[0] * CH1 + layers[1] * CH2) // RING
            with sp.Fori(0, n) as r:
                for s in range(RING):
                    sp.wait_ge(pieces_used, r * (RING * CHUNK // PIECE) + (s + 1) * (CHUNK // PIECE))
                    sp.dma_start(ring[:, s, :], stream[bass.ds(r * RING + s, 1)].rearrange("a p n -> p (a n)"))\
                      .then_inc(landed[s], 16)

        @block.gpsimd
        def _(pool):
            n = (layers[0] * CH1 + layers[1] * CH2) // RING
            per_round = RING * CHUNK // PIECE
            with pool.Fori(0, n) as r:
                for i in range(per_round):
                    pool.wait_ge(hi_written, r * per_round + (i + 1))
                    c, o = i * PIECE // CHUNK, i * PIECE % CHUNK * P
                    x_ = ring[:, c, o:o + PIECE * P]
                    nc.gpsimd.tensor_tensor(ring_lo[:, c, o:o + PIECE * P], x_, hi_ring[:, i % HI_RING, :].bitcast(F32), ALU.subtract).then_inc(pieces_split, 1)

        @block.tensor
        def _(pe):
            pe.sem_inc(pieces_used, RING * CHUNK // PIECE)

            def runner(B, W):
                def mm(o, l, r, start=True, stop=True, full=None, done=None):
                    ins = nc.tensor.matmul(o, l, r, start=start, stop=stop)
                    if full is not None:
                        ins.then_inc(B.full_of(full), 1)
                    elif done is not None:
                        ins.then_inc(done, 1)
                    elif W.pending:
                        W.pending -= 1
                        ins.then_inc(pieces_used, 1)

                def mm3(o, l, r, start, stop, full=None):
                    mm(o, l[0], r[0], start, False)
                    mm(o, l[0], r[1], False, False)
                    mm(o, l[1], r[0], False, stop, full=full)

                def cut(act, *at):
                    return tuple(a[(slice(None), *at)] for a in act)

                def after(signal, base, per):
                    return lambda k: None if k % per else pe.wait_ge(S[signal], base + k // per + 1)

                def project(name, tiles, act, K_=KD, ready=None):
                    bank = B.open(pe, name)
                    for i in range(tiles):
                        q = W.take(name, K_)
                        for k in range(K_):
                            if ready and i == 0:
                                ready(k)
                            mm3(bank[:, i * T:(i + 1) * T], W.block(q + k), cut(act, k), k == 0, k == K_ - 1,
                                full=name if (i, k) == (tiles - 1, K_ - 1) else None)
                            W.done(q + k)

                def project_rows(names, act, width, K_=KD):
                    n = width * P
                    q = W.take(names[0], K_ * width)
                    if len(names) == 2:
                        open_ = [B.open(pe, name) for name in names]
                        for k in range(K_):
                            for t in range(NT):
                                mm3(open_[t][:, 0:n], cut(act, k, slice(t * P, (t + 1) * P)), W.block(q + k * width, width),
                                    k == 0, k == K_ - 1, full=names[t] if k == K_ - 1 else None)
                            for b in range(width):
                                W.done(q + k * width + b)
                        return
                    bank = B.open(pe, names[0])
                    for t in range(NT):
                        for k in range(K_):
                            mm3(bank[:, t * n:(t + 1) * n], cut(act, k, slice(t * P, (t + 1) * P)), W.block(q + k * width, width),
                                k == 0, k == K_ - 1, full=names[0] if (t, k) == (NT - 1, K_ - 1) else None)
                            for b in range(width if t == NT - 1 else 0):
                                W.done(q + k * width + b)

                def sums(name, mat, act, n, rows=P):
                    bank = B.open(pe, name)
                    for i in range(n):
                        mm(bank[0:rows, i * T:(i + 1) * T], mat, act[:, i, :], full=name if i == n - 1 else None)

                def total(name, act, n, ready=None):
                    bank = B.open(pe, name)
                    for i in range(n):
                        if ready:
                            ready(i)
                        mm(bank[:, 0:T], ones, act[:, i, :], i == 0, i == n - 1, full=name if i == n - 1 else None)

                def turn(name, tiles):
                    bank = B.open(pe, name)
                    for i, a in enumerate(tiles):
                        ins = nc.tensor.transpose(bank[:, i * P:(i + 1) * P], a, ident)
                    ins.then_inc(B.full_of(name), 1)

                def attention(tag, batches, q, k, v, pt, before=None):
                    def logits(i):
                        b, tt, heads = batches[i]
                        w = (tt + 1) * P
                        bank = B.open(pe, f"{tag}L{b}")
                        for j, hd in enumerate(heads):
                            mm(bank[:, j * w:(j + 1) * w], q(hd)[:, tt * P:(tt + 1) * P], k(hd)[:, 0:w],
                               full=f"{tag}L{b}" if j == len(heads) - 1 else None)

                    def value(i):
                        b, tt, heads = batches[i]
                        pe.wait_ge(S["probs_ready"], att_base[0] + i + 1)
                        turn(f"{tag}P{b}", [pt[0][i % 2][:, j * P:(j + 1) * P] for j in range(len(heads) * (tt + 1))])
                        pe.wait_ge(S["pt_ready"], att_base[0] + i + 1)
                        firsts = [x_[0] for x_ in batches if x_[1] == tt]
                        if b == firsts[0]:
                            B.open(pe, f"{tag}O{tt}")
                        o = B.tiles[B.slot[f"{tag}O{tt}"][0]]
                        for j, hd in enumerate(heads):
                            r, c = 64 * (hd % 2), hd // 2 * P
                            for s in range(tt + 1):
                                last = j == len(heads) - 1 and s == tt
                                at = (j * (tt + 1) + s) * P
                                mm(o[r:r + 64, c:c + P], v(hd, s), pt[1][i % 2][:, at:at + P], s == 0, s == tt,
                                   full=f"{tag}O{tt}" if last and b == firsts[-1] else None,
                                   done=S["pv_done"] if last and b != firsts[-1] else None)

                    for i in range(len(batches)):
                        logits(i)
                        value(i)
                    att_base[0] += len(batches)

                att_base = [0]
                return mm, mm3, cut, after, project, project_rows, sums, total, turn, attention

            pe.wait_ge(inputs_in, 48)
            with pe.Fori(0, layers[0]) as l:
                W = Weights(pe, ring_lo, hi_ring, pieces_split, pieces_used, l * PIECES1, ends1)
                B = b1
                mm, mm3, cut, after, project, project_rows, sums, total, turn, attention = runner(B, W)
                total("norm", squares, KD, after("squares_ready", 0, 2))
                for i in range(7):
                    project(f"A{i}", 2, u_parts, ready=None if i else after("u_ready", 0, 2))
                project("Bg0", 2, u_parts)
                pe.wait_ge(params_in, (l + 1) * 16)
                up = PAR1.of(par, "wa_up")
                pe.wait_ge(S["rwkv_low_ready"], 1)
                for a, n in ((0, "Wup"), (64, "Aup")):
                    rhs = tw[0:64, :] if a == 0 else pa[64:128, 12, :]
                    for g in range(2):
                        bank = B.open(pe, f"{n}{g}")
                        for i in range(2):
                            j = 2 * g + i
                            mm(bank[:, i * T:(i + 1) * T], up[a:a + 64, j * P:(j + 1) * P], rhs,
                               full=f"{n}{g}" if i else None)
                pe.wait_ge(S["rwkv_low_ready"], 2)
                for g in range(2):
                    bank = B.open(pe, f"Gup{g}")
                    for i in range(2):
                        j = 2 * g + i
                        mm(bank[:, i * T:(i + 1) * T], PAR1.of(par, "g_up")[:, j * P:(j + 1) * P], sg,
                           full=f"Gup{g}" if i else None)
                project("Bg1", 2, u_parts)
                pe.wait_ge(S["kksq_ready"], 1)
                for g in range(2):
                    sums(f"KK{g}", bones, v3(bonus, 4)[:, 2 * g:2 * g + 2, :], 2)
                for n in ("Bq0", "Bq1", "Bf0", "Bf1", "Cq0", "Cq1"):
                    project(n, 2, u_parts)
                pe.wait_ge(S["bonus_in"], 1)
                for g in range(2):
                    sums(f"BON{g}", bones, v3(bonus, 4)[:, 2 * g:2 * g + 2, :], 2)
                project("Ck", 2, u_parts)
                pe.wait_ge(S["rwkv_ops_ready"], 1)
                bt, kt = v3(av, 8), v3(einv, 8)
                for c in range(2):
                    turn(f"Tb{c}", [bt[:, 2 * j + c, :] for j in range(4)])
                    turn(f"Tk{c}", [kt[:, 2 * j + c, :] for j in range(4)])
                    turn(f"Tv{c}", [pa[:, 8 + j, c * P:(c + 1) * P] for j in range(4)])

                def scores(c):
                    for hd in range(8):
                        r, j = 64 * (hd % 2), hd // 2 * 2 + c
                        bank = B.open(pe, f"S{c}{hd}")
                        both = ar[r:r + 64, j, :, :].rearrange("p a t -> p (a t)")
                        mm(bank[:, 0:T], bt[r:r + 64, j, :], both)
                        mm(bank[:, T:2 * T], kt[r:r + 64, j, :], both, full=f"S{c}{hd}")
                    for q in range(2):
                        bank = B.open(pe, f"N{c}{q}")
                        for i, hd in enumerate(HALVES[q]):
                            r, j = 64 * (hd % 2), hd // 2 * 2 + c
                            mm(bank[:, i * P:(i + 1) * P], ar[r:r + 64, j, 0, :], bt[r:r + 64, j, :],
                               full=f"N{c}{q}" if i == 3 else None)

                def level_first(c, k):
                    for q in range(2):
                        pe.wait_ge(S["xz_ready"], c * 2 * LEVELS + (k - 1) * 2 + q + 1)
                        bank = B.open(pe, f"O{c}{k}{q}")
                        for i in range(4):
                            hd = 4 * q + i
                            mm(bank[:, i * P:(i + 1) * P], nn[:, hd, :], xx[:, hd, :],
                               full=f"O{c}{k}{q}" if i == 3 else None)

                def level_second(c, k):
                    for q in range(2):
                        pe.wait_ge(S["o1_ready"], c * 2 * (LEVELS - 1) + (k - 1) * 2 + q + 1)
                        for n, l_, r_ in (("X", zz, o1), ("Z", o1, zz)):
                            if n == "Z" and k == LEVELS - 1:
                                continue
                            bank = B.open(pe, f"{n}{c}{k}{q}")
                            for i in range(4):
                                hd = 4 * q + i
                                mm(bank[:, i * P:(i + 1) * P], l_[:, hd, :], r_[:, hd, :],
                                   full=f"{n}{c}{k}{q}" if i == 3 else None)

                def solve(c):
                    pe.wait_ge(S["tm_ready"], 6)
                    bank = B.open(pe, f"R{c}")
                    for j in range(4):
                        if c:
                            if j == 0:
                                pe.wait_ge(S["state_ready"], 1)
                            mm(bank[:, j * P:(j + 1) * P], ar[:, 2 * j + c, 0, :], st[:, j, :], True, False)
                        for hd in (2 * j, 2 * j + 1):
                            mm(bank[:, hd * 64:hd * 64 + 64], sc[:, hd, 2, :], vtm[:, c, hd * 64:hd * 64 + 64], c == 0, c == 0 or hd % 2 == 1,
                               full=f"R{c}" if hd == 7 else None)
                    pe.wait_ge(S["rhs_ready"], c + 1)
                    pe.wait_ge(S["xz_ready"], (c + 1) * 2 * LEVELS)
                    bank = B.open(pe, f"SA{c}")
                    for hd in range(8):
                        mm(bank[:, hd * 64:hd * 64 + 64], xx[:, 4 * (hd % 2) + hd // 2, :], rs[:, hd * 64:hd * 64 + 64],
                           full=f"SA{c}" if hd == 7 else None)
                    pe.wait_ge(S["sa_ready"], c + 1)
                    bank = B.open(pe, f"Y{c}")
                    for j in range(4):
                        if c:
                            mm(bank[:, j * P:(j + 1) * P], st[:, j, :], ar[:, 2 * j + c, 1, :], True, False)
                        for hd in (2 * j, 2 * j + 1):
                            r = 64 * (hd % 2)
                            o = bank[r:r + 64, j * P:(j + 1) * P]
                            mm(o, sa[:, hd * 64:hd * 64 + 64], sc[:, hd, 1, :], c == 0, False)
                            mm(o, vtm[:, c, hd * 64:hd * 64 + 64], sc[:, hd, 3, :], False, True,
                               full=f"Y{c}" if hd == 7 else None)
                    if c == 0:
                        bank = B.open(pe, "ST")
                        for hd in range(8):
                            r, j = 64 * (hd % 2), hd // 2
                            o = bank[r:r + 64, j * 64:(j + 1) * 64]
                            mm(o, btm[:, 0, hd * 64:hd * 64 + 64], sa[:, hd * 64:hd * 64 + 64], True, False)
                            mm(o, ktm[:, 0, hd * 64:hd * 64 + 64], vtm[:, 0, hd * 64:hd * 64 + 64], False, True,
                               full="ST" if hd == 7 else None)

                def hgrn_pairs(k):
                    pe.wait_ge(S["pairs_ready"], k + 1)
                    qk = v3(hqk, 8)
                    for c in range(2):
                        bank = B.open(pe, f"H{k}{c}")
                        for hd in range(4):
                            i = 2 * hd + c
                            l_, r_ = (qk[:, i, :], qk[:, i, :]) if k < LEVELS else (v3(hks, 8)[:, i, :], v3(bq, 8)[:, i, :])
                            mm(bank[:, hd * P:(hd + 1) * P], l_, r_, full=f"H{k}{c}" if hd == 3 else None)

                def part(hd):
                    return slice(64 * (hd % 2), 64 * (hd % 2) + 64)

                def index():
                    pe.wait_ge(S["rope_ready"], 1)
                    for name, tt, heads in INDEX:
                        w = (tt + 1) * P
                        bank = B.open(pe, name)
                        for i, hd in enumerate(heads):
                            mm(bank[:, i * w:(i + 1) * w], craw[part(hd), 4 + hd // 2, tt * P:(tt + 1) * P],
                               craw[part(hd), 6, 0:w], full=name if i == len(heads) - 1 else None)

                def logits(i):
                    b, tt, heads = ATT1[i]
                    w = (tt + 1) * P
                    bank = B.open(pe, f"CL{b}")
                    for j, hd in enumerate(heads):
                        mm(bank[:, j * w:(j + 1) * w], craw[part(hd), hd // 2, tt * P:(tt + 1) * P], craw[part(hd), 7 + hd // 4, 0:w],
                           full=f"CL{b}" if j == len(heads) - 1 else None)

                def turn_probs(i):
                    b, tt, heads = ATT1[i]
                    pe.wait_ge(S["probs_ready"], i + 1)
                    turn(f"CP{b}", [lg[i % 2][:, j * P:(j + 1) * P] for j in range(len(heads) * (tt + 1))])

                def values(i):
                    b, tt, heads = ATT1[i]
                    pe.wait_ge(S["pt_ready"], i + 1)
                    bank = B.open(pe, f"CO{b}")
                    for j, hd in enumerate(heads):
                        for s in range(tt + 1):
                            at = (j * (tt + 1) + s) * P
                            mm(bank[part(hd), j * P:(j + 1) * P], cvt[:, s, hd // 4 * 64:hd // 4 * 64 + 64], pT[:, at:at + P],
                               s == 0, s == tt, full=f"CO{b}" if j == len(heads) - 1 and s == tt else None)

                scores(0)
                project_rows(["Bi0", "Bi1"], u_parts, 4)
                for k in range(1, LEVELS):
                    level_first(0, k)
                    level_second(0, k)
                    if k == 1:
                        project("Cqi", 2, u_parts)
                    elif k == 2:
                        project("Cki", 1, u_parts)
                    elif k == 3:
                        bank = B.open(pe, "Cv")
                        q = W.take("Cv", 2 * KD)
                        n = P + 4
                        for t in range(NT):
                            for i in range(KD):
                                mm3(bank[:, t * n:(t + 1) * n], cut(u_parts, i, slice(t * P, (t + 1) * P)),
                                    [w[:, 0:n] for w in W.block(q + 2 * i, 2)], i == 0, i == KD - 1,
                                    full="Cv" if (t, i) == (NT - 1, KD - 1) else None)
                                for b in range(2 if t == NT - 1 else 0):
                                    W.done(q + 2 * i + b)
                    elif k == 4:
                        pe.wait_ge(S["raw_ready"], 5)
                        sums("Rq0", K("rot"), craw[:, 0:2, :], 2)
                        sums("Rq1", K("rot"), craw[:, 2:4, :], 2)
                        sums("Rk", K("rot"), craw[:, 7:9, :], 2)
                        sums("Rqi", K("rot"), craw[:, 4:6, :], 2)
                        sums("Rki", K("rot"), craw[:, 6:7, :], 1)
                    elif k == 5:
                        index()
                    else:
                        pe.wait_ge(S["hk_ready"], 1)
                        turn("HT", [v3(hke, 4)[:, hd, :] for hd in range(4)])
                solve(0)
                pe.wait_ge(S["ketm_ready"], 1)
                pe.wait_ge(S["bi_ready"], 2)
                bank = B.open(pe, "HS")
                for hd in range(4):
                    mm(bank[:, hd * P:(hd + 1) * P], ketm[:, hd * P:(hd + 1) * P], bi[:, 0, hd * P:(hd + 1) * P],
                       full="HS" if hd == 3 else None)
                scores(1)
                for k in range(1, LEVELS):
                    level_first(1, k)
                    logits(k - 1)
                    if k > 2:
                        values(k - 3)
                    if k > 1:
                        turn_probs(k - 2)
                    level_second(1, k)
                    if k > 1:
                        hgrn_pairs(k - 2)
                values(len(ATT1) - 2)
                turn_probs(len(ATT1) - 1)
                hgrn_pairs(LEVELS - 2)
                values(len(ATT1) - 1)
                hgrn_pairs(LEVELS - 1)
                hgrn_pairs(LEVELS)
                solve(1)
                pe.wait_ge(S["hsc_ready"], 1)
                pe.wait_ge(S["hqe_ready"], 1)
                pe.wait_ge(S["hstate_ready"], 1)
                for c in range(2):
                    bank = B.open(pe, f"HO{c}")
                    for hd in range(4):
                        o = bank[:, hd * P:(hd + 1) * P]
                        mm(o, bi[:, c, hd * P:(hd + 1) * P], v3(hsc, 8)[:, 2 * hd + c, :], True, c == 0,
                           full=f"HO{c}" if c == 0 and hd == 3 else None)
                        if c:
                            mm(o, v3(hst, 4)[:, hd, :], v3(hqe, 4)[:, hd, :], False, True,
                               full=f"HO{c}" if hd == 3 else None)
                pe.wait_ge(S["y_ready"], 2)
                for g in range(2):
                    sums(f"GM{g}", bones, v3(ya, 4)[:, 2 * g:2 * g + 2, :], 2)
                pe.wait_ge(S["hosq_ready"], 2)
                for g in range(2):
                    sums(f"HN{g}", ones, v3(hE, 4)[:, 2 * g:2 * g + 2, :], 2)
                pe.wait_ge(S["gsq_ready"], 1)
                for g in range(2):
                    sums(f"GV{g}", bones, v3(ysq, 4)[:, 2 * g:2 * g + 2, :], 2)
                ys = [(v3(a, 4), v3(b, 4)) for a, b in ((ya_hi, ya_lo), (yb_hi, yb_lo), (yc_hi, yc_lo))]
                for n in BRANCHES:
                    for j in range(4):
                        project(f"G{j}{n}", 2, u_parts)
                        if j == 0:
                            pe.wait_ge(S[("ya_ready", "yb_ready", "yc_split")[n]], 1)
                        project(f"M{j}{n}", 2, ys[n], 4)
                for j in range(4):
                    project(f"WO{j}", 2, (v3(merged_hi, KD), v3(merged_lo, KD)), ready=None if j else after("merged_ready", 0, 2))
                total("norm2", squares, KD, after("squares_ready", KD // 2, 2))
                for i in range(22):
                    project(f"U{i}", 2, u_parts, ready=None if i else after("u_ready", KD // 2, 2))
                for j in range(4):
                    project(f"D{j}", 2, (hidden_hi, hidden_lo), 22, ready=None if j else after("hidden_ready", 0, 1))
                B.wait(pe, "D3")
                W.skip(BLOCKS1)
                layer_end(pe, l, False)

            W = Weights(pe, ring_lo, hi_ring, pieces_split, pieces_used, 0, {})
            total_, after = (runner(b2, W)[i] for i in (7, 3))
            total_("norm", squares, KD, after("squares_ready", 0, 2))
            pe.wait_ge(S["ready"], 1)
            nc.tensor.matmul(banks[1][:, 0:T], ones[0:1, :], t512[0:1, 0:T], start=True, stop=True)\
              .then_inc(bank_full[1], 1)
            layer_end(pe, layers[0], False)

            if not layers[1]:
                return
            with pe.Fori(0, layers[1]) as l:
                W = Weights(pe, ring_lo, hi_ring, pieces_split, pieces_used, l * PIECES2 + layers[0] * PIECES1, ends2)
                B = b2
                mm, mm3, cut, after, project, project_rows, sums, total, turn, attention = runner(B, W)
                total("norm", squares, KD, after("squares_ready", 0, 2))
                project("qk0", 2, u_parts, ready=after("u_ready", 0, 2))
                project("qk1", 2, u_parts)
                project_rows(["mv0", "mv1"], u_parts, 4)
                project("mo0", 2, u_parts)
                project("mo1", 2, u_parts)
                bank = B.open(pe, "if")
                q = W.take("if", KD)
                for i in range(2):
                    for k in range(KD):
                        mm3(bank[0:4, i * T:(i + 1) * T], [w[:, 32 * i:32 * i + 4] for w in W.block(q + k)], cut(u_parts, k), k == 0, k == KD - 1,
                            full="if" if (i, k) == (1, KD - 1) else None)
                for k in range(KD):
                    W.done(q + k)
                project("aq", 2, u_parts)
                project("ak", 2, u_parts)
                project_rows(["av"], u_parts, 2)
                project("cq0", 2, u_parts)
                project("cq1", 1, u_parts)
                project("ckv", 2, u_parts)
                bank = B.open(pe, "kpe")
                q = W.take("kpe", KD)
                for k in range(KD):
                    mm3(bank[:, 0:T], W.block(q + k), cut(u_parts, k), k == 0, k == KD - 1,
                        full="kpe" if k == KD - 1 else None)
                    W.done(q + k)
                pe.wait_ge(S["d_diff"], 1)
                bank = B.open(pe, "acol")
                for t in range(NT):
                    ins = nc.tensor.transpose(bank[:, 4 * t:4 * t + 4], ifr[0:4, t * P:(t + 1) * P], ident[0:4, 0:4])
                ins.then_inc(B.full_of("acol"), 1)
                pe.wait_ge(S["conv_out"], 4)
                pe.wait_ge(S["v_ready"], 2)
                for hd in range(4):
                    bank = B.open(pe, f"gb{hd}")
                    mm(bank[:, 0:2 * T], ident[0:4, hd:hd + 1].to_broadcast([4, P]), ifr[0:4, 2 * T:4 * T], full=f"gb{hd}")
                    bank = B.open(pe, f"sc{hd}")
                    r = 64 * (hd % 2)
                    qh, kh = qkraw[r:r + 64, hd // 2, :], qkraw[r:r + 64, 2 + hd // 2, :]
                    mm(bank[:, 0:T], kh[:, 0:P], qh)
                    mm(bank[:, T:T + P], kh[:, P:T], qh[:, P:T], full=f"sc{hd}")
                    pe.wait_ge(S["s_ready"], hd + 1)
                    bank = B.open(pe, f"nd{hd}")
                    s_ = sT[hd % 2]
                    for o, l0, l1 in ((0, mvt[:, 0, hd * P:(hd + 1) * P], mvt[:, 1, hd * P:(hd + 1) * P]), (T, ones, ones)):
                        mm(bank[:, o:o + T], l0, s_[:, 0:T], True, False)
                        mm(bank[:, o + P:o + T], l1, s_[:, T:T + P], False, True, full=f"nd{hd}" if o else None)
                pe.wait_ge(S["hosq_ready"], 1)
                for g in range(2):
                    sums(f"mn{g}", ones, v3(sqb, 4)[:, 2 * g:2 * g + 2, :], 2)
                pe.wait_ge(S["kksq_ready"], 1)
                sums("nq", bones, v3(sqb, 4)[:, 0:2, :], 2)
                sums("nk", bones, v3(sqb, 4)[:, 2:4, :], 2)
                pe.wait_ge(S["kk_ready"], 1)
                sums("rq", K("rotp"), aqk[:, 0:2, :], 2)
                sums("rk", K("rotp"), aqk[:, 2:4, :], 2)
                pe.wait_ge(S["rope_ready"], 1)

                def part(hd):
                    return slice(64 * (hd % 2), 64 * (hd % 2) + 64)

                attention("B", ATT2, lambda hd: aqk[part(hd), hd // 2, :], lambda hd: aqk[part(hd), 2 + hd // 2, :],
                          lambda hd, s: avt[:, s, hd * 64:hd * 64 + 64], (lg2, pT2))
                pe.wait_ge(S["gsq_ready"], 2)
                sums("bn", bones, v3(sqb, 4)[:, 0:2, :], 2)
                pe.wait_ge(S["latents_sq"], 1)
                total("ncq", sq2[:, 0:3, :], 3)
                total("nckv", sq2[:, 3:5, :], 2)
                pe.wait_ge(S["latents_ready"], 1)
                latents = (cqk_hi, cqk_lo)
                for g in range(2):
                    bank = B.open(pe, f"uq{g}")
                    for i in range(2):
                        q = W.take(f"uq{g}", 3)
                        for k in range(3):
                            mm3(bank[0:MLA_D, i * T:(i + 1) * T], [w[:, 0:MLA_D] for w in W.block(q + k)], cut(latents, k), k == 0, k == 2,
                                full=f"uq{g}" if (i, k) == (1, 2) else None)
                            W.done(q + k)
                for g in range(2):
                    bank = B.open(pe, f"uk{g}")
                    q = W.take(f"uk{g}", 2)
                    for i in range(2):
                        for k in range(2):
                            mm3(bank[0:64, i * T:(i + 1) * T], [w[:, 64 * i:64 * i + 64] for w in W.block(q + k)], cut(latents, 3 + k),
                                k == 0, k == 1, full=f"uk{g}" if (i, k) == (1, 1) else None)
                    W.done(q)
                    W.done(q + 1)
                project_rows(["uv"], [a[:, 3:5, :] for a in latents], 2, 2)
                pe.wait_ge(S["lse_in"], 1)
                for n, o in (("nlq", 0), ("nlk", 4)):
                    for g in range(2):
                        sums(f"{n}{g}", ones[0:MLA_D, 0:MLA_D], sq2[0:MLA_D, o + 2 * g:o + 2 * g + 2, :], 2, MLA_D)
                pe.wait_ge(S["lse_out"], 1)
                for n, o in (("rlq", 0), ("rlk", 4)):
                    for g in range(2):
                        sums(f"{n}{g}", K("rotd")[0:MLA_D, 0:MLA_D], lqk[0:MLA_D, o + 2 * g:o + 2 * g + 2, :], 2, MLA_D)
                pe.wait_ge(S["rope_ready"], 2)
                attention("M", ATT2, lambda hd: lqk[0:MLA_D, hd, :], lambda hd: lqk[0:MLA_D, 4 + hd, :],
                          lambda hd, s: lvt[:, s, hd * 64:hd * 64 + 64], (lg2, pT2))
                pe.wait_ge(S["gsq_ready"], 4)
                sums("ln", bones, v3(sqb, 4)[:, 0:2, :], 2)
                pe.wait_ge(S["yc_ready"], 1)
                for j in range(4):
                    project(f"WO{j}", 2, (mix_hi, mix_lo))
                total("norm2", squares, KD, after("squares_ready", KD // 2, 2))
                for i in range(16):
                    project(f"U{i}", 2, u_parts, ready=None if i else after("u_ready", KD // 2, 2))
                for j in range(4):
                    project(f"D{j}", 2, (hidden_hi, hidden_lo), 32, ready=None if j else after("hidden_ready", 0, 2))
                B.wait(pe, "D3")
                W.skip(BLOCKS2)
                layer_end(pe, l + (layers[0] + 1), False)

        @block.scalar
        def _(act):
            def A(o, i, f, **kw):
                return nc.scalar.activation(o, i, f, **kw)

            def norm_squares(C, fresh=False):
                for j in range(KD // 2):
                    if fresh:
                        act.wait_ge(S["h_ready"], j + 1)
                    C.link(A(squares[:, 2 * j:2 * j + 2, :], h[:, 2 * j:2 * j + 2, :], ACT.Square), S["squares_ready"])

            def rstd(C, B, names, buf, scale, eps="eps", rows=P, width=512):
                for name in names:
                    B.wait(act, name)
                for g, name in enumerate(names):
                    bank = B.wait(act, name)
                    C.link(A(buf[0:rows, g * width:(g + 1) * width], bank[0:rows, 0:width], ACT.Ln,
                             scale=scale[g] if isinstance(scale, tuple) else scale, bias=K(eps)[0:rows]))
                    B.release(act, name)
                full = buf[0:rows, 0:len(names) * width]
                C.link(A(full, full, ACT.Exp, scale=-0.5), S["rstd_out"])

            def attention(C, B, tag, batches, base, lgs, pts, take):
                for i, (b, tt, heads) in enumerate(batches):
                    w = (tt + 1) * P
                    act.wait_ge(S["probs_in"], base + i + 1)
                    for j in range(len(heads)):
                        C.link(A(lgs[i % 2][:, j * w:(j + 1) * w], lgs[i % 2][:, j * w:(j + 1) * w], ACT.Exp,
                                 bias=nmax[:, j:j + 1], accum_out=ssum[:, j:j + 1]))
                    act.sem_inc(S["logits_ready"], 1)
                    bank = B.wait(act, f"{tag}P{b}")
                    C.link(A(pts[i % 2][:, 0:len(heads) * w], bank[:, 0:len(heads) * w], ACT.Copy), S["pt_ready"])
                    B.release(act, f"{tag}P{b}")
                    if b == [x_[0] for x_ in batches if x_[1] == tt][-1]:
                        bank = B.wait(act, f"{tag}O{tt}")
                        take(tt, bank)
                        B.release(act, f"{tag}O{tt}")

            class HiParts:

                def __init__(self, ends, first, first_round):
                    self.ends, self.first, self.first_round, self.at = ends, first, first_round, 0

                def upto(self, name):
                    stop = HI_RING if name == "start" else min(self.ends[name] + LEAD, max(self.ends.values()))
                    for q in range(self.at, stop):
                        c, o = q * PIECE // CHUNK, q * PIECE % CHUNK * P
                        if o == 0:
                            act.wait_ge(landed[c % RING], (self.first_round + (c // RING + 1)) * 16)
                        act.wait_ge(pieces_used, self.first + (RING * CHUNK // PIECE + q + 1 - HI_RING))
                        A(hi_ring[:, q % HI_RING, :], ring[:, c % RING, o:o + PIECE * P], ACT.Copy).then_inc(hi_written, 1)
                    self.at = max(self.at, stop)

            act.wait_ge(inputs_in, 48)
            with act.Fori(0, layers[0]) as l:
                C, B = Chain(act, S["act_chain"]), b1
                hi = HiParts(ends1, l * PIECES1, l * (CH1 // RING))
                hi.upto("start")
                act.dma_start(par[:, 0:PAR1.size], params1[bass.ds(l, 1)].rearrange("a p n -> p (a n)")).then_inc(params_in, 16)
                norm_squares(C)
                rstd(C, B, ["norm"], tw, 1.0 / D, width=T)
                act.wait_ge(params_in, (l + 1) * 16)
                mu = PAR1.of(par, "mu")
                for i in range(14):
                    hi.upto(f"A{i // 2}")
                    bank = B.wait(act, f"A{i // 2}")
                    if i == 0:
                        act.wait_ge(S["pmu_used"], 1)
                    if i >= 4:
                        act.wait_ge(S["pmu_used"], 2 * (i // 2) - 1)
                    C.link(A(pmu[:, i % 4, 1:], bank[:, i % 2 * T:(i % 2 + 1) * T], ACT.Copy, scale=mu[:, i:i + 1]), S["pmu_ready"])
                act.wait_ge(S["pmu_used"], 15)
                C.link(A(tw[0:64, :], pa[0:64, 12, :], ACT.Tanh), S["rwkv_low_ready"])
                C.link(A(sg, pa[:, 13, :], ACT.Sigmoid), S["rwkv_low_ready"])
                hi.upto("Bg0")
                for n, o, z in (("Wup", einv, "w0"), ("Aup", av, "a0")):
                    for g in range(2):
                        bank = B.wait(act, f"{n}{g}")
                        for i in range(2):
                            j = 2 * g + i
                            C.link(A(v3(o, 4)[:, j, :], bank[:, i * T:(i + 1) * T], ACT.Sigmoid,
                                     bias=PAR1.of(par, z)[:, j:j + 1]), S["squash_ready"])
                        B.release(act, f"{n}{g}")
                for g in range(2):
                    bank = B.wait(act, f"Gup{g}")
                    C.link(A(gA[:, g * 512:(g + 1) * 512], bank[:, :], ACT.Copy), S["gA_ready"])
                    B.release(act, f"Gup{g}")
                act.wait_ge(S["kk_ready"], 1)
                C.link(A(bonus, kk, ACT.Square), S["kksq_ready"])
                for g in range(2):
                    hi.upto(f"Bg{g}")
                    bank = B.wait(act, f"Bg{g}")
                    C.link(A(bsg[:, g * 512:(g + 1) * 512], bank[:, :], ACT.Silu), S["bsg_ready"])
                    B.release(act, f"Bg{g}")
                nc.scalar.preload_act_table_set(LN_EXP)
                hi.upto("Bq0")
                act.wait_ge(S["cum_ready"], 1)
                C.link(A(emid, mid, ACT.Exp, scale=-KAPPA))
                C.link(A(eend, cc[:, :, P], ACT.Exp, scale=-KAPPA))
                C.link(A(ar[:, :, 0, :], cc[:, :, 0:P], ACT.Exp, scale=-KAPPA))
                C.link(A(ar[:, :, 1, :], cc[:, :, 1:P + 1], ACT.Exp, scale=-KAPPA))
                C.link(A(v3(einv, 8), cc[:, :, 1:P + 1], ACT.Exp, scale=KAPPA), S["decay_ready"])
                hi.upto("Bq1")
                act.wait_ge(S["rstd_in"], 1)
                C.link(A(bonus, bonus, ACT.Ln))
                C.link(A(bonus, bonus, ACT.Exp, scale=-0.5), S["rstd_out"])
                for g in range(2):
                    hi.upto(f"Bq{g}")
                    bank = B.wait(act, f"Bq{g}")
                    C.link(A(bq[:, g * 512:(g + 1) * 512], bank[:, :], ACT.Copy))
                    B.release(act, f"Bq{g}")

                def take_raw(n, o, w):
                    hi.upto(n)
                    bank = B.wait(act, n)
                    C.link(A(craw[:, o:o + w, :].rearrange("p a t -> p (a t)"), bank[:, 0:w * T], ACT.Copy), S["raw_ready"])
                    B.release(act, n)

                take_raw("Cq0", 0, 2)
                take_raw("Cq1", 2, 2)
                take_raw("Ck", 7, 2)
                for c in range(2):
                    for n, o in (("Tb", btm), ("Tk", ktm), ("Tv", vtm)):
                        bank = B.wait(act, f"{n}{c}")
                        C.link(A(o[:, c, :], bank[:, :], ACT.Copy), S["tm_ready"])
                        B.release(act, f"{n}{c}")

                def level(c, k):
                    for q in range(2):
                        bank = B.wait(act, f"O{c}{k}{q}")
                        C.link(A(o1[:, 4 * q:4 * q + 4, :].rearrange("p a t -> p (a t)"), bank[:, :], ACT.Copy), S["o1_ready"])
                        B.release(act, f"O{c}{k}{q}")

                def solve(c):
                    bank = B.wait(act, f"R{c}")
                    C.link(A(rs, bank[:, :], ACT.Copy), S["rhs_ready"])
                    B.release(act, f"R{c}")
                    bank = B.wait(act, f"SA{c}")
                    C.link(A(sa, bank[:, :], ACT.Copy), S["sa_ready"])
                    B.release(act, f"SA{c}")
                    bank = B.wait(act, f"Y{c}")
                    C.link(A(v3(ya, 4)[:, :, c * P:(c + 1) * P], v3(bank[:, :], 4), ACT.Copy), S["y_ready"])
                    B.release(act, f"Y{c}")

                def take_values(i):
                    b, tt, heads = ATT1[i]
                    bank = B.wait(act, f"CO{b}")
                    r, n, j0 = 64 * (heads[0] % 2), len(heads), heads[0] // 2
                    C.link(A(v3(yc, 4)[r:r + 64, j0:j0 + n, tt * P:(tt + 1) * P], v3(bank[r:r + 64, 0:n * P], n), ACT.Copy), S["yc_ready"])
                    B.release(act, f"CO{b}")

                def pair_decays(k):
                    act.wait_ge(S["pairs_in"], k + 1)
                    C.link(A(hE, hE, ACT.Exp), S["d_exp"])

                for t in range(NT):
                    hi.upto("Bi0")
                    bank = B.wait(act, f"Bi{t}")
                    C.link(A(bi[:, t, :], bank[:, :], ACT.Copy), S["bi_ready"])
                    B.release(act, f"Bi{t}")
                for k in range(1, LEVELS + 1):
                    if k < LEVELS:
                        level(0, k)
                    if k == 2:
                        take_raw("Cqi", 4, 2)
                        act.wait_ge(S["hcol_in"], 1)
                        C.link(A(lbc, lbc, ACT.Exp), S["hcol_out"])
                    elif k == 3:
                        take_raw("Cki", 6, 1)
                        act.wait_ge(S["hcol_in"], 2)
                        C.link(A(lnA, lnA, ACT.Ln))
                        C.link(A(ln1m, ln1m, ACT.Ln), S["hcol_out"])
                    elif k == 4:
                        act.wait_ge(S["ls_in"], 1)
                        C.link(A(hE, bf, ACT.Abs))
                        C.link(A(hE, hE, ACT.Exp, scale=-1.0))
                        C.link(A(hE, hE, ACT.Ln, bias=1.0), S["ls_out"])
                    elif k == 5:
                        act.wait_ge(S["lse_in"], 1)
                        C.link(A(hks, hks, ACT.Exp))
                        C.link(A(hE, hE, ACT.Abs))
                        C.link(A(hE, hE, ACT.Exp, scale=-1.0))
                        C.link(A(hE, hE, ACT.Ln, bias=1.0), S["lse_out"])
                    elif k == 6:
                        act.wait_ge(S["cum_b"], 1)
                        b8 = v3(hb, 8)
                        for hd in range(4):
                            C.link(A(v3(hke, 4)[:, hd, :], b8[:, 2 * hd, :], ACT.Exp, scale=-1.0, bias=b8[:, 2 * hd, P - 1:P]))
                        C.link(A(v3(hqe, 4), b8[:, 1:8:2, :], ACT.Exp), S["d_exp"])
                    elif k == LEVELS:
                        bank = B.wait(act, "HT")
                        C.link(A(ketm, bank[:, :], ACT.Copy), S["ketm_ready"])
                        B.release(act, "HT")
                    if k <= 3:
                        hi.upto(("Cqi", "Cki", "Cv")[k - 1])
                solve(0)
                bank = B.wait(act, "HS")
                C.link(A(hst.rearrange("p (a t) -> p a t", a=4), v3(bank[:, :], 4), ACT.Copy), S["hstate_ready"])
                B.release(act, "HS")
                def softmax(i):
                    b, tt, heads = ATT1[i]
                    w = (tt + 1) * P
                    act.wait_ge(S["probs_in"], i + 1)
                    for j in range(len(heads)):
                        C.link(A(lg[i % 2][:, j * w:(j + 1) * w], lg[i % 2][:, j * w:(j + 1) * w], ACT.Exp,
                                 bias=nmax[:, j:j + 1], accum_out=ssum[:, j:j + 1]))
                    act.sem_inc(S["logits_ready"], 1)

                def take_turned(i):
                    b, tt, heads = ATT1[i]
                    n = len(heads) * (tt + 1) * P
                    bank = B.wait(act, f"CP{b}")
                    C.link(A(pT[:, 0:n], bank[:, 0:n], ACT.Copy), S["pt_ready"])
                    B.release(act, f"CP{b}")

                for i in range(LEVELS - 1):
                    level(1, i + 1)
                    if i > 1:
                        take_values(i - 2)
                    pair_decays(i)
                    softmax(i)
                    if i:
                        take_turned(i - 1)
                take_values(len(ATT1) - 2)
                take_turned(len(ATT1) - 1)
                take_values(len(ATT1) - 1)
                pair_decays(LEVELS - 1)
                solve(1)
                for c in range(2):
                    bank = B.wait(act, f"HO{c}")
                    C.link(A(v3(yb, 4)[:, :, c * P:(c + 1) * P], v3(bank[:, :], 4), ACT.Copy))
                    C.link(A(v3(hE, 4)[:, :, c * P:(c + 1) * P], v3(bank[:, :], 4), ACT.Square), S["hosq_ready"])
                    B.release(act, f"HO{c}")
                rstd(C, B, ["HN0", "HN1"], hE, 1.0 / 128)
                act.wait_ge(S["fresh_norm"], 1)
                C.link(A(ysq, ya, ACT.Square), S["gsq_ready"])
                rstd(C, B, ["GV0", "GV1"], ysq, 1.0 / 64, "gn_eps")
                for i in range(12):
                    n = f"G{i % 4}{BRANCHES[i // 4]}"
                    hi.upto(n)
                    bank = B.wait(act, n)
                    if i == 0:
                        act.wait_ge(S["yc_split"], 1)
                    if i >= 2:
                        act.wait_ge(S["gate_used"], i - 1)
                    C.link(A(gate_buf[i % 2], bank[:, :], ACT.Sigmoid), S["gate_ready"])
                    B.release(act, n)
                nc.scalar.preload_act_table_set(LN_EXP)
                for j in range(4):
                    hi.upto(f"WO{j}")
                norm_squares(C, True)
                rstd(C, B, ["norm2"], tmp, 1.0 / D, width=T)
                for i in range(23):
                    if i < 22:
                        hi.upto(f"U{i}")
                        bank = B.wait(act, f"U{i}")
                        if i >= 4:
                            act.wait_ge(S["hidden_ready"], i - 3)
                        for j, t in ((0, i), (1, 22 + i)):
                            C.link(A(cb[i % 4][:, j, :], bank[:, j * T:(j + 1) * T], ACT.Identity,
                                     scale=PAR1.of(par, "conv_w2")[:, t:t + 1], bias=PAR1.of(par, "conv_b")[:, t:t + 1]))
                        act.sem_inc(S["conv_in"], 1)
                    if i:
                        act.wait_ge(S["conv_mid"], i)
                        C.link(A(cb[(i - 1) % 4][:, 0, :], cb[(i - 1) % 4][:, 0, :], ACT.Silu), S["conv_out"])
                for j in range(4):
                    hi.upto(f"D{j}")
                hi.upto("end")
                layer_end(act, l, False)

            C, B = Chain(act, S["act_chain"]), b2
            act.dma_start(t512.bitcast(I32)[0:1, T:2 * T], pos_in).then_inc(inputs_in, 16)
            norm_squares(C)
            rstd(C, B, ["norm"], tmp, 1.0 / D, width=T)
            for i in range(4):
                act.wait_ge(S["cum_ready"], i + 1)
                C.link(A(tabs[i], tabs[i], ACT.Sin), S["decay_ready"])
            layer_end(act, layers[0], False)

            if not layers[1]:
                act.dma_start(out, h[:]).then_inc(stored, 16)
                act.wait_ge(stored, 16)
                return
            with act.Fori(0, layers[1]) as l:
                C, B = Chain(act, S["act_chain"]), b2
                hi = HiParts(ends2, l * PIECES2 + layers[0] * PIECES1, l * (CH2 // RING) + layers[0] * (CH1 // RING))
                hi.upto("start")
                act.dma_start(par[:, 0:PAR2.size], params2[bass.ds(l, 1)].rearrange("a p n -> p (a n)")).then_inc(params_in, 16)
                norm_squares(C)
                rstd(C, B, ["norm"], dn, 1.0 / D, width=T)
                act.wait_ge(params_in, (l + (layers[0] + 1)) * 16)
                cw = v3(PAR2.of(par, "conv_w"), 4)
                for i in range(4):
                    hi.upto(f"qk{i // 2}")
                    bank = B.wait(act, f"qk{i // 2}")
                    C.link(A(qkraw[:, i, :], bank[:, i % 2 * T:(i % 2 + 1) * T], ACT.Identity, scale=cw[:, 3, i:i + 1],
                             bias=PAR2.of(par, "conv_b")[:, i:i + 1]), S["conv_in"])
                for t in range(NT):
                    hi.upto("mv0")
                    bank = B.wait(act, f"mv{t}")
                    C.link(A(mvt[:, t, :], bank[:, :], ACT.Copy), S["v_ready"])
                    B.release(act, f"mv{t}")
                for i in range(4):
                    act.wait_ge(S["conv_mid"], i + 1)
                    C.link(A(qkraw[:, i, :], qkraw[:, i, :], ACT.Silu), S["conv_out"])
                for g in range(2):
                    hi.upto(f"mo{g}")
                    bank = B.wait(act, f"mo{g}")
                    C.link(A(mo[:, 2 * g:2 * g + 2, :].rearrange("p a t -> p (a t)"), bank[:, :], ACT.Sigmoid), S["bsg_ready"])
                    B.release(act, f"mo{g}")
                hi.upto("if")
                act.wait_ge(S["ls_in"], 1)
                fz = ifr[0:4, 4 * T:5 * T]
                C.link(A(fz, fz, ACT.Abs))
                C.link(A(fz, fz, ACT.Exp, scale=-1.0))
                C.link(A(fz, fz, ACT.Ln, bias=1.0), S["hcol_out"])
                for n, o, w in (("aq", aqk[:, 0:2, :], 2), ("ak", aqk[:, 2:4, :], 2)):
                    hi.upto(n)
                    bank = B.wait(act, n)
                    C.link(A(o.rearrange("p a t -> p (a t)"), bank[:, :], ACT.Copy), S["raw_ready"])
                    B.release(act, n)
                hi.upto("av")
                bank = B.wait(act, "av")
                C.link(A(avt.rearrange("p a t -> p (a t)"), bank[:, :], ACT.Copy))
                B.release(act, "av")
                for n, o, w in (("cq0", 0, 2), ("cq1", 2, 1), ("ckv", 3, 2)):
                    hi.upto(n)
                    bank = B.wait(act, n)
                    C.link(A(cqk[:, o:o + w, :].rearrange("p a t -> p (a t)"), bank[:, 0:w * T], ACT.Copy))
                    B.release(act, n)
                hi.upto("kpe")
                bank = B.wait(act, "kpe")
                C.link(A(kpe[64:96, :], bank[64:96, 0:T], ACT.Copy), S["raw_ready"])
                B.release(act, "kpe")
                for hd in range(4):
                    bank = B.wait(act, f"gb{hd}")
                    if hd:
                        act.wait_ge(S["dn_ready"], hd)
                    C.link(A(em, bank[:, T:2 * T], ACT.Exp), S["em_ready"])
                    act.wait_ge(S["pairs_in"], hd + 1)
                    C.link(A(dT, dT, ACT.Exp, scale=-1.0), S["d_exp"])
                act.wait_ge(S["dn_ready"], 4)
                C.link(A(sqb, mix[:, 0:4, :].rearrange("p a t -> p (a t)"), ACT.Square), S["hosq_ready"])
                rstd(C, B, ["mn0", "mn1"], sqb, 1.0 / 128)
                act.wait_ge(S["yb_ready"], 1)
                C.link(A(sqb, aqk[:, :, :].rearrange("p a t -> p (a t)"), ACT.Square), S["kksq_ready"])
                rstd(C, B, ["nq", "nk"], sqb, 1.0 / 64)

                def take_heads(o):
                    def take(tt, bank):
                        C.link(A(mix[:, o:o + 2, tt * P:(tt + 1) * P], v3(bank[:, 0:2 * P], 2), ACT.Copy))
                        C.link(A(v3(sqb, 4)[:, 0:2, tt * P:(tt + 1) * P], v3(bank[:, 0:2 * P], 2), ACT.Square), S["gsq_ready"])
                    return take

                attention(C, B, "B", ATT2, 0, lg2, pT2, take_heads(4))
                rstd(C, B, ["bn"], sqb, 1.0 / 64)
                C.link(A(sq2[:, 0:5, :].rearrange("p a t -> p (a t)"), cqk[:, :, :].rearrange("p a t -> p (a t)"), ACT.Square), S["latents_sq"])
                rstd(C, B, ["ncq", "nckv"], t512, (1.0 / 384, 1.0 / 256), width=T)
                for n, o in (("uq", 0), ("uk", 4)):
                    rows = MLA_D if n == "uq" else 64
                    for g in range(2):
                        hi.upto(f"{n}{g}")
                        bank = B.wait(act, f"{n}{g}")
                        C.link(A(lqk[0:rows, o + 2 * g:o + 2 * g + 2, :].rearrange("p a t -> p (a t)"), bank[0:rows, :], ACT.Copy))
                        B.release(act, f"{n}{g}")
                C.link(A(lqk[64:96, 4:8, :], spread(kpe, 4)[64:96], ACT.Copy))
                hi.upto("uv")
                bank = B.wait(act, "uv")
                C.link(A(lvt.rearrange("p a t -> p (a t)"), bank[:, :], ACT.Copy))
                B.release(act, "uv")
                C.link(A(sq2[0:MLA_D].rearrange("p a t -> p (a t)"), lqk[0:MLA_D].rearrange("p a t -> p (a t)"), ACT.Square), S["lse_in"])
                rstd(C, B, ["nlq0", "nlq1", "nlk0", "nlk1"], sq2.rearrange("p a t -> p (a t)"), 1.0 / MLA_D, rows=MLA_D)
                attention(C, B, "M", ATT2, len(ATT2), lg2, pT2, take_heads(6))
                rstd(C, B, ["ln"], sqb, 1.0 / 64)
                for j in range(4):
                    hi.upto(f"WO{j}")
                norm_squares(C, True)
                rstd(C, B, ["norm2"], dn, 1.0 / D, width=T)
                for i in range(16):
                    hi.upto(f"U{i}")
                    bank = B.wait(act, f"U{i}")
                    C.link(A(hidden[:, 2 * i:2 * i + 2, :].rearrange("p a t -> p (a t)"), bank[:, :], ACT.Relu), S["conv_in"])
                    B.release(act, f"U{i}")
                for j in range(4):
                    hi.upto(f"D{j}")
                hi.upto("end")
                layer_end(act, l + (layers[0] + 1), False)
            act.dma_start(out, h[:]).then_inc(stored, 16)
            act.wait_ge(stored, 16)

        @block.vector
        def _(dve):
            V = nc.vector

            def split(C, x_, hi, lo, sig=None):
                C.link(V.tensor_copy(hi, x_))
                C.link(V.tensor_tensor(lo, x_, hi.bitcast(F32), ALU.subtract), sig)

            def norm(C, gain, dst, n, buf, hi=None):
                dve.wait_ge(S["rstd_out"], n)
                for k in range(KD):
                    C.link(V.scalar_tensor_tensor(dst[:, k, :], h[:, k, :], gain[:, k:k + 1], buf, ALU.mult, ALU.mult))
                    if hi is not None and k % 2:
                        split(C, dst[:, k - 1:k + 1, :], hi[:, k - 1:k + 1, :], u_lo[:, k - 1:k + 1, :], S["u_ready"])

            def rope(C, B, name, x_, n, cos, sin, t, rows=P):
                bank = B.wait(dve, name)
                C.link(V.tensor_tensor(t, v3(bank[0:rows, 0:n * T], n), spread(sin, n), ALU.mult))
                B.release(dve, name)
                C.link(V.tensor_tensor(x_, x_, spread(cos, n), ALU.mult))
                C.link(V.tensor_tensor(x_, x_, t, ALU.add))

            def attention(C, B, tag, batches, base, scale, mask, lgs):
                for i, (b, tt, heads) in enumerate(batches):
                    w, n = (tt + 1) * P, len(heads)
                    bank = B.wait(dve, f"{tag}L{b}")
                    if i >= 2:
                        B.wait(dve, f"{tag}P{batches[i - 2][0]}")
                    x_ = v3(lgs[i % 2][:, 0:n * w], n)
                    C.link(V.scalar_tensor_tensor(x_, v3(bank[:, 0:n * w], n), scale, spread(mask(tt), n), ALU.mult, ALU.add))
                    B.release(dve, f"{tag}L{b}")
                    C.link(V.tensor_reduce(nmax[:, 0:n], x_, AX_X, ALU.max, negate=True), S["probs_in"])
                    dve.wait_ge(S["logits_ready"], base + i + 1)
                    C.link(V.reciprocal(ssum[:, 0:n], ssum[:, 0:n]))
                    C.link(V.tensor_tensor(x_, x_, along(ssum[:, 0:n], w), ALU.mult), S["probs_ready"])

            dve.wait_ge(inputs_in, 48)
            C = Chain(dve, ready)
            C.link(V.tensor_copy(msk[:], mask_in))
            with dve.Fori(0, layers[0]) as l:
                C, B = Chain(dve, S["dve_chain"]), b1
                dve.wait_ge(params_in, (l + 1) * 16)
                p = lambda n: PAR1.of(par, n)
                C.link(V.tensor_scalar(omu, p("mu"), -1.0, 1.0, ALU.mult, ALU.add))
                C.link(V.memset(pmu[:, :, 0:1], 0.0), S["pmu_used"])
                C.link(V.memset(cc[:, :, 0:1], 0.0))
                norm(C, p("g_mix"), u, 1, tw, u_hi)
                for i in range(14):
                    dve.wait_ge(S["pmu_ready"], 2 * (i // 2) + 2)
                    bank = B.wait(dve, f"A{i // 2}")
                    C.link(V.scalar_tensor_tensor(pa[:, i, :], bank[:, i % 2 * T:(i % 2 + 1) * T], omu[:, i:i + 1],
                                                  pmu[:, i % 4, 0:T], ALU.mult, ALU.add), S["pmu_used"])
                    if i % 2:
                        B.release(dve, f"A{i // 2}")
                for j in range(4):
                    C.link(V.tensor_scalar(v3(kk, 4)[:, j, :], pa[:, 4 + j, :], p("k_k")[:, j:j + 1], None, ALU.mult))
                dve.sem_inc(S["kk_ready"], 1)
                dve.wait_ge(S["squash_ready"], 4)
                for i in range(8):
                    C.link(V.tensor_tensor_scan(cc[:, i, 1:P + 1], ones, v3(einv, 8)[:, i, :], 0.0, ALU.mult, ALU.add))
                C.link(V.tensor_copy(mid, cc[:, :, 64]))
                C.link(V.tensor_tensor(cc, cc, along(mid, P + 1), ALU.subtract), S["cum_ready"])
                dve.wait_ge(S["squash_ready"], 8)
                for j in range(4):
                    C.link(V.tensor_scalar(v3(kmod, 4)[:, j, :], v3(av, 4)[:, j, :], -1.0, p("k_a")[:, j:j + 1], ALU.add, ALU.mult))
                k_flat = pa[:, 4:8, :].rearrange("p a t -> p (a t)")
                C.link(V.scalar_tensor_tensor(kmod, kmod, 1.0, k_flat, ALU.add, ALU.mult))
                for g in range(2):
                    B.wait(dve, f"KK{g}")
                for g in range(2):
                    bank = B.wait(dve, f"KK{g}")
                    C.link(V.tensor_scalar(bonus[:, g * 512:(g + 1) * 512], bank[:, :], 1e-24, None, ALU.max))
                    B.release(dve, f"KK{g}")
                dve.sem_inc(S["rstd_in"], 1)
                dve.wait_ge(S["rstd_out"], 2)
                C.link(V.tensor_tensor(kk, kk, bonus, ALU.mult))
                for j in range(4):
                    C.link(V.scalar_tensor_tensor(v3(bonus, 4)[:, j, :], pa[:, j, :], p("r_k")[:, j:j + 1],
                                                  v3(kmod, 4)[:, j, :], ALU.mult, ALU.mult))
                dve.sem_inc(S["bonus_in"], 1)
                dve.wait_ge(S["decay_ready"], 1)
                C.link(V.scalar_tensor_tensor(ar[:, :, 0, :], v3(kk, 8), -1.0, ar[:, :, 0, :], ALU.mult, ALU.mult))
                r8 = pa[:, 0:4, :].rearrange("p a (c t) -> p (a c) t", c=2)
                C.link(V.tensor_tensor(ar[:, :, 1, :], r8, ar[:, :, 1, :], ALU.mult))
                C.link(V.tensor_tensor(av, av, kk, ALU.mult))
                C.link(V.tensor_tensor(av, av, einv, ALU.mult))
                C.link(V.tensor_tensor(einv, einv, kmod, ALU.mult), S["rwkv_ops_ready"])
                for g in range(2):
                    bank = B.wait(dve, f"Bf{g}")
                    C.link(V.tensor_copy(bf[:, g * 512:(g + 1) * 512], bank[:, :]))
                    B.release(dve, f"Bf{g}")
                for g in range(2):
                    B.wait(dve, f"BON{g}")
                for g in range(2):
                    bank = B.wait(dve, f"BON{g}")
                    vv = pa[:, 8 + 2 * g:10 + 2 * g, :].rearrange("p a t -> p (a t)")
                    C.link(V.tensor_tensor(bonus[:, g * 512:(g + 1) * 512], bank[:, :], vv, ALU.mult))
                    B.release(dve, f"BON{g}")
                def scores(c):
                    if c:
                        B.wait(dve, "ST")
                    for hd in range(8):
                        bank = B.wait(dve, f"S{c}{hd}")
                        C.link(V.tensor_tensor(sc[:, hd].rearrange("p (b a) t -> p b (a t)", b=2), v3(bank[:, :], 2), spread(K("pairmask"), 2), ALU.mult))
                        B.release(dve, f"S{c}{hd}")
                    for q in range(2):
                        bank = B.wait(dve, f"N{c}{q}")
                        C.link(V.tensor_tensor(nn[:, 4 * q:4 * q + 4, :], v3(bank[:, :], 4), spread(K("lower"), 4), ALU.mult))
                        B.release(dve, f"N{c}{q}")
                    for q in range(2):
                        hs = slice(4 * q, 4 * q + 4)
                        for o, m, s_ in ((xx, upm, sc[:, q:8:2, 0, :]), (zz, lowm, nn[:, hs, :])):
                            C.link(V.tensor_copy(o[:, hs, :], spread(ident, 4)))
                            C.link(V.copy_predicated(o[:, hs, :], spread(m[:, 0, :], 4), s_))
                        dve.sem_inc(S["xz_ready"], 1)

                def level(c, k, q):
                    hs = slice(4 * q, 4 * q + 4)
                    if k < LEVELS - 1:
                        B.wait(dve, f"Z{c}{k}{q}")
                    for n, o, m in (("X", xx, upm), ("Z", zz, lowm)):
                        if n == "Z" and k == LEVELS - 1:
                            continue
                        bank = B.wait(dve, f"{n}{c}{k}{q}")
                        C.link(V.copy_predicated(o[:, hs, :], spread(m[:, k, :], 4), v3(bank[:, :], 4)))
                        B.release(dve, f"{n}{c}{k}{q}")
                    dve.sem_inc(S["xz_ready"], 1)

                def state():
                    bank = B.wait(dve, "ST")
                    e8 = eend.rearrange("p (j c) -> p j c", c=2)
                    m8_ = emid.rearrange("p (j c) -> p j c", c=2)
                    C.link(V.memset(st, 0.0))
                    for j in range(4):
                        for r in (0, 64):
                            C.link(V.tensor_scalar(st[r:r + 64, j, r:r + 64], bank[r:r + 64, j * 64:(j + 1) * 64],
                                                   e8[r:r + 64, j, 0:1], m8_[r:r + 64, j, 1:2], ALU.mult, ALU.mult))
                    dve.sem_inc(S["state_ready"], 1)
                    B.release(dve, "ST")

                def halves(ap, m):
                    return ap.rearrange("p (n a t) -> p n a t", a=2, t=m)

                def pair_decays(k):
                    m = 1 << k
                    b_, e_ = halves(hb, m), halves(hE, m)
                    ref = b_[:, :, 0, m - 1:m].to_broadcast([P, 1024 // (2 * m), m])
                    C.link(V.tensor_tensor(e_[:, :, 0, :], ref, b_[:, :, 0, :], ALU.subtract))
                    C.link(V.tensor_tensor(e_[:, :, 1, :], b_[:, :, 1, :], ref, ALU.subtract), S["pairs_in"])

                def pair_operands(k):
                    m = 1 << k
                    e_, o_ = halves(hE, m), halves(hqk, m)
                    dve.wait_ge(S["d_exp"], k + 2)
                    C.link(V.tensor_tensor(o_[:, :, 0, :], halves(hks, m)[:, :, 0, :], e_[:, :, 0, :], ALU.mult))
                    C.link(V.tensor_tensor(o_[:, :, 1, :], halves(bq, m)[:, :, 1, :], e_[:, :, 1, :], ALU.mult), S["pairs_ready"])

                def take_pairs(k):
                    for c in range(2):
                        bank = B.wait(dve, f"H{k}{c}")
                        m = upm[:, k, :] if k < LEVELS else diagm
                        C.link(V.copy_predicated(v3(hsc, 8)[:, c:8:2, :], spread(m, 4), v3(bank[:, :], 4)))
                        B.release(dve, f"H{k}{c}")

                def rotate_all():
                    cos, sin = K("cos"), K("sin")
                    rope(C, B, "Rq0", craw[:, 0:2, :], 2, cos, sin, scr)
                    rope(C, B, "Rq1", craw[:, 2:4, :], 2, cos, sin, scr)
                    rope(C, B, "Rk", craw[:, 7:9, :], 2, cos, sin, scr)
                    rope(C, B, "Rqi", craw[:, 4:6, :], 2, cos, sin, scr)
                    rope(C, B, "Rki", craw[:, 6:7, :], 1, cos, sin, scr[:, 0:1, :])
                    dve.sem_inc(S["rope_ready"], 1)

                def index_scores(tt):
                    w = (tt + 1) * P
                    for n, _, heads in INDEX[2 * tt:2 * tt + 2]:
                        bank = B.wait(dve, n)
                        for i, hd in enumerate(heads):
                            o = scr[:, tt, 0:w] if hd == 0 else tmp[:, 0:w]
                            C.link(V.tensor_scalar(o, bank[:, i * w:(i + 1) * w], 0.0, wi[:, 4 * tt + hd:4 * tt + hd + 1], ALU.max, ALU.mult))
                            if hd:
                                C.link(V.tensor_tensor(scr[:, tt, 0:w], scr[:, tt, 0:w], o, ALU.add))
                        B.release(dve, n)
                    C.link(V.tensor_tensor(work[tt][:, 0:w], scr[:, tt, 0:w], K("cneg")[:, T - w:T], ALU.add))

                def take_best(tt, rounds):
                    w = (tt + 1) * P
                    for _ in range(rounds):
                        C.link(V.max(m8, work[tt][:, 0:w]))
                        C.link(V.match_replace(work[tt][:, 0:w], m8, work[tt][:, 0:w], TAKEN))

                def best_mask(tt):
                    w = (tt + 1) * P
                    C.link(V.tensor_scalar(amask[:, tt, 0:w], work[tt][:, 0:w], 2 * NEG, None, ALU.is_le))
                    C.link(V.tensor_scalar(amask[:, tt, 0:w], amask[:, tt, 0:w], -1.0, -NEG, ALU.add, ALU.mult))
                    C.link(V.tensor_tensor(amask[:, tt, 0:w], amask[:, tt, 0:w], K("cneg")[:, T - w:T], ALU.min))

                def masked_logits(i):
                    b, tt, heads = ATT1[i]
                    w, n = (tt + 1) * P, len(heads)
                    bank = B.wait(dve, f"CL{b}")
                    if i >= 2:
                        B.wait(dve, f"CP{ATT1[i - 2][0]}")
                    x_ = v3(lg[i % 2][:, 0:n * w], n)
                    C.link(V.scalar_tensor_tensor(x_, v3(bank[:, 0:n * w], n), 0.125, spread(amask[:, tt, 0:w], n), ALU.mult, ALU.add))
                    B.release(dve, f"CL{b}")
                    C.link(V.tensor_reduce(nmax[:, 0:n], x_, AX_X, ALU.max, negate=True), S["probs_in"])

                def probabilities(i):
                    b, tt, heads = ATT1[i]
                    w, n = (tt + 1) * P, len(heads)
                    dve.wait_ge(S["logits_ready"], i + 1)
                    C.link(V.reciprocal(ssum[:, 0:n], ssum[:, 0:n]))
                    x_ = v3(lg[i % 2][:, 0:n * w], n)
                    C.link(V.tensor_tensor(x_, x_, along(ssum[:, 0:n], w), ALU.mult), S["probs_ready"])

                scores(0)
                for k in range(1, LEVELS):
                    level(0, k, 0)
                    level(0, k, 1)
                    if k == 1:
                        C.link(V.tensor_tensor(lbc, p("lb0"), p("lb1"), ALU.subtract), S["hcol_in"])
                    elif k == 2:
                        dve.wait_ge(S["hcol_out"], 1)
                        C.link(V.tensor_scalar(lbc, lbc, 1e30, 1.0, ALU.min, ALU.add))
                        C.link(V.reciprocal(lbc, lbc))
                        C.link(V.tensor_tensor(lbc, lbc, p("not_first"), ALU.mult))
                        C.link(V.tensor_scalar(isz, lbc, 0.0, NEG, ALU.is_le, ALU.mult))
                        C.link(V.tensor_scalar(omlb, lbc, -1.0, 1.0, ALU.mult, ALU.add))
                        C.link(V.tensor_scalar(lnA, lbc, 2.0 ** -64, None, ALU.max))
                        C.link(V.tensor_scalar(ln1m, omlb, 2.0 ** -64, None, ALU.max), S["hcol_in"])
                    elif k == 3:
                        dve.wait_ge(S["hcol_out"], 2)
                        C.link(V.tensor_tensor(lnA, lnA, isz, ALU.add))
                        C.link(V.tensor_scalar(hls, bf, 0.0, None, ALU.min), S["ls_in"])
                        bank = B.wait(dve, "Cv")
                        both = v3(bank[:, 0:2 * (P + 4)], 2)
                        C.link(V.tensor_copy(cvt, both[:, :, 0:P]))
                        C.link(V.tensor_scalar(v3(wi, 2), both[:, :, P:P + 4], 1.0 / 16, None, ALU.mult))
                        B.release(dve, "Cv")
                    elif k == 4:
                        dve.wait_ge(S["ls_out"], 1)
                        C.link(V.tensor_tensor(hls, hls, hE, ALU.subtract))
                        C.link(V.tensor_tensor(hks, hls, bf, ALU.subtract))
                        for j in range(4):
                            s_ = v3(hls, 4)[:, j, :]
                            C.link(V.tensor_scalar(v3(hE, 4)[:, j, :], s_, ln1m[:, j:j + 1], lnA[:, j:j + 1], ALU.add, ALU.subtract))
                            C.link(V.tensor_scalar(s_, s_, ln1m[:, j:j + 1], lnA[:, j:j + 1], ALU.add, ALU.max))
                        dve.sem_inc(S["lse_in"], 1)
                        rotate_all()
                    elif k == 5:
                        dve.wait_ge(S["lse_out"], 1)
                        C.link(V.tensor_tensor(hls, hls, hE, ALU.add))
                        for j in range(4):
                            C.link(V.tensor_scalar(v3(hks, 4)[:, j, :], v3(hks, 4)[:, j, :], omlb[:, j:j + 1], None, ALU.mult))
                        for i in range(8):
                            C.link(V.tensor_tensor_scan(v3(hb, 8)[:, i, :], ones, v3(hls, 8)[:, i, :], 0.0, ALU.mult, ALU.add))
                        dve.sem_inc(S["cum_b"], 1)
                    else:
                        dve.wait_ge(S["d_exp"], 1)
                        C.link(V.tensor_tensor(v3(hke, 4), v3(hke, 4), v3(hks, 8)[:, 0:8:2, :], ALU.mult), S["hk_ready"])
                        C.link(V.tensor_tensor(v3(hqe, 4), v3(hqe, 4), v3(bq, 8)[:, 1:8:2, :], ALU.mult), S["hqe_ready"])
                        C.link(V.memset(hsc, 0.0))
                for tt in range(NT):
                    index_scores(tt)
                take_best(0, TOPK // TOP_STEP)
                best_mask(0)
                state()
                scores(1)
                half_rounds = TOPK // TOP_STEP // 2
                for k in range(1, LEVELS):
                    i = k - 1
                    pair_decays(i)
                    masked_logits(i)
                    level(1, k, 0)
                    level(1, k, 1)
                    if i:
                        take_pairs(i - 1)
                    pair_operands(i)
                    probabilities(i)
                    if k <= 2:
                        take_best(1, half_rounds)
                    if k == 2:
                        best_mask(1)
                take_pairs(LEVELS - 2)
                pair_decays(LEVELS - 1)
                pair_operands(LEVELS - 1)
                dve.sem_inc(S["pairs_ready"], 1)
                take_pairs(LEVELS - 1)
                take_pairs(LEVELS)
                dve.sem_inc(S["hsc_ready"], 1)
                dve.wait_ge(S["yc_ready"], len(ATT1))
                split(C, yc, yc_hi, yc_lo, S["yc_split"])
                for g in range(2):
                    B.wait(dve, f"GM{g}")
                for g in range(2):
                    bank = B.wait(dve, f"GM{g}")
                    y_ = ya[:, g * 512:(g + 1) * 512]
                    C.link(V.scalar_tensor_tensor(y_, bank[:, :], -1.0 / 64, y_, ALU.mult, ALU.add))
                    B.release(dve, f"GM{g}")
                dve.sem_inc(S["fresh_norm"], 1)
                dve.wait_ge(S["rstd_out"], 3)
                C.link(V.tensor_tensor(yb, yb, hE, ALU.mult))
                dve.wait_ge(S["bsg_ready"], 2)
                for j in range(4):
                    C.link(V.scalar_tensor_tensor(v3(yb, 4)[:, j, :], v3(yb, 4)[:, j, :], p("b_gn")[:, j:j + 1], v3(bsg, 4)[:, j, :], ALU.mult, ALU.mult))
                split(C, yb, yb_hi, yb_lo, S["yb_ready"])
                dve.wait_ge(S["rstd_out"], 4)
                C.link(V.tensor_tensor(ya, ya, ysq, ALU.mult))
                for j in range(4):
                    C.link(V.tensor_scalar(v3(ya, 4)[:, j, :], v3(ya, 4)[:, j, :], p("gn_g")[:, j:j + 1], p("gn_b")[:, j:j + 1], ALU.mult, ALU.add))
                C.link(V.tensor_tensor(ya, ya, bonus, ALU.add))
                dve.wait_ge(S["gA_ready"], 2)
                C.link(V.tensor_tensor(ya, ya, gA, ALU.mult))
                split(C, ya, ya_hi, ya_lo, S["ya_ready"])
                for i in range(12):
                    first, last = i < 4, i >= 8
                    j, n = i % 4, BRANCHES[i // 4]
                    bank = B.wait(dve, f"M{j}{n}")
                    dve.wait_ge(S["gate_ready"], i + 1)
                    o = merged[:, j * 512:(j + 1) * 512]
                    C.link(V.tensor_tensor(o if first else mtmp, bank[:, :], gate_buf[i % 2], ALU.mult), S["gate_used"])
                    B.release(dve, f"M{j}{n}")
                    if not first:
                        C.link(V.tensor_tensor(o, o, mtmp, ALU.add))
                    if last:
                        split(C, o, merged_hi[:, j * 512:(j + 1) * 512], merged_lo[:, j * 512:(j + 1) * 512], S["merged_ready"])
                for j in range(4):
                    bank = B.wait(dve, f"WO{j}")
                    o = h[:, 2 * j:2 * j + 2, :].rearrange("p a t -> p (a t)")
                    C.link(V.tensor_tensor(o, o, bank[:, :], ALU.add), S["h_ready"])
                    B.release(dve, f"WO{j}")
                norm(C, p("g_ffn"), u, 5, tmp[:, 0:T], u_hi)
                for i in range(23):
                    if i < 22:
                        bank = B.wait(dve, f"U{i}")
                        dve.wait_ge(S["conv_in"], i + 1)
                        for j, t in ((0, i), (1, 22 + i)):
                            c_ = cb[i % 4][:, j, :]
                            x_ = bank[:, j * T:(j + 1) * T]
                            C.link(V.scalar_tensor_tensor(c_[:, 1:], x_[:, 0:T - 1], p("conv_w1")[:, t:t + 1], c_[:, 1:], ALU.mult, ALU.add))
                            C.link(V.scalar_tensor_tensor(c_[:, 2:], x_[:, 0:T - 2], p("conv_w0")[:, t:t + 1], c_[:, 2:], ALU.mult, ALU.add),
                                   S["conv_mid"] if j else None)
                        B.release(dve, f"U{i}")
                    if i:
                        dve.wait_ge(S["conv_out"], i)
                        c_ = cb[(i - 1) % 4]
                        C.link(V.tensor_tensor(hidden[:, i - 1, :], c_[:, 0, :], c_[:, 1, :], ALU.mult))
                        split(C, hidden[:, i - 1, :], hidden_hi[:, i - 1, :], hidden_lo[:, i - 1, :], S["hidden_ready"])
                for j in range(4):
                    bank = B.wait(dve, f"D{j}")
                    o = h[:, 2 * j:2 * j + 2, :].rearrange("p a t -> p (a t)")
                    C.link(V.tensor_tensor(o, o, bank[:, :], ALU.add))
                    B.release(dve, f"D{j}")
                layer_end(dve, l, True)

            C, B = Chain(dve, S["dve_chain"]), b2
            norm(C, PAR1.of(par, "g_final"), h, 1, tmp[:, 0:T])
            dve.wait_ge(inputs_in, 64)
            C.link(V.tensor_copy(t512[0:1, 0:T], t512.bitcast(I32)[0:1, T:2 * T]), S["ready"])
            dve.wait_ge(bank_full[1], 1)
            two_pi = 2.0 * np.pi
            hi = float(np.float32(6.28125))
            lo = float(np.float32(two_pi - 6.28125))
            rest = float(two_pi - 6.28125 - np.float64(np.float32(two_pi - 6.28125)))
            for i in range(4):
                ang, tn = tabs[i], em
                C.link(V.tensor_scalar(ang, banks[1][:, 0:T], K("freq")[:, i // 2:i // 2 + 1], None, ALU.mult))
                shift = 0.25 if i % 2 == 0 else 0.0
                C.link(V.tensor_scalar(tn, ang, 1.0 / two_pi, shift, ALU.mult, ALU.add))
                C.link(V.tensor_scalar(tn, tn, 12582912.0, None, ALU.add))
                C.link(V.tensor_scalar(tn, tn, -12582912.0, None, ALU.add))
                for part_ in (hi, lo, rest):
                    C.link(V.scalar_tensor_tensor(ang, tn, -part_, ang, ALU.mult, ALU.add))
                if i % 2 == 0:
                    C.link(V.tensor_scalar(ang, ang, np.pi / 2, None, ALU.add))
                C.link(V.tensor_scalar(ang, ang, 3.1415925, -3.1415925, ALU.min, ALU.max), S["cum_ready"])
            dve.wait_ge(S["decay_ready"], 4)
            layer_end(dve, layers[0], True)

            if not layers[1]:
                return
            with dve.Fori(0, layers[1]) as l:
                C, B = Chain(dve, S["dve_chain"]), b2
                dve.wait_ge(params_in, (l + (layers[0] + 1)) * 16)
                p = lambda n: PAR2.of(par, n)
                norm(C, p("g_mix"), u, 1, dn, u_hi)
                cw = v3(p("conv_w"), 4)
                for i in range(4):
                    bank = B.wait(dve, f"qk{i // 2}")
                    dve.wait_ge(S["conv_in"], 2 * (i // 2) + 2)
                    x_ = bank[:, i % 2 * T:(i % 2 + 1) * T]
                    for d in (1, 2, 3):
                        o = qkraw[:, i, d:]
                        C.link(V.scalar_tensor_tensor(o, x_[:, 0:T - d], cw[:, 3 - d, i:i + 1], o, ALU.mult, ALU.add),
                               S["conv_mid"] if d == 3 else None)
                    if i % 2:
                        B.release(dve, f"qk{i // 2}")
                bank = B.wait(dve, "if")
                a_, f_, g_, e_, z_, w_ = (ifr[0:4, i * T:(i + 1) * T] for i in range(6))
                C.link(V.tensor_scalar(a_, bank[0:4, 0:T], p("b_i")[0:4], None, ALU.add))
                C.link(V.tensor_scalar(f_, bank[0:4, T:2 * T], p("b_f")[0:4], None, ALU.add))
                B.release(dve, "if")
                C.link(V.tensor_copy(z_, f_), S["ls_in"])
                C.link(V.tensor_scalar(f_, f_, 0.0, None, ALU.min))
                dve.wait_ge(S["hcol_out"], 1)
                C.link(V.tensor_tensor(f_, z_, f_, ALU.subtract))
                C.link(V.memset(w_, 1.0))
                C.link(V.tensor_tensor_scan(z_, w_, f_, 0.0, ALU.mult, ALU.add))
                C.link(V.tensor_tensor(a_, a_, z_, ALU.add))
                C.link(V.tensor_tensor_scan(g_, a_, a_, 0.0, ALU.max, ALU.max))
                C.link(V.tensor_tensor(e_, z_, g_, ALU.subtract), S["d_diff"])
                bank = B.wait(dve, "acol")
                C.link(V.tensor_copy(acol.rearrange("p a t -> p (a t)"), bank[:, 0:8]))
                B.release(dve, "acol")
                for hd in range(4):
                    bank = B.wait(dve, f"gb{hd}")
                    dve.wait_ge(S["em_ready"], hd + 1)
                    C.link(V.tensor_scalar(dT[:, 0:T], bank[:, 0:T], acol[:, 0, hd:hd + 1], 0.0, ALU.subtract, ALU.max))
                    C.link(V.tensor_scalar(dT[:, T:T + P], bank[:, P:T], acol[:, 1, hd:hd + 1], 0.0, ALU.subtract, ALU.max), S["pairs_in"])
                    dve.wait_ge(S["d_exp"], hd + 1)
                    B.release(dve, f"gb{hd}")
                    for o in (0, T):
                        C.link(V.tensor_tensor(dT[:, o:o + P], dT[:, o:o + P], K("pairmask")[:, P:2 * P], ALU.mult))
                    bank = B.wait(dve, f"sc{hd}")
                    if hd >= 2:
                        B.wait(dve, f"nd{hd - 2}")
                    C.link(V.scalar_tensor_tensor(sT[hd % 2], bank[:, 0:T + P], 0.125, dT, ALU.mult, ALU.mult), S["s_ready"])
                    B.release(dve, f"sc{hd}")
                    bank = B.wait(dve, f"nd{hd}")
                    C.link(V.tensor_tensor(dn, bank[:, T:2 * T], em, ALU.max))
                    C.link(V.scalar_tensor_tensor(dn, bank[:, T:2 * T], -1.0, dn, ALU.mult, ALU.max))
                    C.link(V.reciprocal(dn, dn))
                    C.link(V.tensor_tensor(mix[:, hd, :], bank[:, 0:T], dn, ALU.mult), S["dn_ready"])
                    B.release(dve, f"nd{hd}")
                dve.wait_ge(S["rstd_out"], 2)
                flat = mix[:, 0:4, :].rearrange("p a t -> p (a t)")
                C.link(V.tensor_tensor(flat, flat, sqb, ALU.mult))
                dve.wait_ge(S["bsg_ready"], 2)
                for hd in range(4):
                    C.link(V.scalar_tensor_tensor(mix[:, hd, :], mix[:, hd, :], p("g_mlstm")[:, hd:hd + 1], mo[:, hd, :], ALU.mult, ALU.mult))
                dve.sem_inc(S["yb_ready"], 1)
                dve.wait_ge(S["raw_ready"], 3)
                dve.wait_ge(S["rstd_out"], 3)
                for i, n in ((0, "g_mq"), (2, "g_mk")):
                    x_ = aqk[:, i:i + 2, :].rearrange("p a t -> p (a t)")
                    C.link(V.scalar_tensor_tensor(x_, x_, p(n), sqb[:, i * T:(i + 2) * T], ALU.mult, ALU.mult))
                dve.sem_inc(S["kk_ready"], 1)
                t2 = v3(t512, 2)
                for n in ("rq", "rk"):
                    B.wait(dve, n)
                rope(C, B, "rq", aqk[:, 0:2, :], 2, tabs[0], tabs[1], t2)
                rope(C, B, "rk", aqk[:, 2:4, :], 2, tabs[0], tabs[1], t2)
                dve.sem_inc(S["rope_ready"], 1)
                causal = lambda tt: K("cneg")[:, T - (tt + 1) * P:T]
                attention(C, B, "B", ATT2, 0, 0.125, causal, lg2)

                def head_norm(o, gain, n):
                    dve.wait_ge(S["rstd_out"], n)
                    for i in range(2):
                        C.link(V.scalar_tensor_tensor(mix[:, o + i, :], mix[:, o + i, :], p(gain)[:, i:i + 1], v3(sqb, 4)[:, i, :], ALU.mult, ALU.mult))

                head_norm(4, "g_mobaout", 4)
                dve.wait_ge(S["rstd_out"], 5)
                for i in range(5):
                    g_ = p("g_cq")[:, i:i + 1] if i < 3 else p("g_ckv")[:, i - 3:i - 2]
                    C.link(V.scalar_tensor_tensor(cqk[:, i, :], cqk[:, i, :], g_, t512[:, (i // 3) * T:(i // 3 + 1) * T], ALU.mult, ALU.mult))
                split(C, cqk, cqk_hi, cqk_lo, S["latents_ready"])
                s2f = sq2.rearrange("p a t -> p (a t)")
                dve.wait_ge(S["rstd_out"], 6)
                for i, n in ((0, "g_lq"), (4, "g_lk")):
                    x_ = lqk[0:MLA_D, i:i + 4, :].rearrange("p a t -> p (a t)")
                    C.link(V.scalar_tensor_tensor(x_, x_, p(n)[0:MLA_D], s2f[0:MLA_D, i * T:(i + 4) * T], ALU.mult, ALU.mult))
                dve.sem_inc(S["lse_out"], 1)
                for n in ("rlq0", "rlq1", "rlk0", "rlk1"):
                    B.wait(dve, n)
                for g, n in enumerate(("rlq0", "rlq1", "rlk0", "rlk1")):
                    rope(C, B, n, lqk[0:MLA_D, 2 * g:2 * g + 2, :], 2, tabs[2][0:MLA_D], tabs[3][0:MLA_D], t2[0:MLA_D], MLA_D)
                dve.sem_inc(S["rope_ready"], 1)
                attention(C, B, "M", ATT2, len(ATT2), float(MLA_D) ** -0.5, causal, lg2)
                head_norm(6, "g_mlaout", 7)
                split(C, mix, mix_hi, mix_lo, S["yc_ready"])
                for j in range(4):
                    bank = B.wait(dve, f"WO{j}")
                    o = h[:, 2 * j:2 * j + 2, :].rearrange("p a t -> p (a t)")
                    C.link(V.tensor_tensor(o, o, bank[:, :], ALU.add), S["h_ready"])
                    B.release(dve, f"WO{j}")
                norm(C, p("g_mlp"), u, 8, dn, u_hi)
                for i in range(16):
                    dve.wait_ge(S["conv_in"], 4 + i + 1)
                    x_ = hidden[:, 2 * i:2 * i + 2, :].rearrange("p a t -> p (a t)")
                    C.link(V.tensor_tensor(x_, x_, x_, ALU.mult))
                    split(C, x_, hidden_hi[:, 2 * i:2 * i + 2, :].rearrange("p a t -> p (a t)"), hidden_lo[:, 2 * i:2 * i + 2, :].rearrange("p a t -> p (a t)"), S["hidden_ready"])
                for j in range(4):
                    bank = B.wait(dve, f"D{j}")
                    o = h[:, 2 * j:2 * j + 2, :].rearrange("p a t -> p (a t)")
                    C.link(V.tensor_tensor(o, o, bank[:, :], ALU.add))
                    B.release(dve, f"D{j}")
                layer_end(dve, l + (layers[0] + 1), True)


def lay_out(i):
    f = np.float32
    p1 = []
    for l in range(LAYERS):
        v = {"g_mix": cols(i["norm_mix_g"][l]), "mu": cols(i["a_mu"][l]), "w0": cols(i["a_w0"][l]), "a0": cols(i["a_a0"][l]),
             "k_k": cols(i["a_k_k"][l]), "k_a": cols(i["a_k_a"][l]), "r_k": cols(i["a_r_k"][l].reshape(-1)),
             "gn_g": cols(i["a_gn_g"][l]), "gn_b": cols(i["a_gn_b"][l]), "lb0": cols(i["b_lb_logits"][0]),
             "lb1": cols(i["b_lb_logits"][1]), "not_first": np.full((P, 4), float(l > 0), f), "b_gn": cols(i["b_gn_g"][l]),
             "g_ffn": cols(i["norm_ffn_g"][l]), "conv_b": cols(i["conv_b"][l]), "conv_w0": cols(i["conv_w"][l][0]),
             "conv_w1": cols(i["conv_w"][l][1]), "conv_w2": cols(i["conv_w"][l][2]), "g_final": cols(i["norm_final_g"]),
             "wa_up": np.concatenate([i["a_w_up"][l], i["a_a_up"][l]], 0), "g_up": i["a_g_up"][l]}
        assert list(v) == list(PAR1.at)
        p1.append(np.concatenate(list(v.values()), 1))
    p2 = []
    for l in range(LAYERS):
        w = {n[:-2]: a[l] for n, a in i.items() if n.endswith("_2") and n != "positions_2"}
        v = {"g_mix": cols(w["g_mix_norm"]), "conv_w": np.concatenate([cols(w["conv_w"][j]) for j in range(4)], 1),
             "conv_b": cols(w["conv_b"]), "b_i": col(w["b_igate"]), "b_f": col(w["b_fgate"]),
             "g_mlstm": cols(w["g_mlstm_out"].reshape(-1)), "g_mq": col(np.tile(w["g_moba_q"], 2)),
             "g_mk": col(np.tile(w["g_moba_k"], 2)), "g_mobaout": cols(w["g_moba_out"].reshape(-1)), "g_cq": cols(w["g_cq"]),
             "g_ckv": cols(w["g_ckv"]), "g_lq": col(w["g_mla_q"]), "g_lk": col(w["g_mla_k"]),
             "g_mlaout": cols(w["g_mla_out"].reshape(-1)), "g_mlp": cols(w["g_mlp_norm"])}
        assert list(v) == list(PAR2.at)
        p2.append(np.concatenate(list(v.values()), 1))
    s = [chunks(stream1(i["w_in"][l], i["w_branch"][l], i["w_o"][l], i["w_up"][l], i["w_down"][l])) for l in range(LAYERS)]
    s += [chunks(stream2(*(i[n + "_2"][l] for n in ("w_in", "w_uq", "w_ukv", "w_out", "w_up", "w_down")))) for l in range(LAYERS)]
    c, m = constants()
    return {"x": np.ascontiguousarray(i["x"][0].T.reshape(KD, P, T).transpose(1, 0, 2)), "params1": np.stack(p1), "params2": np.stack(p2),
            "stream": np.concatenate(s), "cst": c, "masks": m, "positions": np.ascontiguousarray(i["positions_2"])}


def kernel(**inputs):
    import concourse.bacc as bacc
    from concourse.bass_utils import run_bass_kernel_spmd

    arrays = lay_out({n: np.asarray(a) for n, a in inputs.items()})
    nc = bacc.Bacc("TRN2", target_bir_lowering=False, num_devices=1)
    args = [nc.dram_tensor(f"in_{n}", a.shape, mybir.dt.from_np(a.dtype), kind="ExternalInput").ap() for n, a in arrays.items()]
    out = nc.dram_tensor("out", (P, KD, T), F32, kind="ExternalOutput").ap()
    build(nc, *args, out)
    r = run_bass_kernel_spmd(nc, [{f"in_{n}": a for n, a in arrays.items()}], core_ids=[0])
    got = r.results[0]["out"]
    return np.ascontiguousarray(got.transpose(1, 0, 2).reshape(D, T).T)[None]
```

```python
from contextlib import ExitStack

import numpy as np

import concourse.bass as bass
from concourse import mybir
from concourse.alu_op_type import AluOpType as ALU

F32 = mybir.dt.float32
I32 = mybir.dt.int32
F32R = mybir.dt.float32r
U8 = mybir.dt.uint8
ACT = mybir.ActivationFunctionType
AX_X = mybir.AxisListType.X

P = 128
T = 256
NT = T // P
D = 1024
KD = D // P
LAYERS = 2
EPS = 1e-6

A_W, A_COLS = 512, 1792
GN_EPS = 64e-5
KAPPA = float(np.exp(-0.5))
C_OFF, G_OFF = 3840, 4932
FF1 = 2816
TOPK, TOP_STEP = 64, 8
BRANCHES = (2, 1, 0)
NEG, TAKEN = -1e30, -3e38
FF2 = 4096
MLA_D = 96

CHUNK = 4
RING = 8
PIECE = 4
HI_RING = 4
LEAD = HI_RING - 1
BLOCKS1, BLOCKS2 = 1216, 800
CH1, CH2 = BLOCKS1 // CHUNK, BLOCKS2 // CHUNK
PIECES1, PIECES2 = BLOCKS1 // PIECE, BLOCKS2 // PIECE
assert CH1 % RING == 0 and CH2 % RING == 0 and CHUNK % PIECE == 0
assert PIECES1 % HI_RING == 0 and PIECES2 % HI_RING == 0
LEVELS = 7
LN_EXP = "natural_log_exp_and_others"
LN = "natural_log"


class Columns:

    def __init__(self, *runs):
        self.at, self.size = {}, 0
        for name, n in runs:
            self.at[name] = (self.size, n)
            self.size += n

    def of(self, table, name):
        a, n = self.at[name]
        return table[:, a:a + n]


PAR1 = Columns(("g_mix", 8), ("mu", 14), ("w0", 4), ("a0", 4), ("k_k", 4), ("k_a", 4), ("r_k", 4), ("gn_g", 4),
               ("gn_b", 4), ("lb0", 4), ("lb1", 4), ("not_first", 4), ("b_gn", 4), ("g_ffn", 8), ("conv_b", 44),
               ("conv_w0", 44), ("conv_w1", 44), ("conv_w2", 44), ("wa_up", A_W), ("g_up", A_W))
PAR2 = Columns(("g_mix", 8), ("conv_w", 16), ("conv_b", 4), ("b_i", 1), ("b_f", 1), ("g_mlstm", 4), ("g_mq", 1),
               ("g_mk", 1), ("g_mobaout", 2), ("g_cq", 3), ("g_ckv", 2), ("g_lq", 1), ("g_lk", 1), ("g_mlaout", 2),
               ("g_mlp", 8), ("g_final", 8))
PAR_SIZE = max(PAR1.size, PAR2.size)
CST = Columns(("ident", P), ("ones", P), ("bones", P), ("pairmask", 2 * P), ("lower", P), ("cneg", T),
              ("rot", P), ("rotp", P), ("rotd", P), ("cos", T), ("sin", T), ("freq", 2),
              ("eps", 1), ("gn_eps", 1))
MERGE = tuple((f"G{j}{n}", f"M{j}{n}", n, j) for n in BRANCHES for j in range(4))
MASKS = Columns(("up", LEVELS * P), ("low", LEVELS * P), ("diag", P))


def blocks(w):
    k, n = w.shape
    w = np.pad(w, ((0, 0), (0, -n % P)))
    return w.reshape(k // P, P, -1, P).transpose(2, 0, 1, 3).reshape(-1, P, P)


def row_blocks(w):
    k, n = w.shape
    w = np.pad(w, ((0, 0), (0, -n % P)))
    return w.reshape(k // P, P, -1, P).transpose(0, 2, 1, 3).reshape(-1, P, P)


def filled(b, n):
    return np.concatenate([b, np.zeros((n - len(b), P, P), b.dtype)])


def stream1(w_in, w_branch, w_o, w_up, w_down):
    b, c = A_COLS, C_OFF
    ki = w_in[:, c + 1024:c + 1088]
    out = [blocks(w_in[:, :b + 1024]),
           blocks(w_in[:, c:c + 512]), blocks(np.concatenate([w_in[:, c + 512 + 64 * (i // 2):c + 576 + 64 * (i // 2)] for i in range(4)], 1)),
           row_blocks(w_in[:, b + 1024:b + 1536]), blocks(w_in[:, c + 768:c + 1024]), blocks(np.concatenate([ki, ki], 1)),
           row_blocks(np.concatenate([w_in[:, c + 640:c + 768], w_in[:, c + 1088:c + 1092]], 1)), blocks(w_in[:, b + 1536:b + 2048])]
    def gate(n, j):
        return blocks(w_in[:, G_OFF + n * D + j * 2 * P:G_OFF + n * D + (j + 1) * 2 * P])

    out.append(gate(*MERGE[0][2:]))
    for i, (_, _, n, j) in enumerate(MERGE):
        out += [gate(*m[2:]) for m in MERGE[i + 1:i + 2]] + [blocks(w_branch[n][:, j * 2 * P:(j + 1) * 2 * P])]
    out.append(blocks(w_o))
    for i in range(0, FF1, P):
        out += [blocks(w_up[:, i:i + P]), blocks(w_up[:, FF1 + i:FF1 + i + P])]
    out.append(blocks(w_down))
    return filled(np.concatenate(out), BLOCKS1)


def stream2(w_in, w_uq, w_ukv, w_out, w_up, w_down):
    i, f = w_in[:, 1536:1540], w_in[:, 1540:1544]
    gap = np.zeros((D, 28), w_in.dtype)
    uq = np.pad(w_uq.reshape(384, 4, MLA_D), ((0, 0), (0, 0), (0, P - MLA_D))).reshape(384, 4 * P)
    kv = w_ukv.reshape(256, 4, 2, 64)
    out = [blocks(w_in[:, 2312:2952]), blocks(np.pad(w_in[:, 2952:2984], ((0, 0), (64, 32)))), blocks(w_in[:, 1544:2056]),
           row_blocks(w_in[:, 2056:2312]), blocks(w_in[:, :512]), blocks(uq), blocks(kv[:, :, 0].reshape(256, 256)),
           row_blocks(kv[:, :, 1].reshape(256, 256)), blocks(np.concatenate([i, gap, f], 1)), row_blocks(w_in[:, 512:1024]),
           blocks(w_in[:, 1024:1536]), blocks(w_out[512:]), blocks(w_out[:512]), blocks(w_up), blocks(w_down)]
    return filled(np.concatenate(out), BLOCKS2)


def chunks(b):
    return b.reshape(-1, CHUNK, P, P).transpose(0, 2, 1, 3).reshape(-1, P, CHUNK * P)


def cols(v):
    return np.ascontiguousarray(v.reshape(-1, P).T)


def col(v, rows=P):
    return np.pad(v.reshape(-1, 1), ((0, rows - v.size), (0, 0)))


def constants():
    s, t = np.arange(P)[:, None], np.arange(P)[None, :]
    f = np.float32
    incl, strict = (s <= t).astype(f), (s < t).astype(f)

    def rotate(n, half, start, size):
        m = np.zeros((P, P), f)
        for base in range(0, n, size):
            for i in range(half):
                a, b = base + start + i, base + start + half + i
                m[b, a], m[a, b] = -1, 1
        return m

    rot = rotate(P, 32, 0, 64)
    inv = (np.float32(10000.0) ** (-np.arange(32, dtype=f) * f(2.0 / 64))).astype(f)
    ang = (np.arange(T, dtype=f)[None, :] * np.tile(inv, 4)[:, None]).astype(f)
    freq = np.zeros((P, 2), f)
    fp = np.power(f(500000.0), -np.arange(0, 16, 2, dtype=f) / f(16)).astype(f)
    fd = np.power(f(10000.0), -np.arange(0, 32, 2, dtype=f) / f(32)).astype(f)
    for base in (0, 64):
        freq[base:base + 16, 0] = np.tile(fp, 2)
    freq[64:96, 1] = np.tile(fd, 2)
    parts = {"ident": np.eye(P, dtype=f), "ones": np.ones((P, P), f), "bones": ((s // 64) == (t // 64)).astype(f),
             "pairmask": np.concatenate([strict, incl], 1), "lower": (s > t).astype(f),
             "cneg": np.concatenate([np.zeros((P, P), f), np.where(t <= s, f(0), f(NEG))], 1),
             "rot": rot, "rotp": rotate(P, 8, 0, 64), "rotd": rotate(MLA_D, 16, 64, MLA_D),
             "cos": np.cos(ang).astype(f), "sin": np.sin(ang).astype(f), "freq": freq,
             "eps": np.full((P, 1), EPS, f), "gn_eps": np.full((P, 1), GN_EPS, f)}
    assert list(parts) == list(CST.at)
    up = []
    for k in range(LEVELS):
        m = 1 << k
        up.append(((s // (2 * m)) == (t // (2 * m))) & (s // m % 2 == 0) & (t // m % 2 == 1))
    masks = np.concatenate(up + [x.T for x in up] + [s == t], 1).astype(f)
    return np.concatenate([parts[n] for n in parts], 1).astype(f), masks


class Chain:

    def __init__(self, eng, sem):
        self.eng, self.sem, self.count = eng, sem, {}

    def link(self, ins, sem=None):
        sem = self.sem if sem is None else sem
        self.count[sem.num] = self.count.get(sem.num, 0) + 1
        ins.then_inc(sem, 1)
        self.eng.wait_ge(sem, self.count[sem.num])


def half_of(ap, k, side):
    return ap.rearrange("p h (n a t) -> p h n a t", a=2, t=1 << k)[:, :, :, side, :]


class Banks:

    def __init__(self, names, tiles, full, free):
        self.slot = {n: (i % 8, i // 8) for i, n in enumerate(names)}
        assert len(self.slot) == len(names)
        self.tiles, self.full, self.free = tiles, full, free

    def open(self, pe, name):
        b, use = self.slot[name]
        if use:
            pe.wait_ge(self.free[b], use)
        return self.tiles[b]

    def full_of(self, name):
        return self.full[self.slot[name][0]]

    def wait(self, eng, name):
        b, use = self.slot[name]
        eng.wait_ge(self.full[b], use + 1)
        return self.tiles[b]

    def free_of(self, name):
        return self.free[self.slot[name][0]]

    def release(self, eng, name):
        eng.sem_inc(self.free[self.slot[name][0]], 1)


class Weights:

    def __init__(self, pe, lo_ring, hi_ring, split, used, first, ends):
        self.pe, self.lo_ring, self.hi_ring, self.split, self.used, self.first = pe, lo_ring, hi_ring, split, used, first
        self.ends, self.seen, self.next, self.pending, self.told = ends, 0, 0, 0, 0

    def take(self, name, n):
        q = self.next
        self.next += n
        self.ends[name] = -(-self.next // PIECE)
        return q

    def block(self, q, n=1):
        p, at = q // PIECE, q % PIECE * P
        assert q % PIECE + n <= PIECE
        if p >= self.seen:
            self.pe.wait_ge(self.split, self.first + (p + 1))
            self.seen = p + 1
        c, o = q // CHUNK % RING, q % CHUNK * P
        return (self.hi_ring[:, p % HI_RING, at:at + n * P], self.lo_ring[:, c, o:o + n * P])

    def skip(self, n):
        self.take("end", n - self.next)
        self.block(n - PIECE)
        self.pe.sem_inc(self.used, self.pending + n // PIECE - self.told)

    def done(self, q):
        if q % PIECE == PIECE - 1:
            self.pending += 1
            self.told += 1


ATT1 = [("0a", 0, [0, 2, 4, 6]), ("0b", 0, [1, 3, 5, 7]), ("1a", 1, [0, 2]), ("1b", 1, [4, 6]), ("1c", 1, [1, 3]), ("1d", 1, [5, 7])]
ATT2 = [("0a", 0, [0, 2]), ("0b", 0, [1, 3]), ("1a", 1, [0, 2]), ("1b", 1, [1, 3])]
INDEX = [("I0a", 0, [0, 2]), ("I0b", 0, [1, 3]), ("I1a", 1, [0, 2]), ("I1b", 1, [1, 3])]
HALVES = [[0, 2, 4, 6], [1, 3, 5, 7]]


def groups1():
    g = [f"A{i}" for i in range(7)] + ["Bq0", "Wup0", "Wup1", "Aup0", "Aup1", "Gup0", "Gup1", "Bq1"]
    g += ["KK0", "KK1", "Bf0", "Bf1", "Cq0", "Cq1", "BON0", "BON1", "Ck"]
    for c in range(2):
        g += [f"Tb{c}", f"Tk{c}", f"Tv{c}"]
    beside = {1: ["Cqi", "Rq0", "Rq1"], 2: ["Cki", "Rk"], 3: ["Cv", "Rqi", "Rki"], 4: ["Bg0"] + [n for n, _, _ in INDEX], 5: ["Bg1"], 6: []}
    for c in range(2):
        g += [f"N{c}0", f"N{c}1"] + [f"S{c}{h}" for q in range(2) for h in HALVES[q]] + (["HS"] if c else ["Bi0", "Bi1"])
        for k in range(1, LEVELS):
            g += [f"O{c}{k}0", f"O{c}{k}1"]
            if c:
                g += [f"CL{ATT1[k - 1][0]}"] + [f"CO{ATT1[k - 3][0]}"] * (k > 2) + [f"CP{ATT1[k - 2][0]}"] * (k > 1)
            for q in range(2):
                g += [f"X{c}{k}{q}"] + ([f"Z{c}{k}{q}"] if k < LEVELS - 1 else [])
            if c == 0:
                g += beside[k]
            else:
                g += [f"H{(k - 2) % (LEVELS + 1)}{t}" for t in range(2)]
        if c:
            g += [f"CO{ATT1[-2][0]}", f"CP{ATT1[-1][0]}", f"H{LEVELS - 2}0", f"H{LEVELS - 2}1", f"CO{ATT1[-1][0]}"]
            g += [f"H{LEVELS - 1}{t}" for t in range(2)]
        g += [f"R{c}", f"SA{c}", f"Y{c}"] + (["ST", "HT"] if c == 0 else [])
    g += ["HO0", "HO1", "GM0", "GM1", MERGE[0][0], "HN0", "HN1", "GV0", "GV1"]
    for i, m in enumerate(MERGE):
        g += [m2[0] for m2 in MERGE[i + 1:i + 2]] + [m[1]]
    g += ["WO0", "WO1", "WO2", "norm2", "WO3"] + [f"U{i}" for i in range(22)] + ["D0", "D1", "D2", "norm", "D3"]
    return g


def groups2():
    g = ["cq0", "cq1", "ckv", "kpe", "aq", "ak", "ncq", "nckv", "av", "nq", "nk", "qk0", "qk1"]
    g += ["uq0", "uq1", "uk0", "uk1", "uv", "rq", "rk", "nlq0", "nlq1", "nlk0", "nlk1", "if", "mv0", "mv1"]
    g += ["rlq0", "rlq1", "rlk0", "rlk1", "acol"]
    for r in range(len(ATT2) + 1):
        now = [ATT2[r][0]] if r < len(ATT2) else []
        last = [ATT2[r - 1][0]] if r else []
        pairs, gate = [x + str(r) for _ in now for x in ("gb", "sc")], [f"mo{r}"] * (r < 2)
        g += gate + pairs if r == 0 else []
        g += [tag + "P" + b for b in last for tag in "BM"] + [tag + "L" + b for b in now for tag in "BM"]
        g += [f"nd{r - 1}"] + pairs + gate if r else []
        g += [tag + "O" + b for b in last for tag in "BM"]
    g += ["bn", "ln", "mn0", "mn1"]
    g += [f"WO{j}" for j in range(4)] + ["norm2"] + [f"U{i}" for i in range(16)] + ["D0", "D1", "D2", "norm", "D3"]
    return g


SIGNALS = """act_chain dve_chain squares_ready norm_ready u_hi_ready u_ready ready
    pmu_ready pmu_used raw_ready rwkv_low_ready squash_ready cum_ready decay_ready kk_ready kksq_ready rstd_in rstd_out
    rwkv_ops_ready bonus_in tm_ready sc_ready n_ready o1_ready xz_ready rhs_ready sa_ready state_ready y_ready gsq_ready
    ya_ready f_ready hcol_in hcol_out ls_in ls_out lse_in lse_out cum_b pairs_in pairs_ready hk_ready hqe_ready ketm_ready
    hstate_ready hsc_ready hosq_ready yb_ready rope_ready cv_ready logits_ready probs_in probs_ready pt_ready pv_done
    yc_ready yc_split gate_ready gate_used merged_ready conv_in conv_mid conv_out hidden_ready h_ready fresh_norm bi_ready
    bsg_ready gA_ready d_diff d_exp s_ready dn_ready v_ready em_ready latents_sq latents_ready
    mix_ready""".split()


def build(nc, x, params, stream, cst_in, masks_in, pos_in, out, layers=(LAYERS, LAYERS)):
    ctx = ExitStack()
    with ctx:
        def sb(name, shape, dt=F32):
            return ctx.enter_context(nc.sbuf_tensor(name, shape, dt))

        def sem(name):
            return ctx.enter_context(nc.semaphore(name))

        landed = [sem(f"chunk_landed{i}") for i in range(RING)]
        inputs_in, params_in, stored = sem("inputs_in"), sem("params_in"), sem("stored")
        hi_written, pieces_split, pieces_used = sem("hi_written"), sem("pieces_split"), sem("pieces_used")
        arrived, gathered, released, ready = sem("arrived"), sem("gathered"), sem("released"), sem("masks_ready")
        bank_full = [sem(f"bank_full{i}") for i in range(8)]
        bank_free = [sem(f"bank_free{i}") for i in range(8)]
        S = {n: sem(n) for n in SIGNALS}
        per_layer = range(bank_full[0].num, S[SIGNALS[-1]].num + 1)
        assert len(per_layer) == 16 + len(SIGNALS)

        def with_twin(name, shape):
            at = -(-nc.sbuf_base // 32) * 32
            t = sb(name, shape)
            return t, nc.alloc_sbuf_tensor_at(name + "_split", shape, F32R, offset=at)

        ring, ring_lo = with_twin("ring", [P, RING, CHUNK * P])
        h = sb("h", [P, KD, T])
        hi_ring = sb("hi_ring", [P, HI_RING, PIECE * P], F32R)
        u, u_lo = with_twin("u", [P, KD, T])
        u_hi = sb("u_hi", [P, KD, T], F32R)
        par = sb("par", [P, PAR_SIZE])
        rn = sb("rn", [P, T])
        cst = sb("cst", [P, CST.size])
        msk = sb("msk", [P, MASKS.size], U8)
        small = sb("small", [P, 128])
        ARENA = 36192
        arena_at = -(-nc.sbuf_base // 32) * 32
        arena = sb("arena", [P, ARENA])
        banks = [ctx.enter_context(nc.psum_tensor(f"bank{i}", [P, 512], F32)) for i in range(8)]

        class Carve:
            def __init__(self, start=0):
                self.at = start

            def __call__(self, n):
                a = self.at
                self.at += n
                assert self.at <= ARENA, self.at
                return arena[:, a:a + n]

        def twin(name, ap):
            n = int(np.prod(ap.shape[1:]))
            return nc.alloc_sbuf_tensor_at(name, [P, n], F32R, offset=arena_at + 4 * ap.offset)[:]

        def K(name):
            return CST.of(cst, name)

        def v3(ap, n):
            return ap.rearrange("p (a b) -> p a b", a=n)

        def spread(ap, n):
            return ap.unsqueeze(1).to_broadcast([ap.shape[0], n, ap.shape[1]])

        def along(ap, n):
            return ap.unsqueeze(2).to_broadcast([ap.shape[0], ap.shape[1], n])

        upm = v3(MASKS.of(msk, "up"), LEVELS)
        lowm = v3(MASKS.of(msk, "low"), LEVELS)
        diagm = MASKS.of(msk, "diag")
        ident, ones, bones = K("ident"), K("ones"), K("bones")

        cv = Carve()
        pa = v3(cv(14 * T), 14)
        cc = v3(cv(8 * 129), 8)
        ar = cv(2048).rearrange("p (j a t) -> p j a t", j=8, a=2)
        einv, av, kk, kmod, bonus, gA = (cv(1024) for _ in range(6))
        low = cv(2 * T)
        tw, sg = low[:, 0:T], low[:, T:2 * T]
        rs = low
        btm, ktm, vtm = (v3(cv(1024), 2) for _ in range(3))
        sc = cv(4096).rearrange("p (h a t) -> p h a t", h=8, a=4)
        nn_at = cv.at
        nn, xx, zz = (v3(cv(1024), 8) for _ in range(3))
        o1_flat = cv(1032)
        o1 = v3(o1_flat[:, 0:1024], 8)
        pmu = v3(o1_flat[:, 0:1028], 4)
        bq, bf, bsg, yb = (cv(1024) for _ in range(4))
        sa, st = cv(512), v3(cv(512), 4)
        bi = v3(cv(1024), 2)
        craw = v3(cv(9 * T), 9)
        cvt = v3(cv(T), 2)
        wi = cv(8)
        ya = pa[:, 0:4, :].rearrange("p a t -> p (a t)")
        merged = ar.rearrange("p j a t -> p (j a t)")
        mask_in = craw.rearrange("p a t -> p (a t)")[:, 0:MASKS.size]
        hE, hqk = kk, kmod
        hls = hqk
        hb = bf
        hks = cc.rearrange("p a t -> p (a t)")[:, 0:1024]
        hsc = pa[:, 4:8, :].rearrange("p a t -> p (a t)")
        yc = pa[:, 8:12, :].rearrange("p a t -> p (a t)")
        hke = pa[:, 12:14, :].rearrange("p a t -> p (a t)")
        ketm = hke
        hqe, hst = cv(512), cv(512)
        scr, amask = (v3(cv(512), 2) for _ in range(2))
        lg = [cv(512), scr.rearrange("p a t -> p (a t)")]
        work = [lg[0][:, 0:P], craw[:, 6, :]]
        tmp = cv(T)
        pT = craw[:, 4:6, :].rearrange("p a t -> p (a t)")
        fv = Carve()
        hidden = v3(fv(32 * T), 32)
        cb = [v3(fv(512), 2) for _ in range(4)]
        hidden_hi, hidden_lo = v3(twin("hidden_hi", arena[:, fv.at + 4 * T:fv.at + 36 * T]), 32), v3(twin("hidden_lo", hidden), 32)
        sc_flat = sc.rearrange("p h a t -> p (h a t)")
        ya_lo, yb_lo, yc_lo = twin("ya_lo", ya), twin("yb_lo", yb), twin("yc_lo", yc)
        ya_hi, yb_hi, yc_hi = twin("ya_hi", sc_flat[:, 0:1024]), twin("yb_hi", hqk), twin("yc_hi", av)
        ysq = einv
        merged_hi, merged_lo = twin("merged_hi", arena[:, nn_at:nn_at + 2048]), twin("merged_lo", merged)
        next_squares = v3(arena[:, nn_at:nn_at + 2048], KD)
        squares = v3(sc.rearrange("p h a t -> p (h a t)")[:, 0:2048], KD)
        gate_buf = [lg[0], lg[1]]
        mtmp = pT
        bv = Carve(fv.at)
        tab = bv(4 * T)
        tabs = [tab[:, i * T:(i + 1) * T] for i in range(4)]
        sq2 = v3(bv(8 * T), 8)
        qkraw = v3(bv(4 * T), 4)
        mvt = v3(bv(1024), 2)
        mo = v3(bv(4 * T), 4)
        ifr = bv(8 * T)
        acol = v3(bv(8), 2)
        dT = bv(384)
        sT = [bv(384), bv(384)]
        em, dn = bv(T), bv(T)
        mix = v3(bv(8 * T), 8)
        aqk = v3(bv(4 * T), 4)
        avt = v3(bv(512), 2)
        cqk = v3(bv(5 * T), 5)
        lqk = v3(bv(8 * T), 8)
        kpe = bv(T)
        lvt = v3(bv(512), 2)
        t512 = bv(512)
        lgpt = bv(2048)
        lg2, pT2 = ([lgpt[:, o + 512 * i:o + 512 * (i + 1)] for i in range(2)] for o in (0, 1024))
        sqb, sqa = bv(1024), bv(1024)
        lrs = bv(512)
        cqk_hi = v3(twin("latents_hi", bv(5 * T)), 5)
        cqk_lo, mix_lo = v3(twin("latents_lo", cqk), 5), v3(twin("mix_lo", mix), 8)
        mix_hi = v3(twin("mix_hi", sq2), 8)
        flat = lambda ap: ap.rearrange("p a t -> p (a t)")
        roots = {"next": (rn[:], next_squares[:, 0, :], next_squares[:, 1, :]),
                 "keys": (flat(zz), bonus, flat(nn)), "hgrn": (hE, hqk, hks),
                 "rwkv": (ysq, sc_flat[:, 1024:2048], sc_flat[:, 2048:3072]), "ffn": (tmp, rs[:, 0:T], rs[:, T:2 * T]),
                 "latents": (lrs, t512, flat(mix[:, 0:2, :])), "block qk": (sqa, sqb, flat(mix[:, 2:6, :])),
                 "latent qk": (flat(sq2), lgpt, flat(mix)), "mlstm": (sqb, ifr[:, 0:1024], ifr[:, 1024:2048]),
                 "block": (sqa[:, 0:512], lg2[0], pT2[0]), "latent": (sqa[:, 512:1024], lg2[1], pT2[1]),
                 "mlp": (dn, dT[:, 0:T], em)}
        mid, emid, eend = small[:, 0:8], small[:, 8:16], small[:, 16:24]
        lbc, lnA, ln1m, omlb = (small[:, 24 + 4 * i:28 + 4 * i] for i in range(4))
        m8, nmax, ssum = small[:, 40:48], small[:, 48:56], small[:, 56:64]
        omu = small[:, 64:78]
        nbf = small[:, 80:81]
        isz = small[:, 84:88]

        b1 = Banks(groups1(), banks, bank_full, bank_free)
        b2 = Banks(groups2(), banks, bank_full, bank_free)
        ends1, ends2 = {}, {}
        u_parts = (u_hi, u_lo)

        block = ctx.enter_context(nc.Block())

        def layer_end(eng, done, leader):
            eng.sem_inc(arrived, 1)
            if leader:
                eng.wait_ge(arrived, (done + 1) * 3)
                eng.sem_inc(gathered, 1)
                eng.sem_clear(per_layer)
                eng.sem_inc(released, 1)
            else:
                eng.wait_ge(released, done + 1)

        @block.sync
        def _(sp):
            sp.dma_start(h[:], x).then_inc(inputs_in, 16)
            sp.dma_start(cst[:], cst_in).then_inc(inputs_in, 16)
            sp.dma_start(mask_in, masks_in).then_inc(inputs_in, 16)
            n = (layers[0] * CH1 + layers[1] * CH2) // RING
            with sp.Fori(0, n) as r:
                for s in range(RING):
                    sp.wait_ge(pieces_used, r * (RING * CHUNK // PIECE) + (s + 1) * (CHUNK // PIECE))
                    sp.dma_start(ring[:, s, :], stream[bass.ds(r * RING + s, 1)].rearrange("a p n -> p (a n)"))\
                      .then_inc(landed[s], 16)

        @block.gpsimd
        def _(pool):
            n = (layers[0] * CH1 + layers[1] * CH2) // RING
            per_round = RING * CHUNK // PIECE
            with pool.Fori(0, n) as r:
                for i in range(per_round):
                    pool.wait_ge(hi_written, r * per_round + (i + 1))
                    c, o = i * PIECE // CHUNK, i * PIECE % CHUNK * P
                    x_ = ring[:, c, o:o + PIECE * P]
                    nc.gpsimd.tensor_tensor(ring_lo[:, c, o:o + PIECE * P], x_, hi_ring[:, i % HI_RING, :].bitcast(F32), ALU.subtract).then_inc(pieces_split, 1)

        @block.tensor
        def _(pe):
            pe.sem_inc(pieces_used, RING * CHUNK // PIECE)

            def runner(B, W):
                def mm(o, l, r, start=True, stop=True, full=None, done=None):
                    ins = nc.tensor.matmul(o, l, r, start=start, stop=stop)
                    if full is not None:
                        ins.then_inc(B.full_of(full), 1)
                    elif done is not None:
                        ins.then_inc(done, 1)
                    elif W.pending:
                        W.pending -= 1
                        ins.then_inc(pieces_used, 1)

                def mm3(o, l, r, start, stop, full=None):
                    mm(o, l[0], r[0], start, False)
                    mm(o, l[0], r[1], False, False)
                    mm(o, l[1], r[0], False, stop, full=full)

                def cut(act, *at):
                    return tuple(a[(slice(None), *at)] for a in act)

                def after(signal, base, per):
                    return lambda k: None if k % per else pe.wait_ge(S[signal], base + k // per + 1)

                def project(name, tiles, act, K_=KD, ready=None):
                    bank = B.open(pe, name)
                    for i in range(tiles):
                        q = W.take(name, K_)
                        for k in range(K_):
                            if ready and i == 0:
                                ready(k)
                            mm3(bank[:, i * T:(i + 1) * T], W.block(q + k), cut(act, k), k == 0, k == K_ - 1,
                                full=name if (i, k) == (tiles - 1, K_ - 1) else None)
                            W.done(q + k)

                def project_rows(names, act, width, K_=KD):
                    n = width * P
                    q = W.take(names[0], K_ * width)
                    if len(names) == 2:
                        open_ = [B.open(pe, name) for name in names]
                        for k in range(K_):
                            for t in range(NT):
                                mm3(open_[t][:, 0:n], cut(act, k, slice(t * P, (t + 1) * P)), W.block(q + k * width, width),
                                    k == 0, k == K_ - 1, full=names[t] if k == K_ - 1 else None)
                            for b in range(width):
                                W.done(q + k * width + b)
                        return
                    bank = B.open(pe, names[0])
                    for t in range(NT):
                        for k in range(K_):
                            mm3(bank[:, t * n:(t + 1) * n], cut(act, k, slice(t * P, (t + 1) * P)), W.block(q + k * width, width),
                                k == 0, k == K_ - 1, full=names[0] if (t, k) == (NT - 1, K_ - 1) else None)
                            for b in range(width if t == NT - 1 else 0):
                                W.done(q + k * width + b)

                def sums(name, mat, act, n, rows=P):
                    bank = B.open(pe, name)
                    for i in range(n):
                        mm(bank[0:rows, i * T:(i + 1) * T], mat, act[:, i, :], full=name if i == n - 1 else None)

                def total(name, act, n, ready=None, tiles=None):
                    bank = banks[B.slot[name][0]] if tiles and tiles[0] else B.open(pe, name)
                    for i in tiles or range(n):
                        if ready:
                            ready(i)
                        mm(bank[:, 0:T], ones, act[:, i, :], i == 0, i == n - 1, full=name if i == n - 1 else None)

                def turn(name, tiles):
                    bank = B.open(pe, name)
                    for i, a in enumerate(tiles):
                        ins = nc.tensor.transpose(bank[:, i * P:(i + 1) * P], a, ident)
                    ins.then_inc(B.full_of(name), 1)

                return mm, mm3, cut, after, project, project_rows, sums, total, turn

            pe.wait_ge(inputs_in, 48)

            def first_total():
                for k in range(KD):
                    if k % 2 == 0:
                        pe.wait_ge(S["squares_ready"], k // 2 + 1)
                    ins = nc.tensor.matmul(banks[0][:, 0:T], ones, next_squares[:, k, :], start=k == 0, stop=k == KD - 1)
                ins.then_inc(bank_full[0], 1)

            first_total()
            layer_end(pe, 0, False)
            with pe.Fori(0, layers[0]) as l:
                W = Weights(pe, ring_lo, hi_ring, pieces_split, pieces_used, l * PIECES1, ends1)
                B = b1
                mm, mm3, cut, after, project, project_rows, sums, total, turn = runner(B, W)
                for i in range(7):
                    project(f"A{i}", 2, u_parts, ready=None if i else after("u_ready", 0, 2))
                project("Bq0", 2, u_parts)
                pe.wait_ge(params_in, (l + 1) * 16)
                up = PAR1.of(par, "wa_up")
                pe.wait_ge(S["rwkv_low_ready"], 1)
                for a, n in ((0, "Wup"), (64, "Aup")):
                    rhs = tw[0:64, :] if a == 0 else pa[64:128, 12, :]
                    for g in range(2):
                        bank = B.open(pe, f"{n}{g}")
                        for i in range(2):
                            j = 2 * g + i
                            mm(bank[:, i * T:(i + 1) * T], up[a:a + 64, j * P:(j + 1) * P], rhs,
                               full=f"{n}{g}" if i else None)
                pe.wait_ge(S["rwkv_low_ready"], 2)
                for g in range(2):
                    bank = B.open(pe, f"Gup{g}")
                    for i in range(2):
                        j = 2 * g + i
                        mm(bank[:, i * T:(i + 1) * T], PAR1.of(par, "g_up")[:, j * P:(j + 1) * P], sg,
                           full=f"Gup{g}" if i else None)
                project("Bq1", 2, u_parts)
                pe.wait_ge(S["kksq_ready"], 1)
                for g in range(2):
                    sums(f"KK{g}", bones, v3(bonus, 4)[:, 2 * g:2 * g + 2, :], 2)
                for n in ("Bf0", "Bf1", "Cq0", "Cq1"):
                    project(n, 2, u_parts)
                pe.wait_ge(S["bonus_in"], 1)
                for g in range(2):
                    sums(f"BON{g}", bones, v3(bonus, 4)[:, 2 * g:2 * g + 2, :], 2)
                project("Ck", 2, u_parts)
                pe.wait_ge(S["rwkv_ops_ready"], 1)
                bt, kt = v3(av, 8), v3(einv, 8)
                for c in range(2):
                    turn(f"Tb{c}", [bt[:, 2 * j + c, :] for j in range(4)])
                    turn(f"Tk{c}", [kt[:, 2 * j + c, :] for j in range(4)])
                    turn(f"Tv{c}", [pa[:, 8 + j, c * P:(c + 1) * P] for j in range(4)])

                def scores(c):
                    for q in range(2):
                        bank = B.open(pe, f"N{c}{q}")
                        for i, hd in enumerate(HALVES[q]):
                            r, j = 64 * (hd % 2), hd // 2 * 2 + c
                            mm(bank[:, i * P:(i + 1) * P], ar[r:r + 64, j, 0, :], bt[r:r + 64, j, :],
                               full=f"N{c}{q}" if i == 3 else None)
                    for hd in HALVES[0] + HALVES[1]:
                        r, j = 64 * (hd % 2), hd // 2 * 2 + c
                        bank = B.open(pe, f"S{c}{hd}")
                        both = ar[r:r + 64, j, :, :].rearrange("p a t -> p (a t)")
                        mm(bank[:, 0:T], bt[r:r + 64, j, :], both)
                        mm(bank[:, T:2 * T], kt[r:r + 64, j, :], both, full=f"S{c}{hd}")

                def level_first(c, k):
                    for q in range(2):
                        pe.wait_ge(S["xz_ready"], c * 2 * LEVELS + (k - 1) * 2 + q + 1)
                        bank = B.open(pe, f"O{c}{k}{q}")
                        for i in range(4):
                            hd = 4 * q + i
                            mm(bank[:, i * P:(i + 1) * P], nn[:, hd, :], xx[:, hd, :],
                               full=f"O{c}{k}{q}" if i == 3 else None)

                def level_second(c, k):
                    for q in range(2):
                        pe.wait_ge(S["o1_ready"], c * 2 * (LEVELS - 1) + (k - 1) * 2 + q + 1)
                        for n, l_, r_ in (("X", zz, o1), ("Z", o1, zz)):
                            if n == "Z" and k == LEVELS - 1:
                                continue
                            bank = B.open(pe, f"{n}{c}{k}{q}")
                            for i in range(4):
                                hd = 4 * q + i
                                mm(bank[:, i * P:(i + 1) * P], l_[:, hd, :], r_[:, hd, :],
                                   full=f"{n}{c}{k}{q}" if i == 3 else None)

                def solve(c):
                    pe.wait_ge(S["tm_ready"], 6)
                    bank = B.open(pe, f"R{c}")
                    for j in range(4):
                        if c:
                            if j == 0:
                                pe.wait_ge(S["state_ready"], 1)
                            mm(bank[:, j * P:(j + 1) * P], ar[:, 2 * j + c, 0, :], st[:, j, :], True, False)
                        for hd in (2 * j, 2 * j + 1):
                            mm(bank[:, hd * 64:hd * 64 + 64], sc[:, hd, 2, :], vtm[:, c, hd * 64:hd * 64 + 64], c == 0, c == 0 or hd % 2 == 1,
                               full=f"R{c}" if hd == 7 else None)
                    pe.wait_ge(S["rhs_ready"], c + 1)
                    pe.wait_ge(S["xz_ready"], (c + 1) * 2 * LEVELS)
                    bank = B.open(pe, f"SA{c}")
                    for hd in range(8):
                        mm(bank[:, hd * 64:hd * 64 + 64], xx[:, 4 * (hd % 2) + hd // 2, :], rs[:, hd * 64:hd * 64 + 64],
                           full=f"SA{c}" if hd == 7 else None)
                    pe.wait_ge(S["sa_ready"], c + 1)
                    bank = B.open(pe, f"Y{c}")
                    for j in range(4):
                        if c:
                            mm(bank[:, j * P:(j + 1) * P], st[:, j, :], ar[:, 2 * j + c, 1, :], True, False)
                        for hd in (2 * j, 2 * j + 1):
                            r = 64 * (hd % 2)
                            o = bank[r:r + 64, j * P:(j + 1) * P]
                            mm(o, sa[:, hd * 64:hd * 64 + 64], sc[:, hd, 1, :], c == 0, False)
                            mm(o, vtm[:, c, hd * 64:hd * 64 + 64], sc[:, hd, 3, :], False, True,
                               full=f"Y{c}" if hd == 7 else None)
                    if c == 0:
                        bank = B.open(pe, "ST")
                        for hd in range(8):
                            r, j = 64 * (hd % 2), hd // 2
                            o = bank[r:r + 64, j * 64:(j + 1) * 64]
                            mm(o, btm[:, 0, hd * 64:hd * 64 + 64], sa[:, hd * 64:hd * 64 + 64], True, False)
                            mm(o, ktm[:, 0, hd * 64:hd * 64 + 64], vtm[:, 0, hd * 64:hd * 64 + 64], False, True,
                               full="ST" if hd == 7 else None)

                def hgrn_pairs(k):
                    if k < LEVELS:
                        pe.wait_ge(S["pairs_ready"], k + 1)
                    qk = v3(hqk, 8)
                    for c in range(2):
                        bank = B.open(pe, f"H{k}{c}")
                        for hd in range(4):
                            i = 2 * hd + c
                            l_, r_ = (qk[:, i, :], qk[:, i, :]) if k < LEVELS else (v3(hks, 8)[:, i, :], v3(bq, 8)[:, i, :])
                            mm(bank[:, hd * P:(hd + 1) * P], l_, r_, full=f"H{k}{c}" if hd == 3 else None)

                def part(hd):
                    return slice(64 * (hd % 2), 64 * (hd % 2) + 64)

                def index():
                    pe.wait_ge(S["rope_ready"], 1)
                    for name, tt, heads in INDEX:
                        w = (tt + 1) * P
                        bank = B.open(pe, name)
                        for i, hd in enumerate(heads):
                            mm(bank[:, i * w:(i + 1) * w], craw[part(hd), 4 + hd // 2, tt * P:(tt + 1) * P],
                               craw[part(hd), 6, 0:w], full=name if i == len(heads) - 1 else None)

                def logits(i):
                    b, tt, heads = ATT1[i]
                    w = (tt + 1) * P
                    bank = B.open(pe, f"CL{b}")
                    for j, hd in enumerate(heads):
                        mm(bank[:, j * w:(j + 1) * w], craw[part(hd), hd // 2, tt * P:(tt + 1) * P], craw[part(hd), 7 + hd // 4, 0:w],
                           full=f"CL{b}" if j == len(heads) - 1 else None)

                def turn_probs(i):
                    b, tt, heads = ATT1[i]
                    pe.wait_ge(S["probs_ready"], i + 1)
                    turn(f"CP{b}", [lg[i % 2][:, j * P:(j + 1) * P] for j in range(len(heads) * (tt + 1))])

                def values(i):
                    b, tt, heads = ATT1[i]
                    pe.wait_ge(S["pt_ready"], i + 1)
                    bank = B.open(pe, f"CO{b}")
                    for j, hd in enumerate(heads):
                        for s in range(tt + 1):
                            at = (j * (tt + 1) + s) * P
                            mm(bank[part(hd), j * P:(j + 1) * P], cvt[:, s, hd // 4 * 64:hd // 4 * 64 + 64], pT[:, at:at + P],
                               s == 0, s == tt, full=f"CO{b}" if j == len(heads) - 1 and s == tt else None)

                scores(0)
                project_rows(["Bi0", "Bi1"], u_parts, 4)
                for k in range(1, LEVELS):
                    level_first(0, k)
                    level_second(0, k)
                    if k == 1:
                        project("Cqi", 2, u_parts)
                        pe.wait_ge(S["raw_ready"], 3)
                        sums("Rq0", K("rot"), craw[:, 0:2, :], 2)
                        sums("Rq1", K("rot"), craw[:, 2:4, :], 2)
                    elif k == 2:
                        project("Cki", 1, u_parts)
                        sums("Rk", K("rot"), craw[:, 7:9, :], 2)
                    elif k == 3:
                        bank = B.open(pe, "Cv")
                        q = W.take("Cv", 2 * KD)
                        n = P + 4
                        for t in range(NT):
                            for i in range(KD):
                                mm3(bank[:, t * n:(t + 1) * n], cut(u_parts, i, slice(t * P, (t + 1) * P)),
                                    [w[:, 0:n] for w in W.block(q + 2 * i, 2)], i == 0, i == KD - 1,
                                    full="Cv" if (t, i) == (NT - 1, KD - 1) else None)
                                for b in range(2 if t == NT - 1 else 0):
                                    W.done(q + 2 * i + b)
                        pe.wait_ge(S["raw_ready"], 5)
                        sums("Rqi", K("rot"), craw[:, 4:6, :], 2)
                        sums("Rki", K("rot"), craw[:, 6:7, :], 1)
                    elif k == 4:
                        project("Bg0", 2, u_parts)
                        index()
                    elif k == 5:
                        project("Bg1", 2, u_parts)
                solve(0)
                pe.wait_ge(S["hk_ready"], 1)
                turn("HT", [v3(hke, 4)[:, hd, :] for hd in range(4)])
                scores(1)
                pe.wait_ge(S["ketm_ready"], 1)
                pe.wait_ge(S["bi_ready"], 2)
                bank = B.open(pe, "HS")
                for hd in range(4):
                    mm(bank[:, hd * P:(hd + 1) * P], ketm[:, hd * P:(hd + 1) * P], bi[:, 0, hd * P:(hd + 1) * P],
                       full="HS" if hd == 3 else None)
                for k in range(1, LEVELS):
                    level_first(1, k)
                    logits(k - 1)
                    if k > 2:
                        values(k - 3)
                    if k > 1:
                        turn_probs(k - 2)
                    level_second(1, k)
                    hgrn_pairs((k - 2) % (LEVELS + 1))
                values(len(ATT1) - 2)
                turn_probs(len(ATT1) - 1)
                hgrn_pairs(LEVELS - 2)
                values(len(ATT1) - 1)
                hgrn_pairs(LEVELS - 1)
                solve(1)
                pe.wait_ge(S["hsc_ready"], 1)
                pe.wait_ge(S["hqe_ready"], 1)
                pe.wait_ge(S["hstate_ready"], 1)
                for c in range(2):
                    bank = B.open(pe, f"HO{c}")
                    for hd in range(4):
                        o = bank[:, hd * P:(hd + 1) * P]
                        mm(o, bi[:, c, hd * P:(hd + 1) * P], v3(hsc, 8)[:, 2 * hd + c, :], True, c == 0,
                           full=f"HO{c}" if c == 0 and hd == 3 else None)
                        if c:
                            mm(o, v3(hst, 4)[:, hd, :], v3(hqe, 4)[:, hd, :], False, True,
                               full=f"HO{c}" if hd == 3 else None)
                pe.wait_ge(S["y_ready"], 2)
                for g in range(2):
                    sums(f"GM{g}", bones, v3(ya, 4)[:, 2 * g:2 * g + 2, :], 2)
                project(MERGE[0][0], 2, u_parts)
                pe.wait_ge(S["hosq_ready"], 2)
                for g in range(2):
                    sums(f"HN{g}", ones, v3(hE, 4)[:, 2 * g:2 * g + 2, :], 2)
                pe.wait_ge(S["gsq_ready"], 1)
                for g in range(2):
                    sums(f"GV{g}", bones, v3(ysq, 4)[:, 2 * g:2 * g + 2, :], 2)
                ys = [(v3(a, 4), v3(b, 4)) for a, b in ((ya_hi, ya_lo), (yb_hi, yb_lo), (yc_hi, yc_lo))]
                for i, (_, output, n, j) in enumerate(MERGE):
                    if i + 1 < len(MERGE):
                        project(MERGE[i + 1][0], 2, u_parts)
                    if j == 0:
                        pe.wait_ge(S[("ya_ready", "yb_ready", "yc_split")[n]], 1)
                    project(output, 2, ys[n], 4)
                for j in range(4):
                    project(f"WO{j}", 2, (v3(merged_hi, KD), v3(merged_lo, KD)), ready=None if j else after("merged_ready", 0, 2))
                    if j == 2:
                        total("norm2", squares, KD, after("squares_ready", 0, 2), range(2))
                total("norm2", squares, KD, after("squares_ready", 0, 2), range(2, KD))
                for i in range(22):
                    project(f"U{i}", 2, u_parts, ready=None if i else after("u_ready", KD // 2, 2))
                for j in range(4):
                    project(f"D{j}", 2, (hidden_hi, hidden_lo), 22, ready=None if j else after("hidden_ready", 0, 1))
                    if j == 2:
                        total("norm", next_squares, KD, after("squares_ready", KD // 2, 2), range(2))
                total("norm", next_squares, KD, after("squares_ready", KD // 2, 2), range(2, KD))
                B.wait(pe, "norm")
                W.skip(BLOCKS1)
                layer_end(pe, l + 1, False)

            pe.wait_ge(S["ready"], 1)
            nc.tensor.matmul(banks[1][:, 0:T], ones[0:1, :], t512[0:1, 0:T], start=True, stop=True)\
              .then_inc(bank_full[1], 1)
            first_total()
            layer_end(pe, layers[0] + 1, False)

            if not layers[1]:
                return
            with pe.Fori(0, layers[1]) as l:
                W = Weights(pe, ring_lo, hi_ring, pieces_split, pieces_used, l * PIECES2 + layers[0] * PIECES1, ends2)
                B = b2
                mm, mm3, cut, after, project, project_rows, sums, total, turn = runner(B, W)
                def part(hd):
                    return slice(64 * (hd % 2), 64 * (hd % 2) + 64)

                project("cq0", 2, u_parts, ready=after("u_ready", 0, 2))
                project("cq1", 1, u_parts)
                project("ckv", 2, u_parts)
                bank = B.open(pe, "kpe")
                q = W.take("kpe", KD)
                for k in range(KD):
                    mm3(bank[:, 0:T], W.block(q + k), cut(u_parts, k), k == 0, k == KD - 1,
                        full="kpe" if k == KD - 1 else None)
                    W.done(q + k)
                project("aq", 2, u_parts)
                project("ak", 2, u_parts)
                pe.wait_ge(S["latents_sq"], 1)
                total("ncq", sq2[:, 0:3, :], 3)
                total("nckv", sq2[:, 3:5, :], 2)
                project_rows(["av"], u_parts, 2)
                pe.wait_ge(S["kksq_ready"], 1)
                sums("nq", bones, v3(sqa, 4)[:, 0:2, :], 2)
                sums("nk", bones, v3(sqa, 4)[:, 2:4, :], 2)
                project("qk0", 2, u_parts)
                project("qk1", 2, u_parts)
                pe.wait_ge(S["latents_ready"], 1)
                latents = (cqk_hi, cqk_lo)
                for g in range(2):
                    bank = B.open(pe, f"uq{g}")
                    for i in range(2):
                        q = W.take(f"uq{g}", 3)
                        for k in range(3):
                            mm3(bank[0:MLA_D, i * T:(i + 1) * T], [w[:, 0:MLA_D] for w in W.block(q + k)], cut(latents, k), k == 0, k == 2,
                                full=f"uq{g}" if (i, k) == (1, 2) else None)
                            W.done(q + k)
                for g in range(2):
                    bank = B.open(pe, f"uk{g}")
                    q = W.take(f"uk{g}", 2)
                    for i in range(2):
                        for k in range(2):
                            mm3(bank[0:64, i * T:(i + 1) * T], [w[:, 64 * i:64 * i + 64] for w in W.block(q + k)], cut(latents, 3 + k),
                                k == 0, k == 1, full=f"uk{g}" if (i, k) == (1, 1) else None)
                    W.done(q)
                    W.done(q + 1)
                project_rows(["uv"], [a[:, 3:5, :] for a in latents], 2, 2)
                pe.wait_ge(S["kk_ready"], 1)
                sums("rq", K("rotp"), aqk[:, 0:2, :], 2)
                sums("rk", K("rotp"), aqk[:, 2:4, :], 2)
                pe.wait_ge(S["lse_in"], 1)
                for n, o in (("nlq", 0), ("nlk", 4)):
                    for g in range(2):
                        sums(f"{n}{g}", ones[0:MLA_D, 0:MLA_D], sq2[0:MLA_D, o + 2 * g:o + 2 * g + 2, :], 2, MLA_D)
                bank = B.open(pe, "if")
                q = W.take("if", KD)
                for i in range(2):
                    for k in range(KD):
                        mm3(bank[0:4, i * T:(i + 1) * T], [w[:, 32 * i:32 * i + 4] for w in W.block(q + k)], cut(u_parts, k), k == 0, k == KD - 1,
                            full="if" if (i, k) == (1, KD - 1) else None)
                        if i:
                            W.done(q + k)
                project_rows(["mv0", "mv1"], u_parts, 4)
                pe.wait_ge(S["lse_out"], 1)
                for n, o in (("rlq", 0), ("rlk", 4)):
                    for g in range(2):
                        sums(f"{n}{g}", K("rotd")[0:MLA_D, 0:MLA_D], lqk[0:MLA_D, o + 2 * g:o + 2 * g + 2, :], 2, MLA_D)
                pe.wait_ge(S["d_diff"], 1)
                bank = B.open(pe, "acol")
                for t in range(NT):
                    ins = nc.tensor.transpose(bank[:, 4 * t:4 * t + 4], ifr[0:4, t * P:(t + 1) * P], ident[0:4, 0:4])
                ins.then_inc(B.full_of("acol"), 1)

                def logits(tag, r):
                    b, tt, heads = ATT2[r]
                    w = (tt + 1) * P
                    bank = B.open(pe, f"{tag}L{b}")
                    for j, hd in enumerate(heads):
                        if tag == "B":
                            q_, k_ = aqk[part(hd), hd // 2, :], aqk[part(hd), 2 + hd // 2, :]
                        else:
                            q_, k_ = lqk[0:MLA_D, hd, :], lqk[0:MLA_D, 4 + hd, :]
                        mm(bank[:, j * w:(j + 1) * w], q_[:, tt * P:(tt + 1) * P], k_[:, 0:w], full=f"{tag}L{b}" if j else None)

                def turn_probs(tag, r):
                    b, tt, heads = ATT2[r]
                    n = "BM".index(tag)
                    pe.wait_ge(S["probs_ready"], 2 * r + n + 1)
                    turn(f"{tag}P{b}", [lg2[n][:, j * P:(j + 1) * P] for j in range(len(heads) * (tt + 1))])

                def values(tag, r):
                    b, tt, heads = ATT2[r]
                    n = "BM".index(tag)
                    v_ = avt if tag == "B" else lvt
                    pe.wait_ge(S["pt_ready"], 2 * r + n + 1)
                    bank = B.open(pe, f"{tag}O{b}")
                    for j, hd in enumerate(heads):
                        for t in range(tt + 1):
                            at = (j * (tt + 1) + t) * P
                            mm(bank[part(hd), j * P:(j + 1) * P], v_[:, t, hd * 64:hd * 64 + 64], pT2[n][:, at:at + P],
                               t == 0, t == tt, full=f"{tag}O{b}" if j and t == tt else None)

                def pair_scores(hd):
                    bank = B.open(pe, f"gb{hd}")
                    mm(bank[:, 0:2 * T], ident[0:4, hd:hd + 1].to_broadcast([4, P]), ifr[0:4, 2 * T:4 * T], full=f"gb{hd}")
                    bank = B.open(pe, f"sc{hd}")
                    qh, kh = qkraw[part(hd), hd // 2, :], qkraw[part(hd), 2 + hd // 2, :]
                    mm(bank[:, 0:T], kh[:, 0:P], qh)
                    mm(bank[:, T:T + P], kh[:, P:T], qh[:, P:T], full=f"sc{hd}")

                def numerator(hd):
                    pe.wait_ge(S["s_ready"], hd + 1)
                    bank = B.open(pe, f"nd{hd}")
                    s_ = sT[hd % 2]
                    for o, l0, l1 in ((0, mvt[:, 0, hd * P:(hd + 1) * P], mvt[:, 1, hd * P:(hd + 1) * P]), (T, ones, ones)):
                        mm(bank[:, o:o + T], l0, s_[:, 0:T], True, False)
                        mm(bank[:, o + P:o + T], l1, s_[:, T:T + P], False, True, full=f"nd{hd}" if o else None)

                project("mo0", 2, u_parts)
                pe.wait_ge(S["conv_out"], 4)
                pe.wait_ge(S["v_ready"], 2)
                pair_scores(0)
                for r in range(len(ATT2) + 1):
                    for tag in "BM" * (r > 0):
                        turn_probs(tag, r - 1)
                    for tag in "BM" * (r < len(ATT2)):
                        if r == 0:
                            pe.wait_ge(S["rope_ready"], 1 + (tag == "M"))
                        logits(tag, r)
                    if r:
                        numerator(r - 1)
                    if 0 < r < len(ATT2):
                        pair_scores(r)
                    if r == 1:
                        project("mo1", 2, u_parts)
                    for tag in "BM" * (r > 0):
                        values(tag, r - 1)
                for n, name, o in ((1, "bn", 0), (2, "ln", 2)):
                    pe.wait_ge(S["gsq_ready"], n)
                    sums(name, bones, v3(sqa, 4)[:, o:o + 2, :], 2)
                pe.wait_ge(S["hosq_ready"], 1)
                for g in range(2):
                    sums(f"mn{g}", ones, v3(sqb, 4)[:, 2 * g:2 * g + 2, :], 2)
                for half in range(2):
                    mix_in = after("mix_ready", 2 * half, 2)
                    for j in range(4):
                        name = f"WO{j}"
                        bank = B.open(pe, name) if half == 0 else banks[B.slot[name][0]]
                        for i in range(2):
                            q = W.take(name if half else name + " attention", 4)
                            for k in range(4):
                                if i == 0 and j == 0:
                                    mix_in(k)
                                mm3(bank[:, i * T:(i + 1) * T], W.block(q + k), cut((mix_hi, mix_lo), 4 * half + k), half == 0 and (i, k) == (0, 0),
                                    (half, i, k) == (1, 1, 3), full=name if (half, i, k) == (1, 1, 3) else None)
                                W.done(q + k)
                        if half and j == 2:
                            total("norm2", squares, KD, after("squares_ready", 0, 2), range(2))
                total("norm2", squares, KD, after("squares_ready", 0, 2), range(2, KD))
                for i in range(16):
                    project(f"U{i}", 2, u_parts, ready=None if i else after("u_ready", KD // 2, 2))
                for j in range(4):
                    project(f"D{j}", 2, (hidden_hi, hidden_lo), 32, ready=None if j else after("hidden_ready", 0, 2))
                    if j == 2:
                        total("norm", next_squares, KD, after("squares_ready", KD // 2, 2), range(2))
                total("norm", next_squares, KD, after("squares_ready", KD // 2, 2), range(2, KD))
                B.wait(pe, "norm")
                W.skip(BLOCKS2)
                layer_end(pe, l + (layers[0] + 2), False)

        @block.scalar
        def _(act):
            def A(o, i, f, **kw):
                return nc.scalar.activation(o, i, f, **kw)

            def norm_squares(C, dst, fresh=None, tiles=range(KD // 2)):
                for j in tiles:
                    if fresh is not None:
                        act.wait_ge(S["h_ready"], fresh + j + 1)
                    C.link(A(dst[:, 2 * j:2 * j + 2, :], h[:, 2 * j:2 * j + 2, :], ACT.Square), S["squares_ready"])

            def norm_hi(C, first, j):
                act.wait_ge(S["norm_ready"], first + j + 1)
                C.link(A(u_hi[:, 2 * j:2 * j + 2, :], u[:, 2 * j:2 * j + 2, :], ACT.Copy), S["u_hi_ready"])

            def guess(C, place, rows=P, weights=None):
                buf, y, sq = (a[0:rows] for a in roots[place])
                C.link(A(buf, y, ACT.Ln))
                if weights:
                    weights.more()
                C.link(A(buf, buf, ACT.Exp, scale=-0.5))
                C.link(A(sq, buf, ACT.Square), S["rstd_out"])
                if weights:
                    weights.more()

            def first_rstd(C):
                act.wait_ge(bank_full[0], 1)
                C.link(A(roots["next"][1], banks[0][:, 0:T], ACT.Identity, scale=1.0 / D, bias=K("eps")))
                guess(C, "next")

            def load_params(row):
                act.dma_start(par[:], params[bass.ds(row, 1)].rearrange("a p n -> p (a n)")).then_inc(params_in, 16)

            def rstd(C, B, names, place, scale, eps="eps", rows=P, width=512, weights=None):
                for name in names:
                    B.wait(act, name)
                for g, name in enumerate(names):
                    bank = B.wait(act, name)
                    C.link(A(roots[place][1][0:rows, g * width:(g + 1) * width], bank[0:rows, 0:width], ACT.Identity,
                             scale=scale[g] if isinstance(scale, tuple) else scale, bias=K(eps)[0:rows]))
                    B.release(act, name)
                if weights:
                    weights.more()
                guess(C, place, rows, weights)

            class HiParts:

                def __init__(self, ends, first, first_round):
                    self.ends, self.first, self.first_round, self.at = ends, first, first_round, 0

                def more(self):
                    self.upto("start", self.at + 1)

                def upto(self, name, lead=LEAD):
                    stop = lead if name == "start" else min(self.ends[name] + lead, max(self.ends.values()))
                    for q in range(self.at, stop):
                        c, o = q * PIECE // CHUNK, q * PIECE % CHUNK * P
                        if o == 0:
                            act.wait_ge(landed[c % RING], (self.first_round + (c // RING + 1)) * 16)
                        act.wait_ge(pieces_used, self.first + (RING * CHUNK // PIECE + q + 1 - HI_RING))
                        A(hi_ring[:, q % HI_RING, :], ring[:, c % RING, o:o + PIECE * P], ACT.Copy).then_inc(hi_written, 1)
                    self.at = max(self.at, stop)

            act.dma_start(par[:], params[0]).then_inc(params_in, 16)
            act.wait_ge(inputs_in, 48)
            C = Chain(act, S["act_chain"])
            nc.scalar.preload_act_table_set(LN_EXP)
            norm_squares(C, next_squares)
            first_rstd(C)
            layer_end(act, 0, False)
            with act.Fori(0, layers[0]) as l:
                C, B = Chain(act, S["act_chain"]), b1
                hi = HiParts(ends1, l * PIECES1, l * (CH1 // RING))
                for j in range(KD // 2):
                    norm_hi(C, 0, j)
                    hi.upto("start", j + 1)
                act.wait_ge(params_in, (l + 1) * 16)
                mu = PAR1.of(par, "mu")
                for i in range(14):
                    hi.upto(f"A{i // 2}")
                    bank = B.wait(act, f"A{i // 2}")
                    if i == 0:
                        act.wait_ge(S["pmu_used"], 1)
                    if i >= 4:
                        act.wait_ge(S["pmu_used"], 2 * (i // 2) - 1)
                    C.link(A(pmu[:, i % 4, 1:], bank[:, i % 2 * T:(i % 2 + 1) * T], ACT.Copy, scale=mu[:, i:i + 1]), S["pmu_ready"])
                act.wait_ge(S["pmu_used"], 15)
                C.link(A(tw[0:64, :], pa[0:64, 12, :], ACT.Tanh), S["rwkv_low_ready"])
                C.link(A(sg, pa[:, 13, :], ACT.Sigmoid), S["rwkv_low_ready"])
                hi.upto("Bq0")
                for n, o, z in (("Wup", einv, "w0"), ("Aup", av, "a0")):
                    for g in range(2):
                        bank = B.wait(act, f"{n}{g}")
                        for i in range(2):
                            j = 2 * g + i
                            C.link(A(v3(o, 4)[:, j, :], bank[:, i * T:(i + 1) * T], ACT.Sigmoid,
                                     bias=PAR1.of(par, z)[:, j:j + 1]), S["squash_ready"])
                        B.release(act, f"{n}{g}")
                for g in range(2):
                    bank = B.wait(act, f"Gup{g}")
                    C.link(A(gA[:, g * 512:(g + 1) * 512], bank[:, :], ACT.Copy), S["gA_ready"])
                    B.release(act, f"Gup{g}")
                hi.upto("Bq1")

                def take_queries(g):
                    bank = B.wait(act, f"Bq{g}")
                    C.link(A(bq[:, g * 512:(g + 1) * 512], bank[:, :], ACT.Copy))
                    B.release(act, f"Bq{g}")

                take_queries(0)
                act.wait_ge(S["kk_ready"], 1)
                C.link(A(bonus, kk, ACT.Square), S["kksq_ready"])
                nc.scalar.preload_act_table_set(LN_EXP)
                take_queries(1)
                act.wait_ge(S["cum_ready"], 1)
                C.link(A(emid, mid, ACT.Exp, scale=-KAPPA))
                C.link(A(eend, cc[:, :, P], ACT.Exp, scale=-KAPPA))
                C.link(A(ar[:, :, 0, :], cc[:, :, 0:P], ACT.Exp, scale=-KAPPA))
                C.link(A(ar[:, :, 1, :], cc[:, :, 1:P + 1], ACT.Exp, scale=-KAPPA))
                C.link(A(v3(einv, 8), cc[:, :, 1:P + 1], ACT.Exp, scale=KAPPA), S["decay_ready"])
                hi.upto("Bf0")
                act.wait_ge(S["rstd_in"], 1)
                guess(C, "keys")

                def take_raw(n, o, w):
                    hi.upto(n)
                    bank = B.wait(act, n)
                    C.link(A(craw[:, o:o + w, :].rearrange("p a t -> p (a t)"), bank[:, 0:w * T], ACT.Copy), S["raw_ready"])
                    B.release(act, n)

                take_raw("Cq0", 0, 2)
                take_raw("Cq1", 2, 2)
                take_raw("Ck", 7, 2)
                for c in range(2):
                    for n, o in (("Tb", btm), ("Tk", ktm), ("Tv", vtm)):
                        bank = B.wait(act, f"{n}{c}")
                        C.link(A(o[:, c, :], bank[:, :], ACT.Copy), S["tm_ready"])
                        B.release(act, f"{n}{c}")

                def level(c, k):
                    for q in range(2):
                        bank = B.wait(act, f"O{c}{k}{q}")
                        C.link(A(half_of(o1[:, 4 * q:4 * q + 4, :], k, 1), half_of(v3(bank[:, :], 4), k, 1), ACT.Copy), S["o1_ready"])
                        B.release(act, f"O{c}{k}{q}")

                def solve(c):
                    bank = B.wait(act, f"R{c}")
                    C.link(A(rs, bank[:, :], ACT.Copy), S["rhs_ready"])
                    B.release(act, f"R{c}")
                    bank = B.wait(act, f"SA{c}")
                    C.link(A(sa, bank[:, :], ACT.Copy), S["sa_ready"])
                    B.release(act, f"SA{c}")
                    bank = B.wait(act, f"Y{c}")
                    C.link(A(v3(ya, 4)[:, :, c * P:(c + 1) * P], v3(bank[:, :], 4), ACT.Copy), S["y_ready"])
                    B.release(act, f"Y{c}")

                def take_values(i):
                    b, tt, heads = ATT1[i]
                    bank = B.wait(act, f"CO{b}")
                    r, n, j0 = 64 * (heads[0] % 2), len(heads), heads[0] // 2
                    C.link(A(v3(yc, 4)[r:r + 64, j0:j0 + n, tt * P:(tt + 1) * P], v3(bank[r:r + 64, 0:n * P], n), ACT.Copy), S["yc_ready"])
                    B.release(act, f"CO{b}")

                def pair_decays(k):
                    act.wait_ge(S["pairs_in"], k + 1)
                    C.link(A(hE, hE, ACT.Exp), S["d_exp"])

                for t in range(NT):
                    hi.upto("Bi0")
                    bank = B.wait(act, f"Bi{t}")
                    C.link(A(bi[:, t, :], bank[:, :], ACT.Copy), S["bi_ready"])
                    B.release(act, f"Bi{t}")
                for k in range(1, LEVELS + 1):
                    if k < LEVELS:
                        level(0, k)
                    if k == 5:
                        hi.upto("Bg1", 0)
                    if 5 <= k <= 6:
                        g = k - 5
                        bank = B.wait(act, f"Bg{g}")
                        C.link(A(bsg[:, g * 512:(g + 1) * 512], bank[:, :], ACT.Copy))
                        B.release(act, f"Bg{g}")
                    if k == 2:
                        take_raw("Cqi", 4, 2)
                        act.wait_ge(S["hcol_in"], 1)
                        C.link(A(lbc, lbc, ACT.Exp), S["hcol_out"])
                    elif k == 3:
                        take_raw("Cki", 6, 1)
                        act.wait_ge(S["hcol_in"], 2)
                        nc.scalar.preload_act_table_set(LN)
                        C.link(A(lnA, lnA, ACT.Ln))
                        C.link(A(ln1m, ln1m, ACT.Ln), S["hcol_out"])
                    elif k == 4:
                        act.wait_ge(S["ls_in"], 1)
                        C.link(A(hE, bf, ACT.Abs))
                        C.link(A(hE, hE, ACT.Exp, scale=-1.0))
                        nc.scalar.preload_act_table_set(LN)
                        C.link(A(hE, hE, ACT.Ln, bias=1.0), S["ls_out"])
                    elif k == 5:
                        act.wait_ge(S["lse_in"], 1)
                        C.link(A(hks, hks, ACT.Exp))
                        C.link(A(hE, hE, ACT.Abs))
                        C.link(A(hE, hE, ACT.Exp, scale=-1.0))
                        nc.scalar.preload_act_table_set(LN)
                        C.link(A(hE, hE, ACT.Ln, bias=1.0), S["lse_out"])
                    elif k == 6:
                        act.wait_ge(S["cum_b"], 1)
                        b8 = v3(hb, 8)
                        for hd in range(4):
                            C.link(A(v3(hke, 4)[:, hd, :], b8[:, 2 * hd, :], ACT.Exp, scale=-1.0, bias=b8[:, 2 * hd, P - 1:P]))
                        C.link(A(v3(hqe, 4), b8[:, 1:8:2, :], ACT.Exp), S["d_exp"])
                    if k <= 3:
                        hi.upto(("Cqi", "Cki", "Cv")[k - 1])
                    elif k == 4:
                        hi.upto("Bg0", 0)
                solve(0)
                bank = B.wait(act, "HT")
                C.link(A(ketm, bank[:, :], ACT.Copy), S["ketm_ready"])
                B.release(act, "HT")
                bank = B.wait(act, "HS")
                C.link(A(hst.rearrange("p (a t) -> p a t", a=4), v3(bank[:, :], 4), ACT.Copy), S["hstate_ready"])
                B.release(act, "HS")
                def softmax(i):
                    b, tt, heads = ATT1[i]
                    w = (tt + 1) * P
                    act.wait_ge(S["probs_in"], i + 1)
                    for j in range(len(heads)):
                        C.link(A(lg[i % 2][:, j * w:(j + 1) * w], lg[i % 2][:, j * w:(j + 1) * w], ACT.Exp,
                                 bias=nmax[:, j:j + 1], accum_out=ssum[:, j:j + 1]))
                    act.sem_inc(S["logits_ready"], 1)

                def take_turned(i):
                    b, tt, heads = ATT1[i]
                    n = len(heads) * (tt + 1) * P
                    bank = B.wait(act, f"CP{b}")
                    C.link(A(pT[:, 0:n], bank[:, 0:n], ACT.Copy), S["pt_ready"])
                    B.release(act, f"CP{b}")

                for i in range(LEVELS - 1):
                    level(1, i + 1)
                    if i > 1:
                        take_values(i - 2)
                    pair_decays(i)
                    softmax(i)
                    if i:
                        take_turned(i - 1)
                pair_decays(LEVELS - 1)
                take_values(len(ATT1) - 2)
                take_turned(len(ATT1) - 1)
                take_values(len(ATT1) - 1)
                hi.upto(MERGE[0][0], 0)
                solve(1)
                C.link(A(bsg, bsg, ACT.Silu), S["bsg_ready"])
                for c in range(2):
                    bank = B.wait(act, f"HO{c}")
                    C.link(A(v3(yb, 4)[:, :, c * P:(c + 1) * P], v3(bank[:, :], 4), ACT.Copy))
                    C.link(A(v3(hE, 4)[:, :, c * P:(c + 1) * P], v3(bank[:, :], 4), ACT.Square), S["hosq_ready"])
                    B.release(act, f"HO{c}")
                nc.scalar.preload_act_table_set(LN_EXP)
                hi.upto(MERGE[0][0])
                act.wait_ge(S["fresh_norm"], 1)
                C.link(A(ysq, ya, ACT.Square), S["gsq_ready"])
                rstd(C, B, ["HN0", "HN1"], "hgrn", 1.0 / 128)
                hi.upto(MERGE[0][1], 0)
                rstd(C, B, ["GV0", "GV1"], "rwkv", 1.0 / 64, "gn_eps")
                for i, (n, _, _, _) in enumerate(MERGE):
                    hi.upto(MERGE[i + 1][0] if i + 1 < len(MERGE) else n)
                    bank = B.wait(act, n)
                    if i == 0:
                        act.wait_ge(S["yc_split"], 1)
                    if i >= 2:
                        act.wait_ge(S["gate_used"], i - 1)
                    C.link(A(gate_buf[i % 2], bank[:, :], ACT.Sigmoid), S["gate_ready"])
                    B.release(act, n)
                nc.scalar.preload_act_table_set(LN_EXP)
                for j in range(4):
                    hi.upto(f"WO{j}")
                    norm_squares(C, squares, 0, range(j - 1, j) if j else ())
                norm_squares(C, squares, 0, range(3, 4))
                rstd(C, B, ["norm2"], "ffn", 1.0 / D, width=T)
                for j in range(KD // 2):
                    norm_hi(C, KD // 2, j)
                for i in range(23):
                    if i < 22:
                        hi.upto(f"U{i}")
                        bank = B.wait(act, f"U{i}")
                        if i >= 4:
                            act.wait_ge(S["hidden_ready"], i - 3)
                        for j, t in ((0, i), (1, 22 + i)):
                            C.link(A(cb[i % 4][:, j, :], bank[:, j * T:(j + 1) * T], ACT.Identity,
                                     scale=PAR1.of(par, "conv_w2")[:, t:t + 1], bias=PAR1.of(par, "conv_b")[:, t:t + 1]))
                        act.sem_inc(S["conv_in"], 1)
                    if i:
                        act.wait_ge(S["conv_mid"], i)
                        C.link(A(cb[(i - 1) % 4][:, 0, :], cb[(i - 1) % 4][:, 0, :], ACT.Silu), S["conv_out"])
                nc.scalar.preload_act_table_set(LN_EXP)
                load_params(l + 1)
                for j in range(4):
                    hi.upto(f"D{j}")
                    norm_squares(C, next_squares, KD // 2, range(j - 1, j) if j else ())
                norm_squares(C, next_squares, KD // 2, range(3, 4))
                rstd(C, B, ["norm"], "next", 1.0 / D, width=T)
                hi.upto("end")
                layer_end(act, l + 1, False)

            C, B = Chain(act, S["act_chain"]), b2
            act.dma_start(t512.bitcast(I32)[0:1, T:2 * T], pos_in).then_inc(inputs_in, 16)
            act.wait_ge(S["cum_ready"], 1)
            C.link(A(tab, tab, ACT.Sin), S["decay_ready"])
            nc.scalar.preload_act_table_set(LN_EXP)
            norm_squares(C, next_squares, 0)
            first_rstd(C)
            layer_end(act, layers[0] + 1, False)

            if not layers[1]:
                act.dma_start(out, h[:]).then_inc(stored, 16)
                act.wait_ge(stored, 16)
                return
            with act.Fori(0, layers[1]) as l:
                C, B = Chain(act, S["act_chain"]), b2
                hi = HiParts(ends2, l * PIECES2 + layers[0] * PIECES1, l * (CH2 // RING) + layers[0] * (CH1 // RING))
                for j in range(KD // 2):
                    norm_hi(C, 0, j)
                    hi.upto("start", j + 1)
                act.wait_ge(params_in, (l + (layers[0] + 1)) * 16)
                def take_raw(n, o, w):
                    hi.upto(n)
                    bank = B.wait(act, n)
                    C.link(A(o.rearrange("p a t -> p (a t)"), bank[:, 0:w * T], ACT.Copy))
                    B.release(act, n)

                take_raw("cq0", cqk[:, 0:2, :], 2)
                take_raw("cq1", cqk[:, 2:3, :], 1)
                take_raw("ckv", cqk[:, 3:5, :], 2)
                hi.upto("kpe")
                bank = B.wait(act, "kpe")
                C.link(A(kpe[64:96, :], bank[64:96, 0:T], ACT.Copy))
                B.release(act, "kpe")
                C.link(A(sq2[:, 0:5, :].rearrange("p a t -> p (a t)"), cqk[:, :, :].rearrange("p a t -> p (a t)"), ACT.Square), S["latents_sq"])
                take_raw("aq", aqk[:, 0:2, :], 2)
                take_raw("ak", aqk[:, 2:4, :], 2)
                C.link(A(sqa, aqk[:, :, :].rearrange("p a t -> p (a t)"), ACT.Square), S["kksq_ready"])
                rstd(C, B, ["ncq", "nckv"], "latents", (1.0 / 384, 1.0 / 256), width=T, weights=hi)
                take_raw("av", avt, 2)
                rstd(C, B, ["nq", "nk"], "block qk", 1.0 / 64, weights=hi)
                cw = v3(PAR2.of(par, "conv_w"), 4)
                for i in range(4):
                    hi.upto(f"qk{i // 2}")
                    bank = B.wait(act, f"qk{i // 2}")
                    C.link(A(qkraw[:, i, :], bank[:, i % 2 * T:(i % 2 + 1) * T], ACT.Identity, scale=cw[:, 3, i:i + 1],
                             bias=PAR2.of(par, "conv_b")[:, i:i + 1]), S["conv_in"])
                for n, o in (("uq", 0), ("uk", 4)):
                    rows = MLA_D if n == "uq" else 64
                    for g in range(2):
                        hi.upto(f"{n}{g}")
                        bank = B.wait(act, f"{n}{g}")
                        C.link(A(lqk[0:rows, o + 2 * g:o + 2 * g + 2, :].rearrange("p a t -> p (a t)"), bank[0:rows, :], ACT.Copy))
                        B.release(act, f"{n}{g}")
                C.link(A(lqk[64:96, 4:8, :], spread(kpe, 4)[64:96], ACT.Copy))
                C.link(A(sq2[0:MLA_D].rearrange("p a t -> p (a t)"), lqk[0:MLA_D].rearrange("p a t -> p (a t)"), ACT.Square), S["lse_in"])
                take_raw("uv", lvt, 2)
                hi.upto("if", 0)
                rstd(C, B, ["nlq0", "nlq1", "nlk0", "nlk1"], "latent qk", 1.0 / MLA_D, rows=MLA_D, weights=hi)
                hi.upto("if")
                act.wait_ge(S["ls_in"], 1)
                fz = ifr[0:4, 4 * T:5 * T]
                C.link(A(fz, fz, ACT.Abs))
                C.link(A(fz, fz, ACT.Exp, scale=-1.0))
                nc.scalar.preload_act_table_set(LN)
                C.link(A(fz, fz, ACT.Ln, bias=1.0), S["hcol_out"])
                for t in range(NT):
                    hi.upto("mv0")
                    bank = B.wait(act, f"mv{t}")
                    C.link(A(mvt[:, t, :], bank[:, :], ACT.Copy), S["v_ready"])
                    B.release(act, f"mv{t}")
                for i in range(4):
                    act.wait_ge(S["conv_mid"], i + 1)
                    C.link(A(qkraw[:, i, :], qkraw[:, i, :], ACT.Silu), S["conv_out"])

                def softmax(tag, r):
                    b, tt, heads = ATT2[r]
                    w, n = (tt + 1) * P, "BM".index(tag)
                    act.wait_ge(S["probs_in"], 2 * r + n + 1)
                    for j in range(len(heads)):
                        C.link(A(lg2[n][:, j * w:(j + 1) * w], lg2[n][:, j * w:(j + 1) * w], ACT.Exp,
                                 bias=nmax[:, 4 * n + j:4 * n + j + 1], accum_out=ssum[:, 4 * n + j:4 * n + j + 1]))
                    act.sem_inc(S["logits_ready"], 1)

                def take_turned(tag, r):
                    b, tt, heads = ATT2[r]
                    n, cols_ = "BM".index(tag), len(heads) * (tt + 1) * P
                    bank = B.wait(act, f"{tag}P{b}")
                    C.link(A(pT2[n][:, 0:cols_], bank[:, 0:cols_], ACT.Copy), S["pt_ready"])
                    B.release(act, f"{tag}P{b}")

                def take_values(tag, r):
                    b, tt, heads = ATT2[r]
                    rows, o = slice(64 * (heads[0] % 2), 64 * (heads[0] % 2) + 64), 2 * "BM".index(tag)
                    bank = B.wait(act, f"{tag}O{b}")
                    C.link(A(mix[rows, o:o + 2, tt * P:(tt + 1) * P], v3(bank[rows, 0:2 * P], 2), ACT.Copy))
                    B.release(act, f"{tag}O{b}")

                def take_gate(r):
                    bank = B.wait(act, f"mo{r}")
                    C.link(A(mo[:, 2 * r:2 * r + 2, :].rearrange("p a t -> p (a t)"), bank[:, :], ACT.Copy))
                    B.release(act, f"mo{r}")

                hi.upto("mo0", 0)
                take_gate(0)
                for r in range(len(ATT2) + 1):
                    if r == len(ATT2):
                        nc.scalar.preload_act_table_set(LN_EXP)
                    for tag in "BM" * (r > 0):
                        take_turned(tag, r - 1)
                    if r == 1:
                        hi.upto(f"mo{r}", 0)
                    elif r == 3:
                        hi.upto("mo1")
                    if r < len(ATT2):
                        softmax("B", r)
                        softmax("M", r)
                        bank = B.wait(act, f"gb{r}")
                        if r:
                            act.wait_ge(S["dn_ready"], r)
                        C.link(A(em, bank[:, T:2 * T], ACT.Exp), S["em_ready"])
                        act.wait_ge(S["pairs_in"], r + 1)
                        C.link(A(dT, dT, ACT.Exp, scale=-1.0), S["d_exp"])
                    if r == 1:
                        take_gate(r)
                    for tag in "BM" * (r > 0):
                        take_values(tag, r - 1)
                for o in (0, 2):
                    C.link(A(v3(sqa, 4)[:, o:o + 2, :], mix[:, o:o + 2, :], ACT.Square), S["gsq_ready"])
                rstd(C, B, ["bn"], "block", 1.0 / 64)
                act.wait_ge(S["dn_ready"], 4)
                C.link(A(sqb, mix[:, 4:8, :].rearrange("p a t -> p (a t)"), ACT.Square), S["hosq_ready"])
                rstd(C, B, ["ln"], "latent", 1.0 / 64)
                rstd(C, B, ["mn0", "mn1"], "mlstm", 1.0 / 128)
                C.link(A(mo.rearrange("p a t -> p (a t)"), mo.rearrange("p a t -> p (a t)"), ACT.Sigmoid), S["bsg_ready"])
                nc.scalar.preload_act_table_set(LN_EXP)
                for j in range(4):
                    hi.upto(f"WO{j} attention")
                for j in range(4):
                    hi.upto(f"WO{j}")
                    norm_squares(C, squares, 0, range(j - 1, j) if j else ())
                norm_squares(C, squares, 0, range(3, 4))
                rstd(C, B, ["norm2"], "mlp", 1.0 / D, width=T)
                for j in range(KD // 2):
                    norm_hi(C, KD // 2, j)
                for i in range(16):
                    hi.upto(f"U{i}")
                    bank = B.wait(act, f"U{i}")
                    C.link(A(hidden[:, 2 * i:2 * i + 2, :].rearrange("p a t -> p (a t)"), bank[:, :], ACT.Relu), S["conv_in"])
                    B.release(act, f"U{i}")
                load_params(l + (layers[0] + 1))
                for j in range(4):
                    hi.upto(f"D{j}")
                    norm_squares(C, next_squares, KD // 2, range(j - 1, j) if j else ())
                norm_squares(C, next_squares, KD // 2, range(3, 4))
                rstd(C, B, ["norm"], "next", 1.0 / D, width=T)
                hi.upto("end")
                layer_end(act, l + (layers[0] + 2), False)
            act.dma_start(out, h[:]).then_inc(stored, 16)
            act.wait_ge(stored, 16)

        @block.vector
        def _(dve):
            V = nc.vector

            def split(C, x_, hi, lo, sig=None):
                C.link(V.tensor_copy(hi, x_))
                C.link(V.tensor_tensor(lo, x_, hi.bitcast(F32), ALU.subtract), sig)

            def refine(C, place, n, rows=P):
                buf, y, sq = (a[0:rows] for a in roots[place])
                dve.wait_ge(S["rstd_out"], n)
                C.link(V.scalar_tensor_tensor(sq, sq, -0.5, y, ALU.mult, ALU.mult))
                C.link(V.scalar_tensor_tensor(buf, sq, 1.5, buf, ALU.add, ALU.mult))

            def norm(C, gain, dst, buf):
                for k in range(KD):
                    ins = V.scalar_tensor_tensor(dst[:, k, :], h[:, k, :], gain[:, k:k + 1], buf, ALU.mult, ALU.mult)
                    if k % 2:
                        C.link(ins, S["h_ready"])

            def norm_parts(C, gain, buf, first):
                for j in range(KD // 2 + 1):
                    if j < KD // 2:
                        for k in (2 * j, 2 * j + 1):
                            ins = V.scalar_tensor_tensor(u[:, k, :], h[:, k, :], gain[:, k:k + 1], buf, ALU.mult, ALU.mult)
                        C.link(ins, S["norm_ready"])
                    if j:
                        two = slice(2 * j - 2, 2 * j)
                        dve.wait_ge(S["u_hi_ready"], first + j)
                        C.link(V.tensor_tensor(u_lo[:, two, :], u[:, two, :], u_hi[:, two, :].bitcast(F32), ALU.subtract), S["u_ready"])

            def rope(C, B, name, x_, n, cos, sin, t, rows=P):
                bank = B.wait(dve, name)
                V.tensor_tensor(t, v3(bank[0:rows, 0:n * T], n), spread(sin, n), ALU.mult).then_inc(B.free_of(name), 1)
                C.link(V.tensor_tensor(x_, x_, spread(cos, n), ALU.mult))
                C.link(V.tensor_tensor(x_, x_, t, ALU.add))

            dve.wait_ge(inputs_in, 48)
            C = Chain(dve, ready)
            C.link(V.tensor_copy(msk[:], mask_in))
            C = Chain(dve, S["dve_chain"])
            refine(C, "next", 1)
            layer_end(dve, 0, True)
            with dve.Fori(0, layers[0]) as l:
                C, B = Chain(dve, S["dve_chain"]), b1
                dve.wait_ge(params_in, (l + 1) * 16)
                p = lambda n: PAR1.of(par, n)
                C.link(V.tensor_scalar(omu, p("mu"), -1.0, 1.0, ALU.mult, ALU.add))
                C.link(V.memset(pmu[:, :, 0:1], 0.0), S["pmu_used"])
                C.link(V.memset(cc[:, :, 0:1], 0.0))
                norm_parts(C, p("g_mix"), rn[:], 0)
                for i in range(14):
                    dve.wait_ge(S["pmu_ready"], 2 * (i // 2) + 2)
                    bank = B.wait(dve, f"A{i // 2}")
                    C.link(V.scalar_tensor_tensor(pa[:, i, :], bank[:, i % 2 * T:(i % 2 + 1) * T], omu[:, i:i + 1],
                                                  pmu[:, i % 4, 0:T], ALU.mult, ALU.add), S["pmu_used"])
                    if i % 2:
                        B.release(dve, f"A{i // 2}")
                for j in range(4):
                    C.link(V.tensor_scalar(v3(kk, 4)[:, j, :], pa[:, 4 + j, :], p("k_k")[:, j:j + 1], None, ALU.mult))
                dve.sem_inc(S["kk_ready"], 1)
                dve.wait_ge(S["squash_ready"], 4)
                for i in range(8):
                    C.link(V.tensor_tensor_scan(cc[:, i, 1:P + 1], ones, v3(einv, 8)[:, i, :], 0.0, ALU.mult, ALU.add))
                C.link(V.tensor_copy(mid, cc[:, :, 64]))
                C.link(V.tensor_tensor(cc, cc, along(mid, P + 1), ALU.subtract), S["cum_ready"])
                dve.wait_ge(S["squash_ready"], 8)
                for j in range(4):
                    C.link(V.tensor_scalar(v3(kmod, 4)[:, j, :], v3(av, 4)[:, j, :], -1.0, p("k_a")[:, j:j + 1], ALU.add, ALU.mult))
                k_flat = pa[:, 4:8, :].rearrange("p a t -> p (a t)")
                C.link(V.scalar_tensor_tensor(kmod, kmod, 1.0, k_flat, ALU.add, ALU.mult))
                for g in range(2):
                    B.wait(dve, f"KK{g}")
                for g in range(2):
                    bank = B.wait(dve, f"KK{g}")
                    C.link(V.tensor_scalar(bonus[:, g * 512:(g + 1) * 512], bank[:, :], 1e-24, None, ALU.max))
                    B.release(dve, f"KK{g}")
                dve.sem_inc(S["rstd_in"], 1)
                refine(C, "keys", 1)
                C.link(V.tensor_tensor(kk, kk, roots["keys"][0], ALU.mult))
                for j in range(4):
                    C.link(V.scalar_tensor_tensor(v3(bonus, 4)[:, j, :], pa[:, j, :], p("r_k")[:, j:j + 1],
                                                  v3(kmod, 4)[:, j, :], ALU.mult, ALU.mult))
                dve.sem_inc(S["bonus_in"], 1)
                dve.wait_ge(S["decay_ready"], 1)
                C.link(V.scalar_tensor_tensor(ar[:, :, 0, :], v3(kk, 8), -1.0, ar[:, :, 0, :], ALU.mult, ALU.mult))
                r8 = pa[:, 0:4, :].rearrange("p a (c t) -> p (a c) t", c=2)
                C.link(V.tensor_tensor(ar[:, :, 1, :], r8, ar[:, :, 1, :], ALU.mult))
                C.link(V.tensor_tensor(av, av, kk, ALU.mult))
                C.link(V.tensor_tensor(av, av, einv, ALU.mult))
                C.link(V.tensor_tensor(einv, einv, kmod, ALU.mult), S["rwkv_ops_ready"])
                for g in range(2):
                    bank = B.wait(dve, f"Bf{g}")
                    C.link(V.tensor_copy(bf[:, g * 512:(g + 1) * 512], bank[:, :]))
                    B.release(dve, f"Bf{g}")
                for g in range(2):
                    B.wait(dve, f"BON{g}")
                for g in range(2):
                    bank = B.wait(dve, f"BON{g}")
                    vv = pa[:, 8 + 2 * g:10 + 2 * g, :].rearrange("p a t -> p (a t)")
                    C.link(V.tensor_tensor(bonus[:, g * 512:(g + 1) * 512], bank[:, :], vv, ALU.mult))
                    B.release(dve, f"BON{g}")
                def scores(c):
                    if c:
                        B.wait(dve, "ST")
                    for q in range(2):
                        V.tensor_copy(xx[:, 4 * q:4 * q + 4, :], spread(ident, 4))
                        C.link(V.tensor_copy(zz[:, 4 * q:4 * q + 4, :], spread(ident, 4)))
                    for q in range(2):
                        bank = B.wait(dve, f"N{c}{q}")
                        C.link(V.tensor_tensor(nn[:, 4 * q:4 * q + 4, :], v3(bank[:, :], 4), spread(K("lower"), 4), ALU.mult))
                        B.release(dve, f"N{c}{q}")
                        V.copy_predicated(zz[:, 4 * q:4 * q + 4, :], spread(lowm[:, 0, :], 4), nn[:, 4 * q:4 * q + 4, :])
                    for q in range(2):
                        for hd in HALVES[q]:
                            bank = B.wait(dve, f"S{c}{hd}")
                            ins = V.tensor_tensor(sc[:, hd].rearrange("p (b a) t -> p b (a t)", b=2), v3(bank[:, :], 2), spread(K("pairmask"), 2), ALU.mult)
                            if hd != HALVES[q][-1]:
                                ins.then_inc(B.free_of(f"S{c}{hd}"), 1)
                        C.link(ins)
                        B.release(dve, f"S{c}{hd}")
                        C.link(V.copy_predicated(xx[:, 4 * q:4 * q + 4, :], spread(upm[:, 0, :], 4), sc[:, q:8:2, 0, :]), S["xz_ready"])

                def spread_half(masks, k, side, rows):
                    return half_of(masks[:, k:k + 1, :], k, side).to_broadcast([P, rows, 64 >> k, 1 << k])

                def level(c, k, q):
                    hs = slice(4 * q, 4 * q + 4)
                    if k < LEVELS - 1:
                        B.wait(dve, f"Z{c}{k}{q}")
                    bank = B.wait(dve, f"X{c}{k}{q}")
                    ins = V.copy_predicated(half_of(xx[:, hs, :], k, 1), spread_half(upm, k, 1, 4), half_of(v3(bank[:, :], 4), k, 1))
                    if k < LEVELS - 1:
                        ins.then_inc(B.free_of(f"X{c}{k}{q}"), 1)
                        bank = B.wait(dve, f"Z{c}{k}{q}")
                        ins = V.copy_predicated(half_of(zz[:, hs, :], k, 0), spread_half(lowm, k, 0, 4), half_of(v3(bank[:, :], 4), k, 0))
                    C.link(ins, S["xz_ready"])
                    B.release(dve, f"{'X' if k == LEVELS - 1 else 'Z'}{c}{k}{q}")

                def state():
                    bank = B.wait(dve, "ST")
                    e8 = eend.rearrange("p (j c) -> p j c", c=2)
                    m8_ = emid.rearrange("p (j c) -> p j c", c=2)
                    C.link(V.memset(st, 0.0))
                    for j in range(4):
                        for r in (0, 64):
                            C.link(V.tensor_scalar(st[r:r + 64, j, r:r + 64], bank[r:r + 64, j * 64:(j + 1) * 64],
                                                   e8[r:r + 64, j, 0:1], m8_[r:r + 64, j, 1:2], ALU.mult, ALU.mult))
                    dve.sem_inc(S["state_ready"], 1)
                    B.release(dve, "ST")

                def halves(ap, m):
                    return ap.rearrange("p (n a t) -> p n a t", a=2, t=m)

                def pair_decays(k):
                    m = 1 << k
                    b_, e_ = halves(hb, m), halves(hE, m)
                    ref = b_[:, :, 0, m - 1:m].to_broadcast([P, 1024 // (2 * m), m])
                    V.tensor_tensor(e_[:, :, 0, :], ref, b_[:, :, 0, :], ALU.subtract)
                    C.link(V.tensor_tensor(e_[:, :, 1, :], b_[:, :, 1, :], ref, ALU.subtract), S["pairs_in"])

                def pair_operands(k):
                    m = 1 << k
                    e_, o_ = halves(hE, m), halves(hqk, m)
                    dve.wait_ge(S["d_exp"], k + 2)
                    V.tensor_tensor(o_[:, :, 0, :], halves(hks, m)[:, :, 0, :], e_[:, :, 0, :], ALU.mult)
                    C.link(V.tensor_tensor(o_[:, :, 1, :], halves(bq, m)[:, :, 1, :], e_[:, :, 1, :], ALU.mult), S["pairs_ready"])

                def take_pairs(k):
                    for c in range(2):
                        bank = B.wait(dve, f"H{k}{c}")
                        o, i = v3(hsc, 8)[:, c:8:2, :], v3(bank[:, :], 4)
                        if k < LEVELS:
                            ins = V.copy_predicated(half_of(o, k, 1), spread_half(upm, k, 1, 4), half_of(i, k, 1))
                        else:
                            ins = V.copy_predicated(o, spread(diagm, 4), i)
                        if k not in (0, LEVELS - 1, LEVELS):
                            ins.then_inc(B.free_of(f"H{k}{c}"), 1)
                        else:
                            C.link(ins)
                            B.release(dve, f"H{k}{c}")

                def rotate(name, at, n):
                    rope(C, B, name, craw[:, at:at + n, :], n, K("cos"), K("sin"), scr[:, 0:n, :])

                def index_scores(tt):
                    w = (tt + 1) * P
                    for n, _, heads in INDEX[2 * tt:2 * tt + 2]:
                        bank = B.wait(dve, n)
                        for i, hd in enumerate(heads):
                            o = scr[:, tt, 0:w] if hd == 0 else tmp[:, 0:w]
                            C.link(V.tensor_scalar(o, bank[:, i * w:(i + 1) * w], 0.0, wi[:, 4 * tt + hd:4 * tt + hd + 1], ALU.max, ALU.mult))
                            if hd:
                                C.link(V.tensor_tensor(scr[:, tt, 0:w], scr[:, tt, 0:w], o, ALU.add))
                        B.release(dve, n)
                    C.link(V.tensor_tensor(work[tt][:, 0:w], scr[:, tt, 0:w], K("cneg")[:, T - w:T], ALU.add))

                def take_best(tt, rounds):
                    w = (tt + 1) * P
                    for _ in range(rounds):
                        C.link(V.max(m8, work[tt][:, 0:w]))
                        C.link(V.match_replace(work[tt][:, 0:w], m8, work[tt][:, 0:w], TAKEN))

                def best_mask(tt):
                    w = (tt + 1) * P
                    C.link(V.tensor_scalar(amask[:, tt, 0:w], work[tt][:, 0:w], 2 * NEG, None, ALU.is_le))
                    C.link(V.tensor_scalar(amask[:, tt, 0:w], amask[:, tt, 0:w], -1.0, -NEG, ALU.add, ALU.mult))
                    C.link(V.tensor_tensor(amask[:, tt, 0:w], amask[:, tt, 0:w], K("cneg")[:, T - w:T], ALU.min))

                def masked_logits(i):
                    b, tt, heads = ATT1[i]
                    w, n = (tt + 1) * P, len(heads)
                    bank = B.wait(dve, f"CL{b}")
                    if i >= 2:
                        B.wait(dve, f"CP{ATT1[i - 2][0]}")
                    x_ = v3(lg[i % 2][:, 0:n * w], n)
                    C.link(V.scalar_tensor_tensor(x_, v3(bank[:, 0:n * w], n), 0.125, spread(amask[:, tt, 0:w], n), ALU.mult, ALU.add))
                    B.release(dve, f"CL{b}")
                    C.link(V.tensor_reduce(nmax[:, 0:n], x_, AX_X, ALU.max, negate=True), S["probs_in"])

                def probabilities(i):
                    b, tt, heads = ATT1[i]
                    w, n = (tt + 1) * P, len(heads)
                    dve.wait_ge(S["logits_ready"], i + 1)
                    C.link(V.reciprocal(ssum[:, 0:n], ssum[:, 0:n]))
                    x_ = v3(lg[i % 2][:, 0:n * w], n)
                    C.link(V.tensor_tensor(x_, x_, along(ssum[:, 0:n], w), ALU.mult), S["probs_ready"])

                half_rounds = TOPK // TOP_STEP // 2
                scores(0)
                for k in range(1, LEVELS):
                    level(0, k, 0)
                    level(0, k, 1)
                    if k == 1:
                        C.link(V.tensor_tensor(lbc, p("lb0"), p("lb1"), ALU.subtract), S["hcol_in"])
                        rotate("Rq0", 0, 2)
                        rotate("Rq1", 2, 2)
                    elif k == 2:
                        dve.wait_ge(S["hcol_out"], 1)
                        C.link(V.tensor_scalar(lbc, lbc, 1e30, 1.0, ALU.min, ALU.add))
                        C.link(V.reciprocal(lbc, lbc))
                        C.link(V.tensor_tensor(lbc, lbc, p("not_first"), ALU.mult))
                        C.link(V.tensor_scalar(isz, lbc, 0.0, NEG, ALU.is_le, ALU.mult))
                        C.link(V.tensor_scalar(omlb, lbc, -1.0, 1.0, ALU.mult, ALU.add))
                        C.link(V.tensor_scalar(lnA, lbc, 2.0 ** -64, None, ALU.max))
                        C.link(V.tensor_scalar(ln1m, omlb, 2.0 ** -64, None, ALU.max), S["hcol_in"])
                        rotate("Rk", 7, 2)
                    elif k == 3:
                        dve.wait_ge(S["hcol_out"], 2)
                        C.link(V.tensor_tensor(lnA, lnA, isz, ALU.add))
                        C.link(V.tensor_scalar(hls, bf, 0.0, None, ALU.min), S["ls_in"])
                        bank = B.wait(dve, "Cv")
                        both = v3(bank[:, 0:2 * (P + 4)], 2)
                        C.link(V.tensor_copy(cvt, both[:, :, 0:P]))
                        C.link(V.tensor_scalar(v3(wi, 2), both[:, :, P:P + 4], 1.0 / 16, None, ALU.mult))
                        B.release(dve, "Cv")
                        rotate("Rqi", 4, 2)
                        rotate("Rki", 6, 1)
                        dve.sem_inc(S["rope_ready"], 1)
                    elif k == 4:
                        dve.wait_ge(S["ls_out"], 1)
                        C.link(V.tensor_tensor(hls, hls, hE, ALU.subtract))
                        C.link(V.tensor_tensor(hks, hls, bf, ALU.subtract))
                        for j in range(4):
                            s_ = v3(hls, 4)[:, j, :]
                            C.link(V.tensor_scalar(v3(hE, 4)[:, j, :], s_, ln1m[:, j:j + 1], lnA[:, j:j + 1], ALU.add, ALU.subtract))
                            C.link(V.tensor_scalar(s_, s_, ln1m[:, j:j + 1], lnA[:, j:j + 1], ALU.add, ALU.max))
                        dve.sem_inc(S["lse_in"], 1)
                        index_scores(0)
                    elif k == 5:
                        index_scores(1)
                        dve.wait_ge(S["lse_out"], 1)
                        C.link(V.tensor_tensor(hls, hls, hE, ALU.add))
                        for j in range(4):
                            C.link(V.tensor_scalar(v3(hks, 4)[:, j, :], v3(hks, 4)[:, j, :], omlb[:, j:j + 1], None, ALU.mult))
                        for i in range(8):
                            C.link(V.tensor_tensor_scan(v3(hb, 8)[:, i, :], ones, v3(hls, 8)[:, i, :], 0.0, ALU.mult, ALU.add))
                        dve.sem_inc(S["cum_b"], 1)
                        take_best(0, TOPK // TOP_STEP)
                    else:
                        dve.wait_ge(S["d_exp"], 1)
                        C.link(V.tensor_tensor(v3(hke, 4), v3(hke, 4), v3(hks, 8)[:, 0:8:2, :], ALU.mult), S["hk_ready"])
                        C.link(V.tensor_tensor(v3(hqe, 4), v3(hqe, 4), v3(bq, 8)[:, 1:8:2, :], ALU.mult), S["hqe_ready"])
                        C.link(V.memset(hsc, 0.0))
                best_mask(0)
                take_best(1, half_rounds)
                state()
                scores(1)
                for k in range(1, LEVELS):
                    i = k - 1
                    pair_decays(i)
                    masked_logits(i)
                    level(1, k, 0)
                    level(1, k, 1)
                    take_pairs((i - 1) % (LEVELS + 1))
                    pair_operands(i)
                    if i == LEVELS - 2:
                        pair_decays(LEVELS - 1)
                    probabilities(i)
                    if k == 1:
                        take_best(1, half_rounds)
                        best_mask(1)
                take_pairs(LEVELS - 2)
                pair_operands(LEVELS - 1)
                take_pairs(LEVELS - 1)
                dve.sem_inc(S["hsc_ready"], 1)
                dve.wait_ge(S["yc_ready"], len(ATT1))
                split(C, yc, yc_hi, yc_lo, S["yc_split"])
                for g in range(2):
                    B.wait(dve, f"GM{g}")
                for g in range(2):
                    bank = B.wait(dve, f"GM{g}")
                    y_ = ya[:, g * 512:(g + 1) * 512]
                    C.link(V.scalar_tensor_tensor(y_, bank[:, :], -1.0 / 64, y_, ALU.mult, ALU.add))
                    B.release(dve, f"GM{g}")
                dve.sem_inc(S["fresh_norm"], 1)
                refine(C, "hgrn", 2)
                C.link(V.tensor_tensor(yb, yb, hE, ALU.mult))
                dve.wait_ge(S["bsg_ready"], 1)
                for j in range(4):
                    C.link(V.scalar_tensor_tensor(v3(yb, 4)[:, j, :], v3(yb, 4)[:, j, :], p("b_gn")[:, j:j + 1], v3(bsg, 4)[:, j, :], ALU.mult, ALU.mult))
                split(C, yb, yb_hi, yb_lo, S["yb_ready"])
                refine(C, "rwkv", 3)
                C.link(V.tensor_tensor(ya, ya, ysq, ALU.mult))
                for j in range(4):
                    C.link(V.tensor_scalar(v3(ya, 4)[:, j, :], v3(ya, 4)[:, j, :], p("gn_g")[:, j:j + 1], p("gn_b")[:, j:j + 1], ALU.mult, ALU.add))
                C.link(V.tensor_tensor(ya, ya, bonus, ALU.add))
                dve.wait_ge(S["gA_ready"], 2)
                C.link(V.tensor_tensor(ya, ya, gA, ALU.mult))
                split(C, ya, ya_hi, ya_lo, S["ya_ready"])
                for i, (_, output, _, j) in enumerate(MERGE):
                    first, last = i < 4, i >= 8
                    bank = B.wait(dve, output)
                    dve.wait_ge(S["gate_ready"], i + 1)
                    o = merged[:, j * 512:(j + 1) * 512]
                    C.link(V.tensor_tensor(o if first else mtmp, bank[:, :], gate_buf[i % 2], ALU.mult), S["gate_used"])
                    B.release(dve, output)
                    if not first:
                        C.link(V.tensor_tensor(o, o, mtmp, ALU.add))
                    if last:
                        split(C, o, merged_hi[:, j * 512:(j + 1) * 512], merged_lo[:, j * 512:(j + 1) * 512], S["merged_ready"])
                for j in range(4):
                    bank = B.wait(dve, f"WO{j}")
                    o = h[:, 2 * j:2 * j + 2, :].rearrange("p a t -> p (a t)")
                    C.link(V.tensor_tensor(o, o, bank[:, :], ALU.add), S["h_ready"])
                    B.release(dve, f"WO{j}")
                refine(C, "ffn", 4)
                norm_parts(C, p("g_ffn"), tmp, KD // 2)
                for i in range(23):
                    if i < 22:
                        bank = B.wait(dve, f"U{i}")
                        dve.wait_ge(S["conv_in"], i + 1)
                        for d, w_, sig in ((1, "conv_w1", None), (2, "conv_w0", S["conv_mid"])):
                            for j, t in ((0, i), (1, 22 + i)):
                                o = cb[i % 4][:, j, d:]
                                ins = V.scalar_tensor_tensor(o, bank[:, j * T:(j + 1) * T - d], p(w_)[:, t:t + 1], o, ALU.mult, ALU.add)
                            C.link(ins, sig)
                        B.release(dve, f"U{i}")
                    if i:
                        dve.wait_ge(S["conv_out"], i)
                        c_ = cb[(i - 1) % 4]
                        C.link(V.tensor_tensor(hidden[:, i - 1, :], c_[:, 0, :], c_[:, 1, :], ALU.mult))
                        split(C, hidden[:, i - 1, :], hidden_hi[:, i - 1, :], hidden_lo[:, i - 1, :], S["hidden_ready"])
                for j in range(4):
                    bank = B.wait(dve, f"D{j}")
                    o = h[:, 2 * j:2 * j + 2, :].rearrange("p a t -> p (a t)")
                    C.link(V.tensor_tensor(o, o, bank[:, :], ALU.add), S["h_ready"])
                    B.release(dve, f"D{j}")
                refine(C, "next", 5)
                layer_end(dve, l + 1, True)

            C, B = Chain(dve, S["dve_chain"]), b2
            dve.wait_ge(inputs_in, 64)
            C.link(V.tensor_copy(t512[0:1, 0:T], t512.bitcast(I32)[0:1, T:2 * T]), S["ready"])
            dve.wait_ge(bank_full[1], 1)
            two_pi = 2.0 * np.pi
            angle_hi = float(np.float32(6.28125))
            angle_lo = float(np.float32(two_pi - 6.28125))
            rest = float(two_pi - 6.28125 - np.float64(np.float32(two_pi - 6.28125)))
            turns = sq2.rearrange("p a t -> p (a t)")[:, 0:4 * T]
            tab4, turns4 = (t_.rearrange("p (f c t) -> p f c t", f=2, c=2) for t_ in (tab, turns))
            for f_ in range(2):
                C.link(V.tensor_scalar(tab4[:, f_], spread(banks[1][:, 0:T], 2), K("freq")[:, f_:f_ + 1], None, ALU.mult))
            for c, quarter in ((0, 0.25), (1, 0.0)):
                C.link(V.tensor_scalar(turns4[:, :, c], tab4[:, :, c], 1.0 / two_pi, quarter, ALU.mult, ALU.add))
            C.link(V.tensor_scalar(turns, turns, 12582912.0, None, ALU.add))
            C.link(V.tensor_scalar(turns, turns, -12582912.0, None, ALU.add))
            for part_ in (angle_hi, angle_lo, rest):
                C.link(V.scalar_tensor_tensor(tab, turns, -part_, tab, ALU.mult, ALU.add))
            C.link(V.tensor_scalar(tab4[:, :, 0], tab4[:, :, 0], np.pi / 2, None, ALU.add))
            C.link(V.tensor_scalar(tab, tab, 3.1415925, -3.1415925, ALU.min, ALU.max), S["cum_ready"])
            dve.wait_ge(params_in, (layers[0] + 1) * 16)
            norm(C, PAR2.of(par, "g_final"), h, rn[:])
            refine(C, "next", 1)
            dve.wait_ge(S["decay_ready"], 1)
            layer_end(dve, layers[0] + 1, True)

            if not layers[1]:
                return
            with dve.Fori(0, layers[1]) as l:
                C, B = Chain(dve, S["dve_chain"]), b2
                dve.wait_ge(params_in, (l + (layers[0] + 1)) * 16)
                p = lambda n: PAR2.of(par, n)
                norm_parts(C, p("g_mix"), rn[:], 0)
                refine(C, "latents", 1)
                for i in range(5):
                    g_ = p("g_cq")[:, i:i + 1] if i < 3 else p("g_ckv")[:, i - 3:i - 2]
                    C.link(V.scalar_tensor_tensor(cqk[:, i, :], cqk[:, i, :], g_, lrs[:, (i // 3) * T:(i // 3 + 1) * T], ALU.mult, ALU.mult))
                split(C, cqk, cqk_hi, cqk_lo, S["latents_ready"])
                refine(C, "block qk", 2)
                for i, n in ((0, "g_mq"), (2, "g_mk")):
                    x_ = aqk[:, i:i + 2, :].rearrange("p a t -> p (a t)")
                    C.link(V.scalar_tensor_tensor(x_, x_, p(n), sqa[:, i * T:(i + 2) * T], ALU.mult, ALU.mult))
                dve.sem_inc(S["kk_ready"], 1)
                cw = v3(p("conv_w"), 4)
                for i in range(4):
                    bank = B.wait(dve, f"qk{i // 2}")
                    dve.wait_ge(S["conv_in"], 2 * (i // 2) + 2)
                    x_ = bank[:, i % 2 * T:(i % 2 + 1) * T]
                    for d in (1, 2, 3):
                        o = qkraw[:, i, d:]
                        C.link(V.scalar_tensor_tensor(o, x_[:, 0:T - d], cw[:, 3 - d, i:i + 1], o, ALU.mult, ALU.add),
                               S["conv_mid"] if d == 3 else None)
                    if i % 2:
                        B.release(dve, f"qk{i // 2}")
                t2 = v3(t512, 2)
                rope(C, B, "rq", aqk[:, 0:2, :], 2, tabs[0], tabs[1], t2)
                rope(C, B, "rk", aqk[:, 2:4, :], 2, tabs[0], tabs[1], t2)
                dve.sem_inc(S["rope_ready"], 1)
                bank = B.wait(dve, "if")
                a_, f_, g_, e_, z_, w_ = (ifr[0:4, i * T:(i + 1) * T] for i in range(6))
                C.link(V.tensor_scalar(a_, bank[0:4, 0:T], p("b_i")[0:4], None, ALU.add))
                C.link(V.tensor_scalar(f_, bank[0:4, T:2 * T], p("b_f")[0:4], None, ALU.add))
                B.release(dve, "if")
                C.link(V.tensor_copy(z_, f_), S["ls_in"])
                C.link(V.tensor_scalar(f_, f_, 0.0, None, ALU.min))
                refine(C, "latent qk", 3, MLA_D)
                s2f = sq2.rearrange("p a t -> p (a t)")
                for i, n in ((0, "g_lq"), (4, "g_lk")):
                    x_ = lqk[0:MLA_D, i:i + 4, :].rearrange("p a t -> p (a t)")
                    C.link(V.scalar_tensor_tensor(x_, x_, p(n)[0:MLA_D], s2f[0:MLA_D, i * T:(i + 4) * T], ALU.mult, ALU.mult))
                dve.sem_inc(S["lse_out"], 1)
                dve.wait_ge(S["hcol_out"], 1)
                C.link(V.tensor_tensor(f_, z_, f_, ALU.subtract))
                C.link(V.memset(w_, 1.0))
                C.link(V.tensor_tensor_scan(z_, w_, f_, 0.0, ALU.mult, ALU.add))
                C.link(V.tensor_tensor(a_, a_, z_, ALU.add))
                C.link(V.tensor_tensor_scan(g_, a_, a_, 0.0, ALU.max, ALU.max))
                C.link(V.tensor_tensor(e_, z_, g_, ALU.subtract), S["d_diff"])
                for g, n in enumerate(("rlq0", "rlq1", "rlk0", "rlk1")):
                    rope(C, B, n, lqk[0:MLA_D, 2 * g:2 * g + 2, :], 2, tabs[2][0:MLA_D], tabs[3][0:MLA_D], t2[0:MLA_D], MLA_D)
                dve.sem_inc(S["rope_ready"], 1)
                bank = B.wait(dve, "acol")
                C.link(V.tensor_copy(acol.rearrange("p a t -> p (a t)"), bank[:, 0:8]))
                B.release(dve, "acol")

                def masked_logits(tag, r):
                    b, tt, heads = ATT2[r]
                    w, m, n = (tt + 1) * P, len(heads), "BM".index(tag)
                    bank = B.wait(dve, f"{tag}L{b}")
                    if r:
                        B.wait(dve, f"{tag}P{ATT2[r - 1][0]}")
                    x_ = v3(lg2[n][:, 0:m * w], m)
                    C.link(V.scalar_tensor_tensor(x_, v3(bank[:, 0:m * w], m), 0.125 if tag == "B" else float(MLA_D) ** -0.5,
                                                  spread(K("cneg")[:, T - w:T], m), ALU.mult, ALU.add))
                    B.release(dve, f"{tag}L{b}")
                    C.link(V.tensor_reduce(nmax[:, 4 * n:4 * n + m], x_, AX_X, ALU.max, negate=True), S["probs_in"])

                def probabilities(tag, r):
                    b, tt, heads = ATT2[r]
                    w, m, n = (tt + 1) * P, len(heads), "BM".index(tag)
                    dve.wait_ge(S["logits_ready"], 2 * r + n + 1)
                    sum_ = ssum[:, 4 * n:4 * n + m]
                    C.link(V.reciprocal(sum_, sum_))
                    x_ = v3(lg2[n][:, 0:m * w], m)
                    C.link(V.tensor_tensor(x_, x_, along(sum_, w), ALU.mult), S["probs_ready"])

                def pair_decays(hd):
                    bank = B.wait(dve, f"gb{hd}")
                    dve.wait_ge(S["em_ready"], hd + 1)
                    C.link(V.tensor_scalar(dT[:, 0:T], bank[:, 0:T], acol[:, 0, hd:hd + 1], 0.0, ALU.subtract, ALU.max))
                    C.link(V.tensor_scalar(dT[:, T:T + P], bank[:, P:T], acol[:, 1, hd:hd + 1], 0.0, ALU.subtract, ALU.max), S["pairs_in"])
                    B.release(dve, f"gb{hd}")

                def weights(hd):
                    dve.wait_ge(S["d_exp"], hd + 1)
                    for o in (0, T):
                        C.link(V.tensor_tensor(dT[:, o:o + P], dT[:, o:o + P], K("pairmask")[:, P:2 * P], ALU.mult))
                    bank = B.wait(dve, f"sc{hd}")
                    C.link(V.scalar_tensor_tensor(sT[hd % 2], bank[:, 0:T + P], 0.125, dT, ALU.mult, ALU.mult), S["s_ready"])
                    B.release(dve, f"sc{hd}")

                def divide(hd):
                    bank = B.wait(dve, f"nd{hd}")
                    C.link(V.tensor_tensor(dn, bank[:, T:2 * T], em, ALU.max))
                    C.link(V.scalar_tensor_tensor(dn, bank[:, T:2 * T], -1.0, dn, ALU.mult, ALU.max))
                    C.link(V.reciprocal(dn, dn))
                    C.link(V.tensor_tensor(mix[:, 4 + hd, :], bank[:, 0:T], dn, ALU.mult), S["dn_ready"])
                    B.release(dve, f"nd{hd}")

                for r in range(len(ATT2) + 1):
                    if r < len(ATT2):
                        masked_logits("B", r)
                        masked_logits("M", r)
                    if r:
                        divide(r - 1)
                    if r < len(ATT2):
                        probabilities("B", r)
                        probabilities("M", r)
                        pair_decays(r)
                        weights(r)

                def split_mix(i):
                    split(C, mix[:, i:i + 2, :], mix_hi[:, i:i + 2, :], mix_lo[:, i:i + 2, :], S["mix_ready"])

                for o, gain, place, n in ((0, "g_mobaout", "block", 4), (2, "g_mlaout", "latent", 5)):
                    refine(C, place, n)
                    for i in range(2):
                        C.link(V.scalar_tensor_tensor(mix[:, o + i, :], mix[:, o + i, :], p(gain)[:, i:i + 1], v3(sqa, 4)[:, o + i, :], ALU.mult, ALU.mult))
                    split_mix(o)
                refine(C, "mlstm", 6)
                dve.wait_ge(S["bsg_ready"], 1)
                for hd in range(4):
                    i = 4 + hd
                    C.link(V.tensor_tensor(mix[:, i, :], mix[:, i, :], v3(sqb, 4)[:, hd, :], ALU.mult))
                    C.link(V.scalar_tensor_tensor(mix[:, i, :], mix[:, i, :], p("g_mlstm")[:, hd:hd + 1], mo[:, hd, :], ALU.mult, ALU.mult))
                    if hd % 2:
                        split_mix(i - 1)
                for j in range(4):
                    bank = B.wait(dve, f"WO{j}")
                    o = h[:, 2 * j:2 * j + 2, :].rearrange("p a t -> p (a t)")
                    C.link(V.tensor_tensor(o, o, bank[:, :], ALU.add), S["h_ready"])
                    B.release(dve, f"WO{j}")
                refine(C, "mlp", 7)
                norm_parts(C, p("g_mlp"), dn, KD // 2)
                for i in range(16):
                    dve.wait_ge(S["conv_in"], 4 + i + 1)
                    x_ = hidden[:, 2 * i:2 * i + 2, :].rearrange("p a t -> p (a t)")
                    C.link(V.tensor_tensor(x_, x_, x_, ALU.mult))
                    split(C, x_, hidden_hi[:, 2 * i:2 * i + 2, :].rearrange("p a t -> p (a t)"), hidden_lo[:, 2 * i:2 * i + 2, :].rearrange("p a t -> p (a t)"), S["hidden_ready"])
                for j in range(4):
                    bank = B.wait(dve, f"D{j}")
                    o = h[:, 2 * j:2 * j + 2, :].rearrange("p a t -> p (a t)")
                    C.link(V.tensor_tensor(o, o, bank[:, :], ALU.add), S["h_ready"])
                    B.release(dve, f"D{j}")
                refine(C, "next", 8)
                layer_end(dve, l + (layers[0] + 2), True)


def lay_out(i):
    f = np.float32
    p1 = []
    for l in range(LAYERS):
        v = {"g_mix": cols(i["norm_mix_g"][l]), "mu": cols(i["a_mu"][l]), "w0": cols(i["a_w0"][l]), "a0": cols(i["a_a0"][l]),
             "k_k": cols(i["a_k_k"][l]), "k_a": cols(i["a_k_a"][l]), "r_k": cols(i["a_r_k"][l].reshape(-1)),
             "gn_g": cols(i["a_gn_g"][l]), "gn_b": cols(i["a_gn_b"][l]), "lb0": cols(i["b_lb_logits"][0]),
             "lb1": cols(i["b_lb_logits"][1]), "not_first": np.full((P, 4), float(l > 0), f), "b_gn": cols(i["b_gn_g"][l]),
             "g_ffn": cols(i["norm_ffn_g"][l]), "conv_b": cols(i["conv_b"][l]), "conv_w0": cols(i["conv_w"][l][0]),
             "conv_w1": cols(i["conv_w"][l][1]), "conv_w2": cols(i["conv_w"][l][2]),
             "wa_up": np.concatenate([i["a_w_up"][l], i["a_a_up"][l]], 0), "g_up": i["a_g_up"][l]}
        assert list(v) == list(PAR1.at)
        p1.append(np.concatenate(list(v.values()), 1))
    p2 = []
    for l in range(LAYERS):
        w = {n[:-2]: a[l] for n, a in i.items() if n.endswith("_2") and n != "positions_2"}
        v = {"g_mix": cols(w["g_mix_norm"]), "conv_w": np.concatenate([cols(w["conv_w"][j]) for j in range(4)], 1),
             "conv_b": cols(w["conv_b"]), "b_i": col(w["b_igate"]), "b_f": col(w["b_fgate"]),
             "g_mlstm": cols(w["g_mlstm_out"].reshape(-1)), "g_mq": col(np.tile(w["g_moba_q"], 2)),
             "g_mk": col(np.tile(w["g_moba_k"], 2)), "g_mobaout": cols(w["g_moba_out"].reshape(-1)), "g_cq": cols(w["g_cq"]),
             "g_ckv": cols(w["g_ckv"]), "g_lq": col(w["g_mla_q"]), "g_lk": col(w["g_mla_k"]),
             "g_mlaout": cols(w["g_mla_out"].reshape(-1)), "g_mlp": cols(w["g_mlp_norm"]), "g_final": cols(i["norm_final_g"])}
        assert list(v) == list(PAR2.at)
        p2.append(np.concatenate(list(v.values()), 1))
    s = [chunks(stream1(i["w_in"][l], i["w_branch"][l], i["w_o"][l], i["w_up"][l], i["w_down"][l])) for l in range(LAYERS)]
    s += [chunks(stream2(*(i[n + "_2"][l] for n in ("w_in", "w_uq", "w_ukv", "w_out", "w_up", "w_down")))) for l in range(LAYERS)]
    c, m = constants()
    return {"x": np.ascontiguousarray(i["x"][0].T.reshape(KD, P, T).transpose(1, 0, 2)), "params": np.stack([np.pad(v, ((0, 0), (0, PAR_SIZE - v.shape[1]))) for v in p1 + p2 + [p2[-1]]]),
            "stream": np.concatenate(s), "cst": c, "masks": m, "positions": np.ascontiguousarray(i["positions_2"])}


def kernel(**inputs):
    import concourse.bacc as bacc
    from concourse.bass_utils import run_bass_kernel_spmd

    arrays = lay_out({n: np.asarray(a) for n, a in inputs.items()})
    nc = bacc.Bacc("TRN2", target_bir_lowering=False, num_devices=1)
    args = [nc.dram_tensor(f"in_{n}", a.shape, mybir.dt.from_np(a.dtype), kind="ExternalInput").ap() for n, a in arrays.items()]
    out = nc.dram_tensor("out", (P, KD, T), F32, kind="ExternalOutput").ap()
    build(nc, *args, out)
    r = run_bass_kernel_spmd(nc, [{f"in_{n}": a for n, a in arrays.items()}], core_ids=[0])
    got = r.results[0]["out"]
    return np.ascontiguousarray(got.transpose(1, 0, 2).reshape(D, T).T)[None]
```
